# Optimizing a Trainium2 kernel written in Bass

```python
import jax, jax.numpy as jnp
from jax import lax
import numpy as np

D_MODEL = 1024
BATCH = 1
SEQ = 512
DEPTH = 2

GRID_W = 64
CTX_LEN = 256
HEAD_DIM = 64
ROPE_THETA = 10000.0
EPS = 1e-6
Q_BLOCK = 128

GLA_HEADS = D_MODEL // 128
GLA_DK = 32
GLA_DV = 64
GLA_RANK = 16
GLA_TAU = 16.0
GLA_CHUNK = 64
GLA_QK_W = GLA_HEADS * GLA_DK
GLA_V_W = GLA_HEADS * GLA_DV
B_HEADS = D_MODEL // 128
B_KV_HEADS = 2
C_HEADS = D_MODEL // HEAD_DIM
C_KV_HEADS = 2
WINDOW = 128
FFN_HIDDEN = -(-8 * D_MODEL // (3 * 256)) * 256

EVEN_WIDTHS = (GLA_QK_W, GLA_QK_W, GLA_V_W, GLA_V_W, GLA_RANK, GLA_RANK,
               B_HEADS * HEAD_DIM, B_KV_HEADS * HEAD_DIM, B_KV_HEADS * HEAD_DIM)
EVEN_IN = sum(EVEN_WIDTHS)
EVEN_MIX = GLA_V_W + B_HEADS * HEAD_DIM
ODD_WIDTHS = (C_HEADS * HEAD_DIM, C_KV_HEADS * HEAD_DIM, C_KV_HEADS * HEAD_DIM)
ODD_IN = sum(ODD_WIDTHS)
ODD_MIX = C_HEADS * HEAD_DIM
N_EVEN = (DEPTH + 1) // 2
N_ODD = DEPTH // 2

kernel_name = "hybrid_gla_gqa_swa_prefix_dit"

def rms_norm(x, g):
    xf = x.astype(jnp.float32)
    y = xf * lax.rsqrt(jnp.mean(xf * xf, axis=-1, keepdims=True) + EPS)
    return y.astype(x.dtype) * g

def modulate(h, shift, scale):
    return h * (1 + scale) + shift

def split_cols(t, widths):
    idx = np.cumsum(np.array(widths))[:-1].tolist()
    return jnp.split(t, idx, axis=-1)

def heads(t, n_heads):
    return t.reshape(t.shape[0], t.shape[1], n_heads, -1)

def rope_tables(n_tokens, dtype):
    rows = n_tokens // GRID_W
    r, cidx = jnp.meshgrid(jnp.arange(rows), jnp.arange(GRID_W), indexing="ij")
    row = r.reshape(-1).astype(jnp.float32)
    col = cidx.reshape(-1).astype(jnp.float32)
    half = HEAD_DIM // 2
    inv = ROPE_THETA ** (-jnp.arange(0, half, 2, dtype=jnp.float32) / half)
    ang_r = row[:, None] * inv[None]
    ang_c = col[:, None] * inv[None]
    ang = jnp.concatenate([ang_r, ang_r, ang_c, ang_c], axis=-1)
    return jnp.cos(ang)[:, None, :].astype(dtype), jnp.sin(ang)[:, None, :].astype(dtype)

def apply_rope(x, cos, sin):
    q = HEAD_DIM // 4
    x0, x1, x2, x3 = x[..., :q], x[..., q:2 * q], x[..., 2 * q:3 * q], x[..., 3 * q:]
    rot = jnp.concatenate([-x1, x0, -x3, x2], axis=-1)
    return x * cos + rot * sin

def gla_chunk_scan(q, k, v, gk, s0):
    bn, L, H, _ = q.shape
    dv = v.shape[-1]
    nc = L // GLA_CHUNK

    def to_chunks(t):
        return t.astype(jnp.float32).reshape(bn, nc, GLA_CHUNK, H, t.shape[-1]).transpose(1, 0, 3, 2, 4)

    lower = jnp.tril(jnp.ones((GLA_CHUNK, GLA_CHUNK), dtype=bool))

    def step(S, inp):
        qc, kc, vc, gc = inp
        b = jnp.cumsum(gc, axis=2)
        o_inter = jnp.einsum("bhik,bhkv->bhiv", qc * jnp.exp(b), S)
        diff = jnp.where(lower[:, :, None], b[:, :, :, None, :] - b[:, :, None, :, :], -jnp.inf)
        A = jnp.einsum("bhik,bhjk,bhijk->bhij", qc, kc, jnp.exp(diff))
        o_intra = jnp.einsum("bhij,bhjv->bhiv", A, vc)
        b_last = b[:, :, -1]
        S = S * jnp.exp(b_last)[..., None] + jnp.einsum(
            "bhjk,bhjv->bhkv", kc * jnp.exp(b_last[:, :, None] - b), vc)
        return S, o_intra + o_inter

    S, o = lax.scan(step, s0, (to_chunks(q), to_chunks(k), to_chunks(v), to_chunks(gk)))
    o = o.transpose(1, 0, 3, 2, 4).reshape(bn, L, H, dv)
    return o, S

def dense_block_attention(q, k, v):
    bn, L, H, D = q.shape
    hkv = k.shape[2]
    nb = L // Q_BLOCK
    qb = q.reshape(bn, nb, Q_BLOCK, hkv, H // hkv, D).transpose(1, 0, 2, 3, 4, 5)
    scale = D ** -0.5

    def one(qblk):
        s = jnp.einsum("bqhgd,bkhd->bhgqk", qblk, k).astype(jnp.float32) * scale
        p = jax.nn.softmax(s, axis=-1).astype(v.dtype)
        return jnp.einsum("bhgqk,bkhd->bqhgd", p, v)

    o = lax.map(one, qb)
    return o.transpose(1, 0, 2, 3, 4, 5).reshape(bn, L, H * D)

def window_sink_attention(q, k, v, kc, vc, sink):
    bn, L, H, D = q.shape
    hkv = k.shape[2]
    g = H // hkv
    nb = L // Q_BLOCK
    band = Q_BLOCK + 2 * WINDOW
    pad = ((0, 0), (WINDOW, WINDOW), (0, 0), (0, 0))
    kp, vp = jnp.pad(k, pad), jnp.pad(v, pad)
    qb = q.reshape(bn, nb, Q_BLOCK, hkv, g, D).transpose(1, 0, 2, 3, 4, 5)
    sink_l = sink.reshape(hkv, g).astype(jnp.float32)
    scale = D ** -0.5
    s_ctx_len = kc.shape[1]

    def one(args):
        n, qblk = args
        start = n * Q_BLOCK
        kb = lax.dynamic_slice_in_dim(kp, start, band, axis=1)
        vb = lax.dynamic_slice_in_dim(vp, start, band, axis=1)
        qpos = start + jnp.arange(Q_BLOCK)
        kpos = start - WINDOW + jnp.arange(band)
        valid = (jnp.abs(qpos[:, None] - kpos[None, :]) <= WINDOW) & (kpos >= 0)[None] & (kpos < L)[None]
        s_loc = jnp.einsum("bqhgd,bkhd->bhgqk", qblk, kb).astype(jnp.float32) * scale
        s_loc = jnp.where(valid, s_loc, -jnp.inf)
        s_ctx = jnp.einsum("bqhgd,bkhd->bhgqk", qblk, kc).astype(jnp.float32) * scale
        s_sink = jnp.broadcast_to(sink_l[None, :, :, None, None], s_loc.shape[:-1] + (1,))
        p = jax.nn.softmax(jnp.concatenate([s_loc, s_ctx, s_sink], axis=-1), axis=-1).astype(v.dtype)
        return (jnp.einsum("bhgqk,bkhd->bqhgd", p[..., :band], vb)
                + jnp.einsum("bhgqk,bkhd->bqhgd", p[..., band:band + s_ctx_len], vc))

    o = lax.map(one, (jnp.arange(nb), qb))
    return o.transpose(1, 0, 2, 3, 4, 5).reshape(bn, L, H * D)

def ctx_sink_attention(q, k, v, sink):
    bn, Lc, H, D = q.shape
    hkv = k.shape[2]
    g = H // hkv
    qg = q.reshape(bn, Lc, hkv, g, D)
    s = jnp.einsum("bqhgd,bkhd->bhgqk", qg, k).astype(jnp.float32) * D ** -0.5
    s_sink = jnp.broadcast_to(sink.reshape(hkv, g).astype(jnp.float32)[None, :, :, None, None], s.shape[:-1] + (1,))
    p = jax.nn.softmax(jnp.concatenate([s, s_sink], axis=-1), axis=-1)[..., :Lc].astype(v.dtype)
    return jnp.einsum("bhgqk,bkhd->bqhgd", p, v).reshape(bn, Lc, H * D)

def even_mixer(hx, hc, w_in, w_out, gk_w, gk_b, gla_g, qn_g, kn_g, cos, sin, with_ctx):
    def project(h):
        gq, gkk, gv, gg, lr_f, lr_b, bq, bk, bv = split_cols(h @ w_in, EVEN_WIDTHS)
        dec_f = jax.nn.log_sigmoid((lr_f @ gk_w[0] + gk_b[0]).astype(jnp.float32)) / GLA_TAU
        dec_b = jax.nn.log_sigmoid((lr_b @ gk_w[1] + gk_b[1]).astype(jnp.float32)) / GLA_TAU
        gla = (heads(gq, GLA_HEADS) * GLA_DK ** -0.5, heads(gkk, GLA_HEADS), heads(gv, GLA_HEADS),
               gg, heads(dec_f, GLA_HEADS), heads(dec_b, GLA_HEADS))
        att = (rms_norm(heads(bq, B_HEADS), qn_g), rms_norm(heads(bk, B_KV_HEADS), kn_g), heads(bv, B_KV_HEADS))
        return gla, att

    (qx, kx, vx, gx, dfx, dbx), (aqx, akx, avx) = project(hx)
    (qc, kc, vc, gc, dfc, dbc), (aqc, akc, avc) = project(hc)

    def flip(t):
        return t[:, ::-1]

    s0 = jnp.zeros((hc.shape[0], GLA_HEADS, GLA_DK, GLA_DV), jnp.float32)
    ocf, s_f = gla_chunk_scan(qc, kc, vc, dfc, s0)
    ocb, s_b = gla_chunk_scan(flip(qc), flip(kc), flip(vc), flip(dbc), s0)
    oxf, _ = gla_chunk_scan(qx, kx, vx, dfx, s_f)
    oxb, _ = gla_chunk_scan(flip(qx), flip(kx), flip(vx), flip(dbx), s_b)

    def gla_out(o, gate):
        o = rms_norm(o.astype(gate.dtype), gla_g) * jax.nn.silu(heads(gate, GLA_HEADS))
        return o.reshape(o.shape[0], o.shape[1], GLA_V_W)

    aqx, akx = apply_rope(aqx, cos, sin), apply_rope(akx, cos, sin)
    k_all = jnp.concatenate([akx, akc], axis=1)
    v_all = jnp.concatenate([avx, avc], axis=1)
    ax = dense_block_attention(aqx, k_all, v_all)
    ox = jnp.concatenate([gla_out(oxf + flip(oxb), gx), ax], axis=-1) @ w_out
    if not with_ctx:
        return ox, None
    ac = dense_block_attention(aqc, akc, avc)
    oc = jnp.concatenate([gla_out(ocf + flip(ocb), gc), ac], axis=-1) @ w_out
    return ox, oc

def odd_mixer(hx, hc, w_in, w_out, sink, cos, sin, with_ctx):
    qx, kx, vx = split_cols(hx @ w_in, ODD_WIDTHS)
    qc, kc, vc = split_cols(hc @ w_in, ODD_WIDTHS)
    qx = apply_rope(heads(qx, C_HEADS), cos, sin)
    kx = apply_rope(heads(kx, C_KV_HEADS), cos, sin)
    vx = heads(vx, C_KV_HEADS)
    qc, kc, vc = heads(qc, C_HEADS), heads(kc, C_KV_HEADS), heads(vc, C_KV_HEADS)
    ox = window_sink_attention(qx, kx, vx, kc, vc, sink) @ w_out
    if not with_ctx:
        return ox, None
    oc = ctx_sink_attention(qc, kc, vc, sink) @ w_out
    return ox, oc

def swiglu(h, w1, w3, w2):
    return (jax.nn.silu(h @ w1) * (h @ w3)) @ w2

def setup_inputs(seed: int = 0) -> dict:
    key = jax.random.key(seed)
    ks = jax.random.split(key, 24)

    def nrm(k, shape, scale):
        return jax.random.normal(k, shape, jnp.float32) * scale

    def gain(k, shape):
        return 1.0 + nrm(k, shape, 0.02)

    D = D_MODEL
    return {
        "x": nrm(ks[0], (BATCH, SEQ, D), 1.0),
        "c": nrm(ks[1], (BATCH, D), 1.0),
        "ctx": nrm(ks[2], (BATCH, CTX_LEN, D), 1.0),
        "c_ctx": nrm(ks[3], (D,), 1.0),
        "ada_w": nrm(ks[4], (DEPTH, D, 6 * D), D ** -0.5),
        "ada_b": nrm(ks[5], (DEPTH, 6 * D), 0.02),
        "norm1_g": gain(ks[6], (DEPTH, D)),
        "norm2_g": gain(ks[7], (DEPTH, D)),
        "ffn_w1": nrm(ks[8], (DEPTH, D, FFN_HIDDEN), D ** -0.5),
        "ffn_w3": nrm(ks[9], (DEPTH, D, FFN_HIDDEN), D ** -0.5),
        "ffn_w2": nrm(ks[10], (DEPTH, FFN_HIDDEN, D), FFN_HIDDEN ** -0.5),
        "mixab_w_in": nrm(ks[11], (N_EVEN, D, EVEN_IN), D ** -0.5),
        "mixab_w_out": nrm(ks[12], (N_EVEN, EVEN_MIX, D), EVEN_MIX ** -0.5),
        "gla_gk_w": nrm(ks[13], (N_EVEN, 2, GLA_RANK, GLA_QK_W), GLA_RANK ** -0.5),
        "gla_gk_b": nrm(ks[14], (N_EVEN, 2, GLA_QK_W), 0.02),
        "gla_norm_g": gain(ks[15], (N_EVEN, GLA_DV)),
        "attn_qnorm_g": gain(ks[16], (N_EVEN, HEAD_DIM)),
        "attn_knorm_g": gain(ks[17], (N_EVEN, HEAD_DIM)),
        "win_w_in": nrm(ks[18], (N_ODD, D, ODD_IN), D ** -0.5),
        "win_w_out": nrm(ks[19], (N_ODD, ODD_MIX, D), ODD_MIX ** -0.5),
        "win_sink": nrm(ks[20], (N_ODD, C_HEADS), 0.5),
        "final_g": gain(ks[21], (D,)),
    }

def reference(x, c, ctx, c_ctx, ada_w, ada_b, norm1_g, norm2_g, ffn_w1, ffn_w3, ffn_w2,
              mixab_w_in, mixab_w_out, gla_gk_w, gla_gk_b, gla_norm_g, attn_qnorm_g, attn_knorm_g,
              win_w_in, win_w_out, win_sink, final_g):
    n_tokens = x.shape[1]
    cos, sin = rope_tables(n_tokens, x.dtype)
    sc = jax.nn.silu(c)
    scc = jax.nn.silu(c_ctx)[None]
    xc = ctx
    for l in range(DEPTH):
        with_ctx = l < DEPTH - 1
        mod_x = (sc @ ada_w[l] + ada_b[l])[:, None, :]
        mod_c = (scc @ ada_w[l] + ada_b[l])[:, None, :]
        sh1x, sc1x, g1x, sh2x, sc2x, g2x = jnp.split(mod_x, 6, axis=-1)
        sh1c, sc1c, g1c, sh2c, sc2c, g2c = jnp.split(mod_c, 6, axis=-1)
        hx = modulate(rms_norm(x, norm1_g[l]), sh1x, sc1x)
        hc = modulate(rms_norm(xc, norm1_g[l]), sh1c, sc1c)
        if l % 2 == 0:
            i = l // 2
            ox, oc = even_mixer(hx, hc, mixab_w_in[i], mixab_w_out[i], gla_gk_w[i], gla_gk_b[i],
                                gla_norm_g[i], attn_qnorm_g[i], attn_knorm_g[i], cos, sin, with_ctx)
        else:
            i = l // 2
            ox, oc = odd_mixer(hx, hc, win_w_in[i], win_w_out[i], win_sink[i], cos, sin, with_ctx)
        x = x + g1x * ox
        x = x + g2x * swiglu(modulate(rms_norm(x, norm2_g[l]), sh2x, sc2x), ffn_w1[l], ffn_w3[l], ffn_w2[l])
        if with_ctx:
            xc = xc + g1c * oc
            xc = xc + g2c * swiglu(modulate(rms_norm(xc, norm2_g[l]), sh2c, sc2c), ffn_w1[l], ffn_w3[l], ffn_w2[l])
    return rms_norm(x, final_g)


_drawn_inputs = setup_inputs


def setup_inputs(seed=0):
    import zlib

    import numpy as np

    out = dict(_drawn_inputs(seed))
    spreads = {}
    factors = {'norm1_g': 3.761,
     'norm2_g': 3.029,
     'gla_gk_b': 8.0,
     'gla_norm_g': 7.294,
     'attn_qnorm_g': 8.0,
     'attn_knorm_g': 8.0,
     'win_sink': 8.0,
     'final_g': 2.736}
    for name, (base, spread) in spreads.items():
        noise = np.random.default_rng([zlib.crc32(name.encode()), seed]).standard_normal(out[name].shape)
        drawn = base * np.exp(spread * noise) if base else spread * noise
        out[name] = __import__('jax').numpy.asarray(drawn.astype(out[name].dtype))
    for name, factor in factors.items():
        out[name] = (out[name] * factor).astype(out[name].dtype)
    return out
```

```python
import math
from contextlib import ExitStack

import concourse.bass as bass
from concourse import mybir

F32 = mybir.dt.float32
F32R = mybir.dt.float32r
ALU = mybir.AluOpType
ACT = mybir.ActivationFunctionType
AX = mybir.AxisListType

P = 128
D = 1024
KT = D // P
NX = 512
NC_ = 256
T = NX + NC_
EPS = 1e-6
HD = 64
FFN = 2816
FT = FFN // P
GROUPS = [(0, 8), (8, 7), (15, 7)]
CH = 64
NCH = T // CH
DK = 32
TAU = 16.0
CLAMP = 80.0 * TAU
RING = 3
ADA_RING = 3
NADA = 12
ADA_EARLY = 4

PC_C = 0
PC_ADAB = PC_C + 2 * KT
PC_N = PC_ADAB + 2 * 48
PC_FIN = PC_N + 4 * KT
PC_GKB = PC_FIN + KT
PC_GLAG = PC_GKB + 4
PC_QN = PC_GLAG + 1
PC_KN = PC_QN + 1
PC_SINK = PC_KN + 1
NPAR = PC_SINK + 16

CC_COS = 0
CC_SIN = CC_COS + NX
CC_ID = CC_SIN + NX
CC_ONES = CC_ID + P
CC_BLK = CC_ONES + P
CC_ROT = CC_BLK + P
CC_MF = CC_ROT + P
CC_MB = CC_MF + CH
NCONST = CC_MB + CH

NEG = -1.0e30


def blocks_of_the_stream():
    out = [dict(kind="proj", layer=0, m=m, nk=KT, tok=T) for m in range(19)]
    out += [dict(kind="out", layer=0, m=m, nk=KT, tok=T) for m in range(KT)]

    def ffn(layer, tok):
        for g, (h0, nh) in enumerate(GROUPS):
            for i in range(nh):
                out.append(dict(kind="w1", layer=layer, g=g, i=i, h=h0 + i, nk=KT, tok=tok))
                out.append(dict(kind="w3", layer=layer, g=g, i=i, h=h0 + i, nk=KT, tok=tok))
            for m in range(KT):
                out.append(dict(kind="w2", layer=layer, g=g, m=m, nk=nh, tok=tok))

    ffn(0, T)
    out += [dict(kind="proj", layer=1, m=m, nk=KT, tok=T if m < 2 else NX) for m in range(10)]
    out += [dict(kind="out", layer=1, m=m, nk=KT, tok=NX) for m in range(KT)]
    ffn(1, NX)
    return out


BLOCKS = blocks_of_the_stream()
NB = len(BLOCKS)
FIRST = {}
for _n, _b in enumerate(BLOCKS):
    FIRST.setdefault((_b["kind"], _b["layer"]), _n)


def attention_units(layer):
    units = []
    for g in range(2):
        for hp in range(2 if layer == 0 else 4):
            for qt in range(6 if layer == 0 else 4):
                if layer == 0 and qt < 4:
                    segs, tiles, mask = [(0, 0, NX), (NX, NX, NC_)], list(range(6)), None
                elif layer == 0:
                    segs, tiles, mask = [(NX, NX, NC_)], [4, 5], None
                else:
                    lo, hi = max(qt - 1, 0), min(qt + 1, 3)
                    segs = [(256, NX, NC_), (512, lo * P, (hi - lo + 1) * P)]
                    tiles = [4, 5] + list(range(lo, hi + 1))
                    mask = (lo - (qt - 1)) * P
                c0 = segs[0][0]
                units.append(dict(g=g, hp=hp, qt=qt, set=len(units) // (6 if layer == 0 else 4), segs=segs,
                                  tiles=tiles, mask=mask, c0=c0, n=len(tiles) * P,
                                  first=qt == 0, last=qt == (5 if layer == 0 else 3)))
    act = dve = allk = 0
    for u in units:
        u["kp"] = (len(u["tiles"]) + 1) // 2
        u["kp0"], u["act0"], u["dve0"] = allk, act, dve
        allk += u["kp"]
        act += (u["kp"] + 1) // 2
        dve += u["kp"] // 2
    return units


def build(nc, x_in, params, consts, masks, gkw_in, ada, weights, out):
    ctx = ExitStack()
    with ctx:
        def sb(name, shape, dt=F32):
            return ctx.enter_context(nc.sbuf_tensor(name, shape, dt))

        base = nc.sbuf_base
        top = [0]

        arena = sb("arena", [P, (nc.sbuf_bytes_remaining - 128) // 4])
        origin = (base + 31) // 32 * 32

        def at(name, shape, offset, dt=F32):
            return nc.alloc_sbuf_tensor_at(name, shape, dt, offset=origin + offset)

        def take(nbytes):
            o = top[0]
            top[0] += (nbytes + 31) // 32 * 32
            return o

        TILE = T * 4
        xT = at("xT", [P, KT, T], take(KT * TILE))
        raw = at("raw", [P, RING, KT * P], take(RING * KT * P * 4))
        whi = at("whi", [P, RING, KT * P], take(RING * KT * P * 4), F32R)
        wlo = at("wlo", [P, RING, KT * P], take(RING * KT * P * 4), F32R)
        con = at("con", [P, NCONST], take(NCONST * 4))
        identr = at("identr", [P, P], take(P * 4), F32R)
        bandm = at("bandm", [P, 3 * P], take(3 * P * 4), F32R)
        par = at("par", [P, NPAR], take(NPAR * 4))
        epsc = at("epsc", [P, 8], take(32))
        gkw = at("gkw", [P, 512], take(512 * 4))
        cpad = at("cpad", [P, KT, 32], take(KT * 32 * 4))
        mod = at("mod", [P, 2, 48, 2], take(2 * 96 * 4))
        modA = at("modA", [P, 4, KT, 2], take(4 * 16 * 4))
        O_ADASB = take(2 * 2048)
        adasb = at("adasb", [P, 2, 512], O_ADASB)
        st_mx = at("st_mx", [P, 2, 2], take(16))
        st_nb = at("st_nb", [P, 2, 2], take(16))
        st_sum = at("st_sum", [P, 2, 2], take(16))
        st_ri = at("st_ri", [P, 2, 2], take(16))
        st_sk = at("st_sk", [P, 2, 2], take(16))
        ge = at("ge", [P, 3, 4, NCH], take(3 * 4 * NCH * 4))
        gd = at("gd", [P, 4, NCH], take(4 * NCH * 4))
        H = take(2 * KT * TILE)
        G = take(2 * KT * TILE)
        E = take(11 * TILE)
        assert top[0] + 32 <= arena.shape[1] * 4, (top[0], arena.shape)

        hhA = at("hhA", [P, 4, T], H, F32R)
        hlA = at("hlA", [P, 4, T], H + 4 * TILE, F32R)
        hhB = at("hhB", [P, 4, T], H + 8 * TILE, F32R)
        hlB = at("hlB", [P, 4, T], H + 12 * TILE, F32R)

        def hh(k):
            return (hhA if k < 4 else hhB)[:, k % 4, :]

        def hl(k):
            return (hlA if k < 4 else hlB)[:, k % 4, :]

        gh = at("gh", [P, KT, T], G, F32R)
        gl = at("gl", [P, KT, T], G + KT * TILE, F32R)
        big = at("big", [P, 2 * KT, T], G)
        ex = at("ex", [P, 3, T], E)
        ada_w = at("ada_w", [P, ADA_RING, 4, 512], E + 3 * TILE)
        tmps = at("tmps", [P, 8, T], E + 3 * TILE)

        S0, S1 = H, G + 10 * TILE
        qst = [at(f"qst{L}", [P, 2, 2, 2, T], E + 3 * TILE, F32R) for L in range(2)]
        prob = [at("prob0", [P, 2, 2, T], S0), at("prob1", [P, 2, 2, T], S1)]
        kst = [at("kst0", [P, 2, T], S0 + 4 * TILE, F32R), at("kst1", [P, 2, T], S1 + 4 * TILE, F32R)]
        probT = [at("probT0", [P, 3, 512], S0 + 6 * TILE), at("probT1", [P, 3, 512], E)]
        vtok = [at("vtok0", [P, 6, P], E + TILE), at("vtok1", [P, 6, P], E + 2 * TILE)]
        ropet = [at("ropet0", [P, 2, T], S0 + 6 * TILE), at("ropet1", [P, 2, T], E)]
        osum = at("osum", [P, 2, 2, 256], O_ADASB)
        assert top[0] + 32 <= arena.shape[1] * 4, (top[0], arena.shape)

        gsc = at("gsc", [P, 8, T], H)
        dec = at("dec", [P, 4, T], G + 12 * TILE)
        vgt = at("vgt", [P, 6, 512], E + 3 * TILE)
        kgt = at("kgt", [P, 4, 6, P], G + 4 * TILE)
        cmask = at("cmask", [P, 2, T], E + 7 * TILE)
        state = at("state", [P, 2, 2, 2, CH], E + 7 * TILE)
        statr = at("statr", [P, 2, 2, CH], E + 8 * TILE)
        supd = at("supd", [P, 2, 2, 2, CH], E + 9 * TILE)
        attnT = at("attnT", [P, 2, 512], E)
        attnM = at("attnM", [P, 512], E + TILE + 1024)
        og = at("og", [P, 4, T], G)
        gt = at("gt", [P, 4, T], G + 12 * TILE)

        psum = ctx.enter_context(nc.psum_tensor("psum", [P, 4096], F32))
        lin = [psum[:, 1024 * i:1024 * i + 1024] for i in range(2)]
        wk = [psum[:, 1024 * i:1024 * i + 1024] for i in range(2, 4)]

        ident = con[:, CC_ID:CC_ID + P]
        ones = con[:, CC_ONES:CC_ONES + P]
        blk = con[:, CC_BLK:CC_BLK + P]
        rot = con[:, CC_ROT:CC_ROT + P]
        cos = con[:, CC_COS:CC_COS + NX]
        sin = con[:, CC_SIN:CC_SIN + NX]
        mgla = [con[:, CC_MF:CC_MF + CH], con[:, CC_MB:CC_MB + CH]]

        sems = {}

        def sem(name):
            if name not in sems:
                sems[name] = ctx.enter_context(nc.semaphore(name))
            return sems[name]

        names = ["s_par", "s_con", "s_x", "s_adaload0", "s_adaload1", "s_adaload2", "s_adamm", "s_adacp", "s_adaT",
                 "s_adar", "s_mod", "s_modA", "s_cpad0", "s_cpad", "s_idr", "s_hi", "s_lo", "s_acc", "s_ev0", "s_ev1",
                 "s_gh", "s_gl", "s_out", "s_fin", "s_outdma",
                 "s_fence", "s_nln", "a_ln", "g_nln"] + [f"s_raw{i}" for i in range(RING)]
        names += [f"s_{n}" for n in ("sq", "sqadd", "nps", "rs", "nt", "nhh", "nhf", "nhl")]
        names += [f"a_{n}" for n in ("sq", "ms", "rs", "nrm", "rot", "rsin", "rcos", "rope", "khi", "klo", "vps", "vtok",
                                     "qhi", "qlo", "S", "mx", "nb", "exp", "sk", "sum", "smax", "shift", "ri", "nrmp",
                                     "T", "ptA", "ptD", "O", "ocp", "oadd", "ohi", "olo")]
        names += [f"g_{n}" for n in ("z", "zc", "abs", "exp", "ln", "dec", "cm", "scan", "ref", "refe", "d", "dc", "e1",
                                     "e2", "qe", "ke", "vT", "vcpA", "vcpD", "kT", "kcpA", "kcpD", "A", "am", "am2", "at", "O",
                                     "ocp", "U", "ud", "uk", "st", "sr", "I", "oi", "sq", "ms", "rs", "on", "of", "hi",
                                     "lo")]
        for n_ in names:
            sem(n_)

        def ev(n):
            return sem(f"s_ev{n % 2}"), n // 2 + 1

        U = [attention_units(0), attention_units(1)]
        NORM = [dict(q=0, a=0, layer=0, sh=0, tok=T), dict(q=1, a=1, layer=0, sh=24, tok=T),
                dict(q=2, a=2, layer=1, sh=0, tok=T), dict(q=3, a=3, layer=1, sh=24, tok=NX),
                dict(q=4, a=None, layer=1, sh=None, tok=NX)]
        NORM_FOR = {("proj", 0): 0, ("w1", 0): 1, ("proj", 1): 2, ("w1", 1): 3}

        def nq(name, q, v):
            per = {"sq": KT, "sqadd": KT - 1, "nps": 1, "rs": 1, "nt": KT, "nhl": KT}
            if name in ("nhh", "nhf"):
                return sem("s_" + name), v + sum(KT * len(parts(NORM[p]["tok"])) for p in range(q))
            return sem("s_" + name), v + per[name] * q

        first = U[0]
        ONCE = {"rot": 5, "rsin": 5, "rcos": 5, "rope": 5, "khi": 2, "klo": 2, "vps": 1, "vtok": 1, "qhi": 2 * 4,
                "qlo": 4 * 4, "S": 2 * len(first), "mx": 2 * len(first), "exp": 2 * len(first),
                "nrmp": 2 * len(first), "T": first[-1]["kp0"] + first[-1]["kp"],
                "ptA": first[-1]["act0"] + (first[-1]["kp"] + 1) // 2, "ptD": first[-1]["dve0"] + first[-1]["kp"] // 2}

        def na(name, L, v):
            return sem("a_" + name), v + L * ONCE.get(name, len(first))

        def norm_tmp(q, i):
            return big[:, KT + i, :] if q == 0 else tmps[:, i, :]

        def parts(tok):
            return [(0, 0, NX)] + ([(1, NX, T)] if tok == T else [])

        def qsrc(L, g, hp):
            base_t = 12 if L == 0 else 2
            return big[64 * g:64 * g + 64, base_t + 2 * hp:base_t + 2 * hp + 2, :]

        def ksrc(L):
            return ex[:, 1, :] if L == 0 else big[:, 0, :]

        def vsrc(L):
            return ex[:, 2, :] if L == 0 else big[:, 1, :]

        def prep_tiles(L):
            return [(ksrc(0), PC_KN)] + [(big[:, 12 + t, :], PC_QN) for t in range(4)] if L == 0 else \
                [(ksrc(1), None)] + [(big[:, 2 + t, :], None) for t in range(8)]

        def mix_rows(L, g, hp, qt):
            t0 = (4 if L == 0 else 0) + 2 * hp
            h_, l_ = (hhA, hlA) if t0 < 4 else (hhB, hlB)
            sl = (slice(64 * g, 64 * g + 64), slice(t0 % 4, t0 % 4 + 2), slice(qt * P, qt * P + P))
            return h_[sl], l_[sl]

        NSEQ = [[8, 9, 10, 11] + list(range(8)), [11, 10, 9, 8] + list(range(7, -1, -1))]

        def fence(eng, which, k):
            eng.drain().then_inc(sem("s_fence"), 1)
            eng.wait_ge(sem("s_fence"), 3 * k)

        block = ctx.enter_context(nc.Block())

        @block.sync
        def _(sp):
            def load_raw(n):
                if n >= RING:
                    sp.wait_ge(sem("s_lo"), n - RING + 1)
                sp.dma_start(raw[:, n % RING, :], weights[n, :, :]).then_inc(sem(f"s_raw{n % RING}"), 16)

            def load_ada(h):
                if h >= ADA_RING:
                    sp.wait_ge(sem("s_adamm"), h - ADA_RING + 1)
                sp.dma_start(ada_w[:, h % ADA_RING, :, :], ada[h, :, :].rearrange("p (k n) -> p k n", k=4)) \
                    .then_inc(sem(f"s_adaload{h % ADA_RING}"), 16)

            sp.dma_start(par[:, :], params).then_inc(sem("s_par"), 16)
            sp.dma_start(con[:, :], consts).then_inc(sem("s_con"), 16)
            for h in range(ADA_RING):
                load_ada(h)
            sp.dma_start(xT[:, :, :], x_in.rearrange("p (k t) -> p k t", k=KT)).then_inc(sem("s_x"), 16)
            sp.dma_start(gkw[0:32, :], gkw_in).then_inc(sem("s_con"), 16)
            for n in range(RING):
                load_raw(n)
            for h in range(ADA_RING, 2 * ADA_EARLY):
                load_ada(h)
            h = 2 * ADA_EARLY
            for n in range(RING, NB):
                load_raw(n)
                for _ in range(2):
                    if h < 4 * NADA:
                        load_ada(h)
                        h += 1
            for k in range(KT):
                sp.wait_ge(sem("s_fin"), k + 1)
                sp.dma_start(out[:, k * NX:(k + 1) * NX], big[:, k, 0:NX]).then_inc(sem("s_outdma"), 16)
            sp.wait_ge(sem("s_outdma"), 16 * KT)

        @block.gpsimd
        def _(pool):
            pool.dma_start(bandm[:, :], masks).then_inc(sem("s_idr"), 16)
            pool.dma_start(identr[:, :], consts[:, CC_ID:CC_ID + P]).then_inc(sem("s_idr"), 16)
            for n in range(NB):
                s = n % RING
                w = BLOCKS[n]["nk"] * P
                pool.wait_ge(sem("s_hi"), n + 1)
                if n >= RING:
                    pool.wait_ge(sem("s_acc"), n - RING + 1)
                nc.gpsimd.tensor_tensor(wlo[:, s, 0:w], raw[:, s, 0:w], whi[:, s, 0:w].bitcast(F32),
                                        ALU.subtract).then_inc(sem("s_lo"), 1)

        @block.scalar
        def _(act):
            A = nc.scalar.activation

            def high(n):
                if n >= NB:
                    return
                s = n % RING
                w = BLOCKS[n]["nk"] * P
                act.wait_ge(sem(f"s_raw{s}"), 16 * (n // RING + 1))
                if n >= RING:
                    act.wait_ge(sem("s_acc"), n - RING + 1)
                    act.wait_ge(sem("s_lo"), n - RING + 1)
                A(whi[:, s, 0:w], raw[:, s, 0:w], ACT.Copy).then_inc(sem("s_hi"), 1)

            def ada_copy(c):
                act.wait_ge(sem("s_adamm"), 2 * (c + 1))
                if c >= 2:
                    act.wait_ge(sem("s_adaT"), c - 1)
                A(adasb[:, c % 2, :], wk[0][:, 512 * (c % 2):512 * (c % 2) + 512], ACT.Copy) \
                    .then_inc(sem("s_adacp"), 1)

            def square(q, k, tok):
                if k >= 3:
                    act.wait_ge(*nq("sqadd", q, k - 2))
                A(norm_tmp(q, 0 if k == 0 else 1 + k % 2)[:, 0:tok], xT[:, k, 0:tok], ACT.Square) \
                    .then_inc(sem("s_sq"), 1)

            def root(q, tok):
                act.wait_ge(*nq("nps", q, 1))
                y = norm_tmp(q, 3)[:, 0:tok]
                A(y, wk[0][:, 0:tok], ACT.Ln, bias=epsc[:, 0:1]).then_inc(sem("s_nln"), 1)
                act.wait_ge(sem("s_nln"), q + 1)
                A(y, y, ACT.Exp, scale=-0.5).then_inc(sem("s_rs"), 1)

            def norm_high(nd):
                q, tok = nd["q"], nd["tok"]
                root(q, tok)
                act.wait_ge(sem("s_modA"), 1 if q == 0 else 4)
                for k in range(KT):
                    act.wait_ge(*nq("nt", q, k + 1))
                    for c, a, b in parts(tok):
                        A(hh(k)[:, a:b], norm_tmp(q, 4 + k % 2)[:, a:b], ACT.Identity,
                          scale=modA[:, nd["a"], k, c:c + 1],
                          bias=mod[:, nd["layer"], nd["sh"] + k, c:c + 1]).then_inc(sem("s_nhh"), 1)

            act.wait_ge(sem("s_par"), 16)
            act.wait_ge(sem("s_cpad0"), 1)
            A(cpad[:, :, 0:2], par[:, PC_C:PC_C + 16].rearrange("p (k c) -> p k c", c=2), ACT.Silu) \
                .then_inc(sem("s_cpad"), 1)
            act.wait_ge(sem("s_x"), 16)
            for k in range(KT):
                square(0, k, T)
            high(0)
            high(1)
            for c in range(ADA_EARLY):
                ada_copy(c)
            norm_high(NORM[0])

            def mixer_projection(layer, n, b):
                m = b["m"]
                tok = b["tok"]
                act.wait_ge(sem("s_acc"), n + 1)
                s_, v_ = ev(n)
                ps = lin[n % 2][:, 0:tok]
                if layer == 1:
                    A(big[:, m, 0:tok], ps, ACT.Copy).then_inc(s_, 1)
                elif m < 2:
                    A(big[:, m, :], ps, ACT.Copy, scale=DK ** -0.5).then_inc(s_, 1)
                elif 8 <= m < 12:
                    A(big[:, m, :], ps, ACT.Silu).then_inc(s_, 1)
                elif m < 16:
                    A(big[:, m, :], ps, ACT.Copy).then_inc(s_, 1)
                else:
                    A(ex[:, m - 16, :], ps, ACT.Copy).then_inc(s_, 1)

            def attention(L):
                units = U[L]
                tiles = prep_tiles(L)
                def keys_high():
                    act.wait_ge(*na("rope", L, 1))
                    A(kst[L][0:64, 0, :], ksrc(L)[0:64, :], ACT.Copy).then_inc(sem("a_khi"), 1)
                    A(kst[L][64:128, 1, :], ksrc(L)[64:128, :], ACT.Copy).then_inc(sem("a_khi"), 1)

                def head_square(j):
                    if j >= 2:
                        act.wait_ge(sem("a_ms"), j - 1)
                    A(prob[0][:, 0, j % 2, :], tiles[j][0], ACT.Square).then_inc(sem("a_sq"), 1)

                def head_root(j):
                    act.wait_ge(sem("a_ms"), j + 1)
                    if j >= 2:
                        act.wait_ge(sem("a_nrm"), j - 1)
                    y = prob[0][:, 1, j % 2, :]
                    A(y, wk[j % 2][:, 0:T], ACT.Ln, bias=epsc[:, 0:1]).then_inc(sem("a_ln"), 1)
                    act.wait_ge(sem("a_ln"), j + 1)
                    A(y, y, ACT.Exp, scale=-0.5).then_inc(sem("a_rs"), 1)

                if L == 0:
                    head_square(0)
                    for j in range(len(tiles)):
                        if j + 1 < len(tiles):
                            head_square(j + 1)
                        head_root(j)
                        if j == 1:
                            keys_high()
                else:
                    keys_high()

                def q_high(s):
                    tok = T if L == 0 else NX
                    u = next(x for x in units if x["set"] == s)
                    act.wait_ge(*na("rope", L, 1 + 2 * u["hp"] + 2))
                    if s >= 2:
                        last = max(i for i, x in enumerate(units) if x["set"] == s - 2)
                        act.wait_ge(*na("S", L, 2 * (last + 1)))
                    src = qsrc(L, u["g"], u["hp"])
                    for half in range(2):
                        A(qst[L][64 * half:64 * half + 64, s % 2, 0, :, 0:tok], src[:, :, 0:tok], ACT.Copy) \
                            .then_inc(sem("a_qhi"), 1)

                def exps(i):
                    u = units[i]
                    c0, n = u["c0"], u["n"]
                    act.wait_ge(*na("nb", L, i + 1))
                    if i >= 2:
                        act.wait_ge(*na("T", L, units[i - 2]["kp0"] + units[i - 2]["kp"]))
                        act.wait_ge(*na("ri", L, i - 1))
                    for h in range(2):
                        A(prob[L][:, i % 2, h, 0:n], lin[h][:, c0:c0 + n], ACT.Exp, scale=HD ** -0.5,
                          bias=st_nb[:, i % 2, h:h + 1], accum_out=st_sum[:, i % 2, h:h + 1]) \
                            .then_inc(sem("a_exp"), 1)
                    if L == 1:
                        head = 8 * u["g"] + 2 * u["hp"]
                        for h in range(2):
                            A(st_sk[:, i % 2, h:h + 1], par[:, PC_SINK + head + h:PC_SINK + head + h + 1], ACT.Exp,
                              bias=st_nb[:, i % 2, h:h + 1]).then_inc(sem("a_sk"), 1)

                def pt_copy(i, kp):
                    u = units[i]
                    w = min(2, len(u["tiles"]) - 2 * kp) * 256
                    act.wait_ge(*na("T", L, u["kp0"] + kp + 1))
                    if i >= 1:
                        act.wait_ge(*na("O", L, i))
                    j = u["kp0"] + kp
                    A(probT[L][:, kp, 0:w], wk[0][:, 512 * (j % 2):512 * (j % 2) + w], ACT.Copy) \
                        .then_inc(sem("a_ptA"), 1)

                def out_copy(i):
                    act.wait_ge(*na("O", L, i + 1))
                    if i >= 2:
                        act.wait_ge(*na("olo", L, i - 1))
                    A(osum[0:64, i % 2, 0, :], wk[1][64:128, 512 * (i % 2):512 * (i % 2) + 256], ACT.Copy) \
                        .then_inc(sem("a_ocp"), 1)

                def out_high(i):
                    u = units[i]
                    act.wait_ge(*na("oadd", L, i + 1))
                    A(mix_rows(L, u["g"], u["hp"], u["qt"])[0],
                      osum[0:64, i % 2, 1, :].rearrange("p (h q) -> p h q", h=2), ACT.Copy) \
                        .then_inc(sem("a_ohi"), 1)

                q_high(0)
                exps(0)
                for i in range(len(units)):
                    u = units[i]
                    if u["qt"] == 1 and u["set"] + 1 <= units[-1]["set"]:
                        q_high(u["set"] + 1)
                    pt_copy(i, 0)
                    if i + 1 < len(units):
                        exps(i + 1)
                    if u["kp"] > 2:
                        pt_copy(i, 2)
                    out_copy(i)
                    out_high(i)

            def gla():
                for i in range(4):
                    act.wait_ge(sem("g_z"), i + 1)
                    z = (lin[i] if i < 2 else wk[i - 2])[:, 0:T]
                    A(gsc[:, i, :], z, ACT.Abs, bias=par[:, PC_GKB + i:PC_GKB + i + 1]).then_inc(sem("g_abs"), 1)
                    A(dec[:, i, :], z, ACT.Identity, bias=par[:, PC_GKB + i:PC_GKB + i + 1]) \
                        .then_inc(sem("g_zc"), 1)
                for i in range(4):
                    act.wait_ge(sem("g_abs"), i + 1)
                    A(gsc[:, i, :], gsc[:, i, :], ACT.Exp, scale=-1.0).then_inc(sem("g_exp"), 1)
                for tt in range(0, 6, 2):
                    act.wait_ge(sem("g_vT"), tt + 1)
                    A(vgt[:, tt, :], lin[0][:, 0:512], ACT.Copy).then_inc(sem("g_vcpA"), 1)
                for i in range(4):
                    act.wait_ge(sem("g_exp"), i + 1)
                    A(gsc[:, 4 + i, :], gsc[:, i, :], ACT.Ln, bias=epsc[:, 1:2]).then_inc(sem("g_ln"), 1)
                act.wait_ge(sem("g_ref"), 8)
                A(ge[:, 0, :, :], gd[:, :, :], ACT.Exp, scale=1.0 / TAU).then_inc(sem("g_refe"), 1)
                act.wait_ge(sem("g_ref"), 12)
                A(ge[:, 1, :, :], ge[:, 1, :, :], ACT.Exp, scale=1.0 / TAU).then_inc(sem("g_refe"), 1)
                A(ge[:, 2, :, :], ge[:, 2, :, :], ACT.Exp, scale=1.0 / TAU).then_inc(sem("g_refe"), 1)
                for i in range(4):
                    act.wait_ge(sem("g_dc"), i + 1)
                    A(gsc[:, i, :], dec[:, i, :], ACT.Exp, scale=1.0 / TAU).then_inc(sem("g_e1"), 1)
                    A(gsc[:, 4 + i, :], dec[:, i, :], ACT.Exp, scale=-1.0 / TAU).then_inc(sem("g_e2"), 1)
                for i in range(0, 4, 2):
                    act.wait_ge(sem("g_kT"), i + 1)
                    A(kgt[:, i, :, :], lin[0][:, 0:T].rearrange("p (t d) -> p t d", d=P), ACT.Copy) \
                        .then_inc(sem("g_kcpA"), 1)
                for pr in range(6):
                    act.wait_ge(sem("g_O"), pr + 1)
                    src = wk[pr % 2].rearrange("p (half x) -> p half x", half=2)
                    src = src[:, :, 0:256].rearrange("p half (h t) -> p h half t", h=4)
                    A(og[:, :, pr * P:pr * P + P].rearrange("p h (half t) -> p h half t", half=2), src, ACT.Copy) \
                        .then_inc(sem("g_ocp"), 1)
                act.wait_ge(sem("g_oi"), 2 * (NCH - 1))
                for t in range(6):
                    if t < 4:
                        if t >= 2:
                            act.wait_ge(sem("g_ms"), t - 1)
                        A(big[:, 4 + t % 2, :], og[:, t, :], ACT.Square).then_inc(sem("g_sq"), 1)
                    if 1 <= t < 5:
                        act.wait_ge(sem("g_ms"), t)
                        if t >= 3:
                            act.wait_ge(sem("g_on"), t - 2)
                        y = big[:, 6 + (t - 1) % 2, :]
                        A(y, wk[(t - 1) % 2][:, 0:T], ACT.Ln, bias=epsc[:, 0:1]).then_inc(sem("g_nln"), 1)
                        act.wait_ge(sem("g_nln"), t)
                        A(y, y, ACT.Exp, scale=-0.5).then_inc(sem("g_rs"), 1)
                    if t >= 2:
                        act.wait_ge(sem("g_of"), t - 1)
                        A(hhA[:, t - 2, :], gt[:, t - 2, :], ACT.Copy).then_inc(sem("g_hi"), 1)

            for n, b in enumerate(BLOCKS):
                kind, L = b["kind"], b["layer"]
                if n == FIRST[("out", 0)]:
                    fence(act, "act", 1)
                    attention(0)
                    fence(act, "act", 2)
                    gla()
                    fence(act, "act", 3)
                if n == FIRST[("out", 1)]:
                    fence(act, "act", 4)
                    attention(1)
                    fence(act, "act", 5)
                if (kind, L) in NORM_FOR and n == FIRST[(kind, L)] and n > 0:
                    norm_high(NORM[NORM_FOR[(kind, L)]])
                high(n + 2)
                if kind == "proj":
                    mixer_projection(L, n, b)
                    if L == 0:
                        ada_copy(ADA_EARLY + n)
                        if n == 18:
                            ada_copy(2 * NADA - 1)
                elif kind == "w1":
                    i = (n - FIRST[("w1", L)])
                    act.wait_ge(sem("s_acc"), n + 1)
                    j = b["h"] + FT * L
                    if j >= 2:
                        act.wait_ge(sem("s_gl"), j - 1)
                    A(tmps[:, 4 + b["h"] % 2, 0:b["tok"]], lin[n % 2][:, 0:b["tok"]], ACT.Silu).then_inc(ev(n)[0], 1)
                elif kind == "w3":
                    act.wait_ge(*ev(n))
                    A(gh[:, b["i"], 0:b["tok"]], tmps[:, 6 + b["h"] % 2, 0:b["tok"]], ACT.Copy) \
                        .then_inc(sem("s_gh"), 1)
                elif kind == "out" or (kind == "w2" and b["g"] == len(GROUPS) - 1):
                    q = {("out", 0): 1, ("w2", 0): 2, ("out", 1): 3, ("w2", 1): 4}[(kind, L)]
                    act.wait_ge(*ev(n))
                    square(q, b["m"], NORM[q]["tok"])
            root(4, NX)

        @block.vector
        def _(dve):
            V = nc.vector
            TT, TS, STT = V.tensor_tensor, V.tensor_scalar, V.scalar_tensor_tensor

            V.memset(epsc[:, 0:1], EPS)
            V.memset(epsc[:, 1:2], 1.0)
            V.memset(cpad[:, :, :], 0.0).then_inc(sem("s_cpad0"), 1)

            def ada_reduce(c):
                layer, cc = divmod(c, NADA)
                dve.wait_ge(sem("s_adaT"), c + 1)
                dst = mod[:, layer, 4 * cc:4 * cc + 4, :]
                src = wk[1][:, 512 * (c % 2):512 * (c % 2) + 512].rearrange("p (q g r) -> p q r g", g=4, r=32)
                V.tensor_reduce(dst, src[:, :, 0:2, :], AX.X, ALU.add).then_inc(sem("s_adar"), 1)
                dve.wait_ge(sem("s_adar"), c + 1)
                bias = par[:, PC_ADAB + 48 * layer + 4 * cc:PC_ADAB + 48 * layer + 4 * cc + 4]
                TT(dst, dst, bias.unsqueeze(2).to_broadcast([P, 4, 2]), ALU.add).then_inc(sem("s_mod"), 1)

            def mod_scale(a):
                layer, second = divmod(a, 2)
                c0 = 32 if second else 8
                gain = par[:, PC_N + KT * a:PC_N + KT * a + KT].unsqueeze(2).to_broadcast([P, KT, 2])
                STT(out=modA[:, a, :, :], in0=mod[:, layer, c0:c0 + KT, :], scalar=1.0, in1=gain, op0=ALU.add,
                    op1=ALU.mult).then_inc(sem("s_modA"), 1)

            def add_square(q, k, tok):
                if k == 0:
                    return
                dve.wait_ge(*nq("sq", q, k + 1))
                if k > 1:
                    dve.wait_ge(*nq("sqadd", q, k - 1))
                acc = norm_tmp(q, 0)[:, 0:tok]
                TT(acc, acc, norm_tmp(q, 1 + k % 2)[:, 0:tok], ALU.add).then_inc(sem("s_sqadd"), 1)

            def rstd(q, tok):
                dve.wait_ge(*nq("rs", q, 1))

            def norm_apply(nd):
                q, tok = nd["q"], nd["tok"]
                rstd(q, tok)
                dve.wait_ge(sem("s_modA"), 1 if q == 0 else 4)

                def scaled(k):
                    if k >= 2:
                        dve.wait_ge(*nq("nhh", q, len(parts(tok)) * (k - 1)))
                    TT(norm_tmp(q, 4 + k % 2)[:, 0:tok], xT[:, k, 0:tok], norm_tmp(q, 3)[:, 0:tok], ALU.mult) \
                        .then_inc(sem("s_nt"), 1)

                scaled(0)
                for k in range(KT):
                    if k + 1 < KT:
                        scaled(k + 1)
                    dve.wait_ge(*nq("nt", q, k + 1))
                    if k >= 2:
                        dve.wait_ge(*nq("nhl", q, k - 1))
                    for c, a, b in parts(tok):
                        TS(norm_tmp(q, 6 + k % 2)[:, a:b], norm_tmp(q, 4 + k % 2)[:, a:b],
                           modA[:, nd["a"], k, c:c + 1], mod[:, nd["layer"], nd["sh"] + k, c:c + 1],
                           ALU.mult, ALU.add).then_inc(sem("s_nhf"), 1)
                    dve.wait_ge(*nq("nhf", q, len(parts(tok)) * (k + 1)))
                    dve.wait_ge(*nq("nhh", q, len(parts(tok)) * (k + 1)))
                    TT(hl(k)[:, 0:tok], norm_tmp(q, 6 + k % 2)[:, 0:tok], hh(k)[:, 0:tok].bitcast(F32),
                       ALU.subtract).then_inc(sem("s_nhl"), 1)

            dve.wait_ge(sem("s_par"), 16)
            for k in range(KT):
                if k == 1:
                    dve.wait_ge(*nq("sq", 0, 1))
                add_square(0, k, T)
            for c in range(ADA_EARLY):
                ada_reduce(c)
            dve.wait_ge(sem("s_mod"), ADA_EARLY)
            mod_scale(0)
            norm_apply(NORM[0])

            def attention(L):
                units = U[L]
                tiles = prep_tiles(L)

                def normed(j):
                    t, g = tiles[j]
                    dve.wait_ge(sem("a_rs"), j + 1)
                    STT(out=t, in0=t, scalar=par[:, g:g + 1], in1=prob[0][:, 1, j % 2, :], op0=ALU.mult,
                        op1=ALU.mult).then_inc(sem("a_nrm"), 1)

                def roped(j):
                    t = tiles[j][0][:, 0:NX]
                    dve.wait_ge(*na("rot", L, j + 1))
                    rs_ = ropet[L][:, j % 2, 0:NX]
                    TT(rs_, lin[j % 2][:, 0:NX], sin, ALU.mult).then_inc(sem("a_rsin"), 1)
                    TT(t, t, cos, ALU.mult).then_inc(sem("a_rcos"), 1)
                    dve.wait_ge(*na("rsin", L, j + 1))
                    dve.wait_ge(*na("rcos", L, j + 1))
                    TT(t, t, rs_, ALU.add).then_inc(sem("a_rope"), 1)

                def keys_low():
                    dve.wait_ge(*na("rope", L, 1))
                    dve.wait_ge(*na("khi", L, 2))
                    k_ = ksrc(L)
                    for g in range(2):
                        a, b = 64 * g, 64 - 64 * g
                        TT(kst[L][b:b + 64, g, :], k_[a:a + 64, :], kst[L][a:a + 64, g, :].bitcast(F32),
                           ALU.subtract).then_inc(sem("a_klo"), 1)

                dve.wait_ge(sem("s_con"), 32)
                if L == 0:
                    normed(0)
                for j in range(len(tiles)):
                    if L == 0 and j + 1 < len(tiles):
                        normed(j + 1)
                    roped(j)
                    if j == 0:
                        keys_low()
                        dve.wait_ge(*na("vps", L, 1))
                        if L == 0:
                            dve.wait_ge(sem("a_klo"), 2)
                        V.tensor_copy(vtok[L][:, :, :], lin[1][:, 0:T].rearrange("p (t d) -> p t d", d=P)) \
                            .then_inc(sem("a_vtok"), 1)

                def q_low(s):
                    tok = T if L == 0 else NX
                    u = next(x for x in units if x["set"] == s)
                    g = u["g"]
                    dve.wait_ge(*na("qhi", L, 2 * (s + 1)))
                    src = qsrc(L, g, u["hp"])
                    for half in range(2):
                        for h in range(2):
                            TT(qst[L][64 * half:64 * half + 64, s % 2, 1, h, 0:tok], src[:, h, 0:tok],
                               qst[L][64 * g:64 * g + 64, s % 2, 0, h, 0:tok].bitcast(F32), ALU.subtract) \
                                .then_inc(sem("a_qlo"), 1)

                def maxima(i):
                    u = units[i]
                    c0, n = u["c0"], u["n"]
                    for h in range(2):
                        dve.wait_ge(*na("S", L, 2 * i + h + 1))
                        V.reduce_max(st_mx[:, i % 2, h:h + 1], lin[h][:, c0:c0 + n], AX.X).then_inc(sem("a_mx"), 1)
                    dve.wait_ge(*na("mx", L, 2 * i + 2))
                    if L == 0:
                        TS(st_nb[:, i % 2, :], st_mx[:, i % 2, :], -HD ** -0.5, None, ALU.mult) \
                            .then_inc(sem("a_nb"), 1)
                    else:
                        head = 8 * u["g"] + 2 * u["hp"]
                        STT(out=st_mx[:, i % 2, :], in0=st_mx[:, i % 2, :], scalar=HD ** -0.5,
                            in1=par[:, PC_SINK + head:PC_SINK + head + 2], op0=ALU.mult, op1=ALU.max) \
                            .then_inc(sem("a_smax"), 1)
                        dve.wait_ge(sem("a_smax"), i + 1)
                        TS(st_nb[:, i % 2, :], st_mx[:, i % 2, :], -1.0, None, ALU.mult).then_inc(sem("a_nb"), 1)

                def normalise(i):
                    u = units[i]
                    n = u["n"]
                    dve.wait_ge(*na("exp", L, 2 * i + 2))
                    if L == 1:
                        dve.wait_ge(sem("a_sk"), 2 * i + 2)
                        TT(st_sum[:, i % 2, :], st_sum[:, i % 2, :], st_sk[:, i % 2, :], ALU.add) \
                            .then_inc(sem("a_sum"), 1)
                        dve.wait_ge(sem("a_sum"), i + 1)
                    V.reciprocal(st_ri[:, i % 2, :], st_sum[:, i % 2, :]).then_inc(sem("a_ri"), 1)
                    dve.wait_ge(*na("ri", L, i + 1))
                    for h in range(2):
                        TS(prob[L][:, i % 2, h, 0:n], prob[L][:, i % 2, h, 0:n], st_ri[:, i % 2, h:h + 1], None,
                           ALU.mult).then_inc(sem("a_nrmp"), 1)

                def pt_copy(i, kp):
                    u = units[i]
                    w = min(2, len(u["tiles"]) - 2 * kp) * 256
                    dve.wait_ge(*na("T", L, u["kp0"] + kp + 1))
                    if i >= 1:
                        dve.wait_ge(*na("O", L, i))
                    j = u["kp0"] + kp
                    V.tensor_copy(probT[L][:, kp, 0:w], wk[0][:, 512 * (j % 2):512 * (j % 2) + w]) \
                        .then_inc(sem("a_ptD"), 1)

                def out_sum(i):
                    dve.wait_ge(*na("ocp", L, i + 1))
                    TT(osum[0:64, i % 2, 1, :], wk[1][0:64, 512 * (i % 2):512 * (i % 2) + 256],
                       osum[0:64, i % 2, 0, :], ALU.add).then_inc(sem("a_oadd"), 1)

                def out_low(i):
                    u = units[i]
                    dve.wait_ge(*na("ohi", L, i + 1))
                    h_, l_ = mix_rows(L, u["g"], u["hp"], u["qt"])
                    if u["g"] == 0:
                        TT(l_, osum[0:64, i % 2, 1, :].rearrange("p (h q) -> p h q", h=2), h_.bitcast(F32),
                           ALU.subtract).then_inc(sem("a_olo"), 1)
                    else:
                        V.tensor_copy(osum[64:128, i % 2, 1, :], osum[0:64, i % 2, 1, :]).then_inc(sem("a_shift"), 1)
                        cnt = sum(1 for x in units[:i + 1] if x["g"] == 1) + \
                            (sum(1 for x in U[0] if x["g"] == 1) if L == 1 else 0)
                        dve.wait_ge(sem("a_shift"), cnt)
                        TT(l_, osum[64:128, i % 2, 1, :].rearrange("p (h q) -> p h q", h=2), h_.bitcast(F32),
                           ALU.subtract).then_inc(sem("a_olo"), 1)

                q_low(0)
                maxima(0)
                normalise(0)
                for i in range(len(units)):
                    u = units[i]
                    if u["qt"] == 1 and u["set"] + 1 <= units[-1]["set"]:
                        q_low(u["set"] + 1)
                    if u["kp"] > 1:
                        pt_copy(i, 1)
                    if i + 1 < len(units):
                        maxima(i + 1)
                        normalise(i + 1)
                    out_sum(i)
                    out_low(i)

            def gla():
                for d in range(2):
                    V.memset(cmask[:, d, :], 1.0).then_inc(sem("g_cm"), 1)
                dve.wait_ge(sem("g_cm"), 2)
                for d in range(2):
                    V.memset(cmask[:, d, :].rearrange("p (c t) -> p c t", t=CH)[:, :, (CH - 1) * d], 0.0) \
                        .then_inc(sem("g_cm"), 1)
                for tt in range(1, 6, 2):
                    dve.wait_ge(sem("g_vT"), tt + 1)
                    V.tensor_copy(vgt[:, tt, :], lin[1][:, 0:512]).then_inc(sem("g_vcpD"), 1)
                for i in range(4):
                    dve.wait_ge(sem("g_ln"), i + 1)
                    STT(out=dec[:, i, :], in0=dec[:, i, :], scalar=0.0, in1=gsc[:, 4 + i, :], op0=ALU.min,
                        op1=ALU.subtract).then_inc(sem("g_dec"), 1)
                dve.wait_ge(sem("g_cm"), 4)
                for i in range(4):
                    dve.wait_ge(sem("g_dec"), i + 1)
                    if i < 2:
                        V.tensor_tensor_scan(gsc[:, i, :], cmask[:, 0, :], dec[:, i, :], 0.0, ALU.mult, ALU.add) \
                            .then_inc(sem("g_scan"), 1)
                    else:
                        V.tensor_tensor_scan(gsc[:, i, T - 1::-1], cmask[:, 1, T - 1::-1], dec[:, i, T - 1::-1], 0.0,
                                             ALU.mult, ALU.add).then_inc(sem("g_scan"), 1)

                def chunks(i):
                    return gsc[:, i, :].rearrange("p (c t) -> p c t", t=CH)

                dve.wait_ge(sem("g_scan"), 4)
                for i in range(4):
                    V.tensor_copy(gd[:, i, :], chunks(i)[:, :, CH // 2 - 1]).then_inc(sem("g_ref"), 1)
                for i in range(4):
                    last = (CH - 1) if i < 2 else 0
                    V.tensor_copy(ge[:, 1, i, :], chunks(i)[:, :, last]).then_inc(sem("g_ref"), 1)
                for i in range(4):
                    last = (CH - 1) if i < 2 else 0
                    TT(ge[:, 2, i, :], chunks(i)[:, :, last], chunks(i)[:, :, CH // 2 - 1], ALU.subtract) \
                        .then_inc(sem("g_ref"), 1)
                dve.wait_ge(sem("g_ref"), 4)
                for i in range(4):
                    TT(dec[:, i, :].rearrange("p (c t) -> p c t", t=CH), chunks(i),
                       gd[:, i, :].unsqueeze(2).to_broadcast([P, NCH, CH]), ALU.subtract).then_inc(sem("g_d"), 1)
                for i in range(4):
                    dve.wait_ge(sem("g_d"), i + 1)
                    TS(dec[:, i, :], dec[:, i, :], -CLAMP, CLAMP, ALU.max, ALU.min).then_inc(sem("g_dc"), 1)
                for i in range(4):
                    g2 = i % 2
                    dve.wait_ge(sem("g_e1"), i + 1)
                    TT(gsc[:, i, :], gsc[:, i, :], big[:, g2, :], ALU.mult).then_inc(sem("g_qe"), 1)
                    dve.wait_ge(sem("g_e2"), i + 1)
                    TT(gsc[:, 4 + i, :], gsc[:, 4 + i, :], big[:, 2 + g2, :], ALU.mult).then_inc(sem("g_ke"), 1)
                for i in range(1, 4, 2):
                    dve.wait_ge(sem("g_kT"), i + 1)
                    V.tensor_copy(kgt[:, i, :, :], lin[1][:, 0:T].rearrange("p (t d) -> p t d", d=P)) \
                        .then_inc(sem("g_kcpD"), 1)
                for pr in range(6):
                    dve.wait_ge(sem("g_A"), pr + 1)
                    if pr >= 2:
                        dve.wait_ge(sem("g_O"), pr - 1)
                    ps = psum[:, 0:2048].rearrange("p (r x) -> p r x", r=4)
                    ps = [ps[:, :, P * d:P * d + P].rearrange("p r (g t) -> p r g t", g=2) for d in range(2)]
                    bc = [m_.unsqueeze(1).unsqueeze(1).to_broadcast([P, 4, 2, CH]) for m_ in mgla]
                    o_ = attnT[:, pr % 2, :].rearrange("p (r g t) -> p r g t", r=4, g=2)
                    TT(o_, ps[0], bc[0], ALU.mult).then_inc(sem("g_am"), 1)
                    if pr >= 1:
                        dve.wait_ge(sem("g_at"), pr)
                    TT(attnM[:, :].rearrange("p (r g t) -> p r g t", r=4, g=2), ps[1], bc[1], ALU.mult) \
                        .then_inc(sem("g_am2"), 1)
                    dve.wait_ge(sem("g_am"), pr + 1)
                    dve.wait_ge(sem("g_am2"), pr + 1)
                    TT(attnT[:, pr % 2, :], attnT[:, pr % 2, :], attnM[:, :], ALU.add).then_inc(sem("g_at"), 1)
                dve.wait_ge(sem("g_refe"), 3)
                dve.wait_ge(sem("g_ocp"), 6)
                nst = 0
                for s in range(NCH):
                    for d in range(2):
                        c = NSEQ[d][s]
                        j = 2 * s + d
                        if s >= 1:
                            dve.wait_ge(sem("g_I"), 2 * (s - 1) + d + 1)
                            o_ = og[:, :, c * CH:c * CH + CH].rearrange("p (g b) t -> p b g t", b=2)
                            if d == 1 or s >= 2:
                                dve.wait_ge(sem("g_oi"), 2 * (s - 1) + d)
                            give = (lin[1] if d == 0 else wk[1]).rearrange("p (b x) -> p b x", b=2)
                            give = give[:, :, 0:2 * CH].rearrange("p b (g t) -> p b g t", g=2)
                            TT(o_, o_, give, ALU.add) \
                                .then_inc(sem("g_oi"), 1)
                        if s == NCH - 1:
                            continue
                        dve.wait_ge(sem("g_U"), j + 1)
                        gi = slice(2 * d, 2 * d + 2)
                        new = state[:, d, (s + 1) % 2, :, :]
                        old = state[:, d, s % 2, :, :]
                        kept, upd = supd[:, d, 0, :, :], supd[:, d, 1, :, :]
                        el = ge[:, 1, gi, c:c + 1].to_broadcast([P, 2, CH])
                        U_ = (wk[0] if d == 0 else lin[0])[:, 0:512]
                        if s >= 2:
                            dve.wait_ge(sem("g_st"), 2 * (s - 2) + d + 1)
                        for r in range(4):
                            rows = slice(32 * r, 32 * r + 32)
                            tgt = upd if s >= 1 else new
                            TT(tgt[rows], U_[rows, :].rearrange("p (g v) -> p g v", g=2)[:, :, 64 * r:64 * r + 64],
                               ge[rows, 2, gi, c:c + 1].to_broadcast([32, 2, CH]), ALU.mult) \
                                .then_inc(sem("g_ud"), 1)
                        if s >= 1:
                            TT(kept, old, el, ALU.mult).then_inc(sem("g_uk"), 1)
                            dve.wait_ge(sem("g_ud"), 4 * (j + 1))
                            dve.wait_ge(sem("g_uk"), 2 * (s - 1) + d + 1)
                            TT(new, kept, upd, ALU.add).then_inc(sem("g_st"), 1)
                            dve.wait_ge(sem("g_st"), 2 * (s - 1) + d + 1)
                        else:
                            dve.wait_ge(sem("g_ud"), 4 * (j + 1))
                        cn = NSEQ[d][s + 1]
                        if s >= 1:
                            dve.wait_ge(sem("g_I"), 2 * (s - 1) + d + 1)
                        TT(statr[:, d, :, :], new, ge[:, 0, gi, cn:cn + 1].to_broadcast([P, 2, CH]), ALU.mult) \
                            .then_inc(sem("g_sr"), 1)
                for t in range(4):
                    dve.wait_ge(sem("g_rs"), t + 1)
                    TT(og[:, t, :], og[:, t, :], big[:, 6 + t % 2, :], ALU.mult).then_inc(sem("g_on"), 1)
                    dve.wait_ge(sem("g_on"), t + 1)
                    STT(out=gt[:, t, :], in0=og[:, t, :], scalar=par[:, PC_GLAG:PC_GLAG + 1], in1=big[:, 8 + t, :],
                        op0=ALU.mult, op1=ALU.mult).then_inc(sem("g_of"), 1)
                    dve.wait_ge(sem("g_hi"), t + 1)
                    TT(hlA[:, t, :], gt[:, t, :], hhA[:, t, :].bitcast(F32), ALU.subtract).then_inc(sem("g_lo"), 1)

            def residual(n, b, gate):
                L, m = b["layer"], b["m"]
                dve.wait_ge(sem("s_acc"), n + 1)
                if n >= 1 and BLOCKS[n - 1]["kind"] == "x":
                    pass
                for c, a, e in parts(b["tok"]):
                    ins = STT(out=xT[:, m, a:e], in0=lin[n % 2][:, a:e], scalar=mod[:, L, gate + m, c:c + 1],
                              in1=xT[:, m, a:e], op0=ALU.mult, op1=ALU.add)
                ins.then_inc(ev(n)[0], 1)

            for n, b in enumerate(BLOCKS):
                kind, L = b["kind"], b["layer"]
                if n == FIRST[("out", 0)]:
                    ada_reduce(2 * NADA - 1)
                    dve.wait_ge(sem("s_mod"), 2 * NADA)
                    for a in range(1, 4):
                        mod_scale(a)
                    fence(dve, "dve", 1)
                    attention(0)
                    fence(dve, "dve", 2)
                    gla()
                    fence(dve, "dve", 3)
                if n == FIRST[("out", 1)]:
                    fence(dve, "dve", 4)
                    attention(1)
                    fence(dve, "dve", 5)
                if (kind, L) in NORM_FOR and n == FIRST[(kind, L)] and n > 0:
                    add_square(NORM_FOR[(kind, L)], KT - 1, NORM[NORM_FOR[(kind, L)]]["tok"])
                    norm_apply(NORM[NORM_FOR[(kind, L)]])
                if kind == "proj" and L == 0:
                    ada_reduce(ADA_EARLY + n)
                elif kind == "w3":
                    j = b["h"] + FT * L
                    dve.wait_ge(sem("s_acc"), n + 1)
                    dve.wait_ge(*ev(n - 1))
                    TT(tmps[:, 6 + b["h"] % 2, 0:b["tok"]], tmps[:, 4 + b["h"] % 2, 0:b["tok"]],
                       lin[n % 2][:, 0:b["tok"]], ALU.mult).then_inc(ev(n)[0], 1)
                    dve.wait_ge(*ev(n))
                    dve.wait_ge(sem("s_gh"), j + 1)
                    TT(gl[:, b["i"], 0:b["tok"]], tmps[:, 6 + b["h"] % 2, 0:b["tok"]],
                       gh[:, b["i"], 0:b["tok"]].bitcast(F32), ALU.subtract).then_inc(sem("s_gl"), 1)
                elif kind in ("out", "w2"):
                    if kind == "w2" or n == FIRST[(kind, L)]:
                        pass
                    if kind == "w2" and b["g"] > 0:
                        dve.wait_ge(*ev(n - (BLOCKS[n]["nk"] * 2 + KT)))
                    residual(n, b, 16 if kind == "out" else 40)
                    if (kind == "out" or b["g"] == len(GROUPS) - 1) and b["m"] >= 1:
                        q = {("out", 0): 1, ("w2", 0): 2, ("out", 1): 3, ("w2", 1): 4}[(kind, L)]
                        add_square(q, b["m"] - 1, NORM[q]["tok"])
            add_square(4, KT - 1, NX)
            dve.wait_ge(*nq("nhl", 3, KT))
            rstd(4, NX)
            for k in range(KT):
                STT(out=big[:, k, 0:NX], in0=xT[:, k, 0:NX], scalar=par[:, PC_FIN + k:PC_FIN + k + 1],
                    in1=norm_tmp(4, 3)[:, 0:NX], op0=ALU.mult, op1=ALU.mult).then_inc(sem("s_fin"), 1)

        @block.tensor
        def _(pe):
            MM, TR = nc.tensor.matmul, nc.tensor.transpose

            def ada_mm(c):
                if c >= 2:
                    pe.wait_ge(sem("s_adacp"), c - 1)
                for half in range(2):
                    h = 2 * c + half
                    pe.wait_ge(sem(f"s_adaload{h % ADA_RING}"), 16 * (h // ADA_RING + 1))
                    for g in range(4):
                        last = MM(wk[0][32 * g:32 * g + 32, 512 * (c % 2):512 * (c % 2) + 512],
                                  cpad[:, 4 * half + g, :], ada_w[:, h % ADA_RING, g, :], start=half == 0,
                                  stop=half == 1, skip_group_check=True)
                    last.then_inc(sem("s_adamm"), 1)

            def ada_T(c):
                pe.wait_ge(sem("s_adacp"), c + 1)
                if c >= 2:
                    pe.wait_ge(sem("s_mod"), c - 1)
                for q in range(4):
                    last = TR(wk[1][:, 512 * (c % 2) + P * q:512 * (c % 2) + P * q + P],
                              adasb[:, c % 2, q * P:q * P + P], ident)
                last.then_inc(sem("s_adaT"), 1)

            def block_product(n):
                b = BLOCKS[n]
                kind, L, tok = b["kind"], b["layer"], b["tok"]
                s = n % RING
                pe.wait_ge(sem("s_hi"), n + 1)
                pe.wait_ge(sem("s_lo"), n + 1)
                if n >= 2:
                    pe.wait_ge(*ev(n - 2))
                q = NORM_FOR.get((kind, L)) if n == FIRST[(kind, L)] else None
                out_ = lin[n % 2]
                for k in range(b["nk"]):
                    if q is not None:
                        np_ = len(parts(NORM[q]["tok"]))
                        pe.wait_ge(*nq("nhh", q, np_ * (k + 1)))
                        pe.wait_ge(*nq("nhl", q, k + 1))
                    if kind == "w2" and b["m"] == 0:
                        j = GROUPS[b["g"]][0] + FT * L + k + 1
                        pe.wait_ge(sem("s_gh"), j)
                        pe.wait_ge(sem("s_gl"), j)
                    hi_, lo_ = (gh[:, k, :], gl[:, k, :]) if kind == "w2" else (hh(k), hl(k))
                    wh_, wl_ = whi[:, s, k * P:k * P + P], wlo[:, s, k * P:k * P + P]
                    first, end = k == 0, k == b["nk"] - 1
                    for j, (w_, a_) in enumerate(((wh_, hi_), (wh_, lo_), (wl_, hi_))):
                        for _, t0, t1 in parts(tok):
                            last = MM(out_[:, t0:t1], w_, a_[:, t0:t1], start=first and j == 0, stop=end and j == 2)
                last.then_inc(sem("s_acc"), 1)

            def mean_square(q, tok):
                pe.wait_ge(*nq("sqadd", q, KT - 1))
                for _, a, b in parts(tok):
                    last = MM(wk[0][:, a:b], ones, norm_tmp(q, 0)[:, a:b], start=True, stop=True)
                last.then_inc(sem("s_nps"), 1)

            pe.wait_ge(sem("s_cpad"), 1)
            pe.wait_ge(sem("s_con"), 32)
            for c in range(ADA_EARLY):
                ada_mm(c)
                if c >= 1:
                    ada_T(c - 1)
            ada_T(ADA_EARLY - 1)
            pe.wait_ge(sem("s_adacp"), ADA_EARLY)
            mean_square(0, T)

            def attention(L):
                units = U[L]
                tiles = prep_tiles(L)

                def means(j):
                    pe.wait_ge(sem("a_sq"), j + 1)
                    if j >= 2:
                        pe.wait_ge(sem("a_rs"), j - 1)
                    for a, b in ((0, NX), (NX, T)):
                        last = MM(wk[j % 2][:, a:b], blk, prob[0][:, 0, j % 2, a:b], start=True, stop=True)
                    last.then_inc(sem("a_ms"), 1)

                def rotated(j):
                    if L == 0:
                        pe.wait_ge(sem("a_nrm"), j + 1)
                    if j >= 2:
                        pe.wait_ge(*na("rsin", L, j - 1))
                    if j == 1:
                        pe.wait_ge(*na("vtok", L, 1))
                    MM(lin[j % 2][:, 0:NX], rot, tiles[j][0][:, 0:NX], start=True, stop=True) \
                        .then_inc(sem("a_rot"), 1)

                if L == 0:
                    means(0)
                    means(1)
                for tt in range(6):
                    last = TR(lin[1][:, tt * P:tt * P + P], vsrc(L)[:, tt * P:tt * P + P], ident)
                last.then_inc(sem("a_vps"), 1)
                for j in range(len(tiles)):
                    rotated(j)
                    if L == 0 and j + 2 < len(tiles):
                        means(j + 2)

                def scores(i):
                    u = units[i]
                    s, qt, g = u["set"], u["qt"], u["g"]
                    pe.wait_ge(*na("qlo", L, 4 * (s + 1)))
                    for h in range(2):
                        if i == 0:
                            pe.wait_ge(*na("klo", L, 2))
                            pe.wait_ge(*na("rope", L, len(tiles)))
                        else:
                            pe.wait_ge(*na("exp", L, 2 * (i - 1) + h + 1))
                        for c, (col, key, w) in enumerate(u["segs"]):
                            masked = u["mask"] is not None and c == 1
                            for part in range(2):
                                last = MM(lin[h][:, col:col + w], qst[L][:, s % 2, part, h, qt * P:qt * P + P],
                                          kst[L][:, g, key:key + w], start=part == 0, stop=part == 1 and not masked)
                            if masked:
                                last = MM(lin[h][:, col:col + w], identr[:, :], bandm[:, u["mask"]:u["mask"] + w],
                                          start=False, stop=True)
                        last.then_inc(sem("a_S"), 1)

                def transposed(i):
                    u = units[i]
                    nt = len(u["tiles"])
                    pe.wait_ge(*na("nrmp", L, 2 * i + 2))
                    for kp in range(u["kp"]):
                        j = u["kp0"] + kp
                        if j >= 2:
                            v = next(x for x in units if x["kp0"] <= j - 2 < x["kp0"] + x["kp"])
                            kk = j - 2 - v["kp0"]
                            pe.wait_ge(*na("ptA" if kk % 2 == 0 else "ptD", L,
                                           v["act0" if kk % 2 == 0 else "dve0"] + kk // 2 + 1))
                        for q in range(min(2, nt - 2 * kp)):
                            for h in range(2):
                                c = (2 * kp + q) * P
                                last = TR(wk[0][:, 512 * (j % 2) + 256 * q + P * h:512 * (j % 2) + 256 * q + P * h + P],
                                          prob[L][:, i % 2, h, c:c + P], ident)
                        last.then_inc(sem("a_T"), 1)

                def values(i):
                    u = units[i]
                    nt = len(u["tiles"])
                    if i >= 2:
                        pe.wait_ge(*na("oadd", L, i - 1))
                    for kt, tile_ in enumerate(u["tiles"]):
                        kp = kt // 2
                        if kt % 2 == 0:
                            pe.wait_ge(*na("ptA" if kp % 2 == 0 else "ptD", L,
                                           u["act0" if kp % 2 == 0 else "dve0"] + kp // 2 + 1))
                        half = kt % 2
                        last = MM(wk[1][64 * half:64 * half + 64, 512 * (i % 2):512 * (i % 2) + 256],
                                  vtok[L][:, tile_, 64 * u["g"]:64 * u["g"] + 64],
                                  probT[L][:, kp, 256 * half:256 * half + 256], start=kt < 2, stop=kt >= nt - 2,
                                  skip_group_check=True)
                    last.then_inc(sem("a_O"), 1)

                pe.wait_ge(sem("s_idr"), 32)
                scores(0)
                for i in range(len(units)):
                    if i + 1 < len(units):
                        scores(i + 1)
                    transposed(i)
                    values(i)

            def gla():
                for d in range(2):
                    for g2 in range(2):
                        i = 2 * d + g2
                        for a, b in ((0, NX), (NX, T)):
                            last = MM((lin[i] if i < 2 else wk[i - 2])[:, a:b],
                                      gkw[0:32, 256 * d + P * g2:256 * d + P * g2 + P], ex[0:32, 0, a:b],
                                      start=True, stop=True)
                        last.then_inc(sem("g_z"), 1)
                for tt in range(6):
                    if tt < 2:
                        pe.wait_ge(sem("g_zc"), tt + 1)
                    else:
                        pe.wait_ge(sem("g_vcpA" if tt % 2 == 0 else "g_vcpD"), tt // 2)
                    for t in range(4):
                        last = TR(lin[tt % 2][:, P * t:P * t + P], big[:, 4 + t, tt * P:tt * P + P], ident)
                    last.then_inc(sem("g_vT"), 1)
                pe.wait_ge(sem("g_vcpA"), 3)
                pe.wait_ge(sem("g_vcpD"), 3)
                for i in range(4):
                    pe.wait_ge(sem("g_ke"), i + 1)
                    if i >= 2:
                        pe.wait_ge(sem("g_kcpA" if i % 2 == 0 else "g_kcpD"), i // 2)
                    for tt in range(6):
                        last = TR(lin[i % 2][:, P * tt:P * tt + P], gsc[:, 4 + i, tt * P:tt * P + P], ident)
                    last.then_inc(sem("g_kT"), 1)

                def scores(pr):
                    if pr == 0:
                        pe.wait_ge(sem("g_kcpA"), 2)
                        pe.wait_ge(sem("g_kcpD"), 2)
                        pe.wait_ge(sem("g_qe"), 4)
                    if pr >= 1:
                        pe.wait_ge(sem("g_at"), pr)
                    for d in range(2):
                        for h in range(8):
                            i, r = 2 * d + h // 4, h % 4
                            rows = slice(32 * r, 32 * r + 32)
                            for half in range(2):
                                c = pr * P + half * CH
                                col = 512 * r + P * d + CH * (h // 4)
                                last = MM(psum[64 * half:64 * half + 64, col:col + CH],
                                          gsc[rows, 4 + i, c:c + CH], gsc[rows, i, c:c + CH], start=True, stop=True,
                                          tile_position=(32 * r, 64 * half), skip_group_check=True)
                    last.then_inc(sem("g_A"), 1)

                def within(pr):
                    pe.wait_ge(sem("g_at"), pr + 1)
                    if pr >= 2:
                        pe.wait_ge(sem("g_ocp"), pr - 1)
                    for h in range(8):
                        for half in range(2):
                            rows = slice(64 * half, 64 * half + 64)
                            c = 512 * half + CH * (h // 2)
                            a = CH * (2 * (h % 4) + h // 4)
                            last = MM(wk[pr % 2][64 * (h % 2):64 * (h % 2) + 64, c:c + CH],
                                      vgt[rows, pr, 64 * h:64 * h + 64], attnT[rows, pr % 2, a:a + CH],
                                      start=True, stop=True, skip_group_check=True)
                    last.then_inc(sem("g_O"), 1)

                scores(0)
                for pr in range(6):
                    if pr + 1 < 6:
                        scores(pr + 1)
                    within(pr)
                pe.wait_ge(sem("g_ocp"), 6)
                for s in range(NCH):
                    for d in range(2):
                        j = 2 * s + d
                        if s >= 1:
                            c = NSEQ[d][s]
                            pe.wait_ge(sem("g_sr"), 2 * (s - 1) + d + 1)
                            if s >= 2:
                                pe.wait_ge(sem("g_oi"), 2 * (s - 2) + d + 1)
                            for h in range(8):
                                g2, r = h // 4, h % 4
                                rows = slice(32 * r, 32 * r + 32)
                                col = 512 * (r // 2) + CH * g2
                                last = MM((lin[1] if d == 0 else wk[1])[64 * (h % 2):64 * (h % 2) + 64, col:col + CH],
                                          statr[rows, d, g2, :], gsc[rows, 2 * d + g2, c * CH:c * CH + CH],
                                          start=True, stop=True, tile_position=(32 * r, 64 * (h % 2)),
                                          skip_group_check=True)
                            last.then_inc(sem("g_I"), 1)
                        if s == NCH - 1:
                            continue
                        c = NSEQ[d][s]
                        if s >= 1:
                            pe.wait_ge(sem("g_ud"), 4 * (2 * (s - 1) + d + 1))
                        rows = slice(64 * (c % 2), 64 * (c % 2) + 64)
                        for g2 in range(2):
                            last = MM((wk[0] if d == 0 else lin[0])[:, 256 * g2:256 * g2 + 256],
                                      kgt[rows, 2 * d + g2, c // 2, :], vgt[rows, c // 2, 256 * g2:256 * g2 + 256],
                                      start=True, stop=True, skip_group_check=True)
                        last.then_inc(sem("g_U"), 1)
                for t in range(4):
                    pe.wait_ge(sem("g_sq"), t + 1)
                    if t >= 2:
                        pe.wait_ge(sem("g_rs"), t - 1)
                    for a, b in ((0, NX), (NX, T)):
                        last = MM(wk[t % 2][:, a:b], blk, big[:, 4 + t % 2, a:b], start=True, stop=True)
                    last.then_inc(sem("g_ms"), 1)

            for n, b in enumerate(BLOCKS):
                kind, L = b["kind"], b["layer"]
                if n == FIRST[("out", 0)]:
                    ada_mm(2 * NADA - 1)
                    ada_T(2 * NADA - 2)
                    ada_T(2 * NADA - 1)
                    fence(pe, "pe", 1)
                    attention(0)
                    fence(pe, "pe", 2)
                    gla()
                    fence(pe, "pe", 3)
                if n == FIRST[("out", 1)]:
                    fence(pe, "pe", 4)
                    attention(1)
                    fence(pe, "pe", 5)
                if (kind, L) in NORM_FOR and n == FIRST[(kind, L)] and n > 0:
                    mean_square(NORM_FOR[(kind, L)], NORM[NORM_FOR[(kind, L)]]["tok"])
                block_product(n)
                if kind == "proj" and L == 0:
                    ada_mm(ADA_EARLY + n)
                    if n >= 1:
                        ada_T(ADA_EARLY + n - 1)
            mean_square(4, NX)


def _shape_constants():
    import numpy as np
    half, quarter, width = HD // 2, HD // 4, 64
    tok = np.arange(NX)
    inv = (10000.0 ** (-np.arange(0, half, 2, dtype=np.float32) / half)).astype(np.float32)
    ang_r = (tok // width).astype(np.float32)[:, None] * inv[None]
    ang_c = (tok % width).astype(np.float32)[:, None] * inv[None]
    ang = np.concatenate([ang_r, ang_r, ang_c, ang_c], axis=-1).T
    con = np.zeros((P, NCONST), np.float32)
    con[:, CC_COS:CC_COS + NX] = np.tile(np.cos(ang), (2, 1))
    con[:, CC_SIN:CC_SIN + NX] = np.tile(np.sin(ang), (2, 1))
    con[:, CC_ID:CC_ID + P] = np.eye(P)
    con[:, CC_ONES:CC_ONES + P] = 1.0 / D
    con[:, CC_BLK:CC_BLK + P] = np.kron(np.eye(2), np.ones((64, 64))) / 64.0
    r = np.zeros((64, 64), np.float32)
    for j in range(quarter):
        r[quarter + j, j] = -1.0
        r[j, quarter + j] = 1.0
        r[3 * quarter + j, 2 * quarter + j] = -1.0
        r[2 * quarter + j, 3 * quarter + j] = 1.0
    con[:, CC_ROT:CC_ROT + P] = np.kron(np.eye(2), r)
    j, i = np.arange(CH)[:, None], np.arange(CH)[None, :]
    con[:, CC_MF:CC_MF + CH] = np.tile(j <= i, (2, 1))
    con[:, CC_MB:CC_MB + CH] = np.tile(j >= i, (2, 1))
    q, k = np.arange(P)[:, None], np.arange(P)[None, :]
    band = np.zeros((P, 3 * P), np.float32)
    band[:, 0:P] = np.where(k >= q, 0.0, NEG)
    band[:, 2 * P:] = np.where(k <= q, 0.0, NEG)
    return con, band


def kernel(**inputs):
    import numpy as np
    import concourse.bacc as bacc
    from concourse.bass_utils import run_bass_kernel_spmd

    a = {k: np.asarray(v) for k, v in inputs.items()}
    f = np.float32

    x = np.concatenate([a["x"][0], a["ctx"][0]], axis=0)
    x_in = x.T.reshape(KT, P, T).transpose(1, 0, 2).reshape(P, KT * T)

    def cols(v):
        return v.reshape(-1, P).T

    params = np.zeros((P, NPAR), f)
    params[:, PC_C:PC_C + 2 * KT] = np.stack([cols(a["c"][0]), cols(a["c_ctx"])], axis=2).reshape(P, 2 * KT)
    for layer in range(2):
        params[:, PC_ADAB + 48 * layer:PC_ADAB + 48 * layer + 48] = cols(a["ada_b"][layer])
        params[:, PC_N + 2 * KT * layer:PC_N + 2 * KT * layer + KT] = cols(a["norm1_g"][layer])
        params[:, PC_N + 2 * KT * layer + KT:PC_N + 2 * KT * layer + 2 * KT] = cols(a["norm2_g"][layer])
    params[:, PC_FIN:PC_FIN + KT] = cols(a["final_g"])
    params[:, PC_GKB:PC_GKB + 4] = cols(a["gla_gk_b"][0].reshape(-1))
    for col, name in ((PC_GLAG, "gla_norm_g"), (PC_QN, "attn_qnorm_g"), (PC_KN, "attn_knorm_g")):
        params[:, col] = np.tile(a[name][0], 2)
    params[:, PC_SINK:PC_SINK + 16] = a["win_sink"][0][None, :]
    gkw = np.zeros((32, 512), f)
    gkw[0:16, 0:256] = a["gla_gk_w"][0, 0]
    gkw[16:32, 256:512] = a["gla_gk_w"][0, 1]

    ada = a["ada_w"].reshape(2, 2, 4, P, NADA, 512).transpose(0, 4, 1, 3, 2, 5).reshape(4 * NADA, P, 4 * 512)

    def heads_paired(w, n_heads):
        order = np.arange(n_heads).reshape(2, n_heads // 2).T.reshape(-1)
        return w.reshape(w.shape[0], n_heads, HD)[:, order].reshape(w.shape[0], n_heads * HD)

    win = a["mixab_w_in"][0]
    lr = np.zeros((D, P), f)
    lr[:, 0:32] = win[:, 1536:1568]
    proj0 = np.concatenate([win[:, 0:1536], heads_paired(win[:, 1568:2080], 8), lr, win[:, 2080:2336]], axis=1)
    wout0 = a["mixab_w_out"][0]
    out0 = np.concatenate([wout0[0:512], heads_paired(wout0[512:].T, 8).T], axis=0)
    win1 = a["win_w_in"][0]
    proj1 = np.concatenate([win1[:, 1024:1280], heads_paired(win1[:, 0:1024], 16)], axis=1)
    out1 = heads_paired(a["win_w_out"][0].T, 16).T

    weights = np.zeros((NB, P, KT * P), f)
    for n, b in enumerate(BLOCKS):
        kind, layer = b["kind"], b["layer"]
        if kind in ("proj", "out"):
            w = {("proj", 0): proj0, ("out", 0): out0, ("proj", 1): proj1, ("out", 1): out1}[(kind, layer)]
            sub = w[:, b["m"] * P:b["m"] * P + P]
        elif kind in ("w1", "w3"):
            sub = a["ffn_w1" if kind == "w1" else "ffn_w3"][layer][:, b["h"] * P:b["h"] * P + P]
        else:
            h0, nh = GROUPS[b["g"]]
            sub = a["ffn_w2"][layer][h0 * P:(h0 + nh) * P, b["m"] * P:b["m"] * P + P]
        nk = b["nk"]
        weights[n, :, 0:nk * P] = sub.reshape(nk, P, P).transpose(1, 0, 2).reshape(P, nk * P)

    con, band = _shape_constants()
    arrays = {"x_in": x_in, "params": params, "consts": con, "masks": band, "gkw": gkw, "ada": ada,
              "weights": weights}
    nc = bacc.Bacc("TRN2", target_bir_lowering=False, num_devices=1)
    args, feed = [], {}
    for name, arr in arrays.items():
        arr = np.ascontiguousarray(arr, dtype=f)
        feed[name + "_dram"] = arr
        args.append(nc.dram_tensor(name + "_dram", arr.shape, F32, kind="ExternalInput").ap())
    out = nc.dram_tensor("out_dram", (P, KT * NX), F32, kind="ExternalOutput").ap()
    build(nc, *args, out)
    r = run_bass_kernel_spmd(nc, [feed], core_ids=[0])
    got = r.results[0]["out_dram"]
    return got.reshape(P, KT, NX).transpose(2, 1, 0).reshape(1, NX, D)
```

```python
import math
from contextlib import ExitStack

import concourse.bass as bass
from concourse import mybir

F32 = mybir.dt.float32
F32R = mybir.dt.float32r
ALU = mybir.AluOpType
ACT = mybir.ActivationFunctionType
AX = mybir.AxisListType

P = 128
D = 1024
KT = D // P
NX = 512
NC_ = 256
T = NX + NC_
EPS = 1e-6
HD = 64
FFN = 2816
FT = FFN // P
GROUPS = [(0, 8), (8, 7), (15, 7)]
CH = 64
NCH = T // CH
DK = 32
TAU = 16.0
CLAMP = 80.0 * TAU
RING = 3
ADA_RING = 3
NADA = 12
ADA_EARLY = 4

PC_C = 0
PC_ADAB = PC_C + 2 * KT
PC_N = PC_ADAB + 2 * 48
PC_FIN = PC_N + 4 * KT
PC_GKB = PC_FIN + KT
PC_GLAG = PC_GKB + 4
PC_QN = PC_GLAG + 1
PC_KN = PC_QN + 1
PC_SINK = PC_KN + 1
NPAR = PC_SINK + 16

CC_COS = 0
CC_SIN = CC_COS + NX
CC_ID = CC_SIN + NX
CC_ONES = CC_ID + P
CC_BLK = CC_ONES + P
CC_ROT = CC_BLK + P
CC_MF = CC_ROT + P
CC_MB = CC_MF + CH
NCONST = CC_MB + CH

NEG = -1.0e30
LN_EXP = "natural_log_exp_and_others"
NPT = 4
SCALE = HD ** -0.5


def blocks_of_the_stream():
    out = [dict(kind="proj", layer=0, m=m, nk=KT, tok=T) for m in range(19)]
    out += [dict(kind="out", layer=0, m=m, nk=KT, tok=T) for m in range(KT)]

    def ffn(layer, tok):
        for g, (h0, nh) in enumerate(GROUPS):
            for i in range(nh):
                out.append(dict(kind="w1", layer=layer, g=g, i=i, h=h0 + i, nk=KT, tok=tok))
                out.append(dict(kind="w3", layer=layer, g=g, i=i, h=h0 + i, nk=KT, tok=tok))
            for m in range(KT):
                out.append(dict(kind="w2", layer=layer, g=g, m=m, nk=nh, tok=tok))

    ffn(0, T)
    out += [dict(kind="proj", layer=1, m=m, nk=KT, tok=T if m < 2 else NX) for m in range(10)]
    out += [dict(kind="out", layer=1, m=m, nk=KT, tok=NX) for m in range(KT)]
    ffn(1, NX)
    return out


BLOCKS = blocks_of_the_stream()
NB = len(BLOCKS)
FIRST = {}
for _n, _b in enumerate(BLOCKS):
    FIRST.setdefault((_b["kind"], _b["layer"]), _n)


def attention_units(layer):
    units = []
    for head in range(8 if layer == 0 else 16):
        j, g = divmod(head, 2)
        base = dict(head=head, j=j, g=g)
        if layer == 0:
            units.append(dict(base, q0=0, nq=NX, c0=0, n=T, maxima=[[(0, 0, NX, None), (NX, NX, NC_, None)]] * 4,
                              steps=[(kt, 0, NX, None) for kt in range(6)]))
            units.append(dict(base, q0=NX, nq=NC_, c0=0, n=NC_, maxima=[[(0, NX, NC_, None)]] * 2,
                              steps=[(4, 0, NC_, None), (5, 0, NC_, None)]))
        else:
            near = [(max(t - 1, 0), min(t + 1, 3)) for t in range(4)]
            units.append(dict(base, q0=0, nq=NX, c0=256, n=None,
                              maxima=[[(256, NX, NC_, None), (512, lo * P, (hi - lo + 1) * P, (lo - t + 1) * P)]
                                      for t, (lo, hi) in enumerate(near)],
                              steps=[(4, 0, NX, None), (5, 0, NX, None)] +
                                    [(t, lo * P, (hi + 1) * P, (lo - t + 1) * P) for t, (lo, hi) in enumerate(near)]))
    m = t = 0
    for u in units:
        u["m0"], u["t0"] = m, t
        m += len(u["maxima"])
        t += len(u["steps"])
    return units


def build(nc, x_in, params, consts, masks, gkw_in, ada, weights, out):
    ctx = ExitStack()
    with ctx:
        def sb(name, shape, dt=F32):
            return ctx.enter_context(nc.sbuf_tensor(name, shape, dt))

        base = nc.sbuf_base
        top = [0]

        arena = sb("arena", [P, (nc.sbuf_bytes_remaining - 128) // 4])
        origin = (base + 31) // 32 * 32

        def at(name, shape, offset, dt=F32):
            return nc.alloc_sbuf_tensor_at(name, shape, dt, offset=origin + offset)

        def take(nbytes):
            o = top[0]
            top[0] += (nbytes + 31) // 32 * 32
            return o

        TILE = T * 4
        xT = at("xT", [P, KT, T], take(KT * TILE))
        raw = at("raw", [P, RING, KT * P], take(RING * KT * P * 4))
        whi = at("whi", [P, RING, KT * P], take(RING * KT * P * 4), F32R)
        wlo = at("wlo", [P, RING, KT * P], take(RING * KT * P * 4), F32R)
        con = at("con", [P, NCONST], take(NCONST * 4))
        identr = at("identr", [P, P], take(P * 4), F32R)
        bandm = at("bandm", [P, 3 * P], take(3 * P * 4), F32R)
        par = at("par", [P, NPAR], take(NPAR * 4))
        epsc = at("epsc", [P, 8], take(32))
        gkw = at("gkw", [P, 512], take(512 * 4))
        cpad = at("cpad", [P, KT, 32], take(KT * 32 * 4))
        mod = at("mod", [P, 2, 48, 2], take(2 * 96 * 4))
        modA = at("modA", [P, 4, KT, 2], take(4 * 16 * 4))
        O_ADASB = take(2 * 2048)
        adasb = at("adasb", [P, 2, 512], O_ADASB)
        st_mx = at("st_mx", [P, 3, 4], take(48))
        ge = at("ge", [P, 3, 4, NCH], take(3 * 4 * NCH * 4))
        gd = at("gd", [P, 4, NCH], take(4 * NCH * 4))
        H = take(2 * KT * TILE)
        G = take(2 * KT * TILE)
        E = take(11 * TILE)
        assert top[0] + 32 <= arena.shape[1] * 4, (top[0], arena.shape)

        hhA = at("hhA", [P, 4, T], H, F32R)
        hlA = at("hlA", [P, 4, T], H + 4 * TILE, F32R)
        hhB = at("hhB", [P, 4, T], H + 8 * TILE, F32R)
        hlB = at("hlB", [P, 4, T], H + 12 * TILE, F32R)

        def hh(k):
            return (hhA if k < 4 else hhB)[:, k % 4, :]

        def hl(k):
            return (hlA if k < 4 else hlB)[:, k % 4, :]

        gh = at("gh", [P, KT, T], G, F32R)
        gl = at("gl", [P, KT, T], G + KT * TILE, F32R)
        big = at("big", [P, 2 * KT, T], G)
        ex = at("ex", [P, 3, T], E)
        ada_w = at("ada_w", [P, ADA_RING, 4, 512], E + 3 * TILE)
        tmps = at("tmps", [P, 8, T], E + 3 * TILE)

        S = [H, G + 10 * TILE]
        NQ = [2, 3]
        QW = [T, NX]
        kst1 = [at(f"kst1_{L}", [P, 2, T], S[L], F32R) for L in range(2)]
        kst2 = [at(f"kst2_{L}", [P, 2, T], S[L] + 2 * TILE, F32R) for L in range(2)]
        vaug = [at(f"vaug{L}", [P, 6, 2, P], S[L] + 4 * TILE) for L in range(2)]
        qst1 = [at(f"qst1_{L}", [P, NQ[L], QW[L]], E + 3 * TILE, F32R) for L in range(2)]
        qst2 = [at(f"qst2_{L}", [P, NQ[L], QW[L]], E + 5 * TILE, F32R) for L in range(2)]
        probT = at("probT", [P, NPT, NX], E + 7 * TILE)
        osb = at("osb", [P, 2, NX], E + 7 * TILE + NPT * NX * 4)
        rsum = at("rsum", [P, 2, NX], O_ADASB)
        esink = at("esink", [P, 2, NX], E)
        zones = at("zones", [P, 2, P], E + 2 * NX * 4)
        sink8 = at("sink8", [P, 16], E + 2 * NX * 4 + 2 * P * 4)
        ropet = [at("ropet0", [P, 2, T], S[0] + 6 * TILE), at("ropet1", [P, 2, T], E + 9 * TILE)]
        hsq = at("hsq", [P, 2, T], E + 7 * TILE)
        hrs = at("hrs", [P, 2, T], E + 9 * TILE)
        assert top[0] + 32 <= arena.shape[1] * 4, (top[0], arena.shape)

        gsc = at("gsc", [P, 8, T], H)
        dec = at("dec", [P, 4, T], G + 12 * TILE)
        vgt = at("vgt", [P, 6, 512], E + 3 * TILE)
        kgt = at("kgt", [P, 4, 6, P], G + 4 * TILE)
        cmask = at("cmask", [P, 2, T], E + 7 * TILE)
        state = at("state", [P, 2, 2, 2, CH], E + 7 * TILE)
        statr = at("statr", [P, 2, 2, CH], E + 8 * TILE)
        supd = at("supd", [P, 2, 2, 2, CH], E + 9 * TILE)
        attnT = at("attnT", [P, 2, 512], E)
        attnM = at("attnM", [P, 512], E + TILE + 1024)
        og = at("og", [P, 4, T], G)
        gt = at("gt", [P, 4, T], G + 12 * TILE)

        psum = ctx.enter_context(nc.psum_tensor("psum", [P, 4096], F32))
        lin = [psum[:, 1024 * i:1024 * i + 1024] for i in range(2)]
        wk = [psum[:, 1024 * i:1024 * i + 1024] for i in range(2, 4)]

        ident = con[:, CC_ID:CC_ID + P]
        ones = con[:, CC_ONES:CC_ONES + P]
        blk = con[:, CC_BLK:CC_BLK + P]
        rot = con[:, CC_ROT:CC_ROT + P]
        cos = con[:, CC_COS:CC_COS + NX]
        sin = con[:, CC_SIN:CC_SIN + NX]
        mgla = [con[:, CC_MF:CC_MF + CH], con[:, CC_MB:CC_MB + CH]]

        sems = {}

        def sem(name):
            if name not in sems:
                sems[name] = ctx.enter_context(nc.semaphore(name))
            return sems[name]

        names = ["s_par", "s_con", "s_x", "s_adaload0", "s_adaload1", "s_adaload2", "s_adamm", "s_adacp", "s_adaT",
                 "s_adar", "s_mod", "s_modA", "s_cpad0", "s_cpad", "s_idr", "s_hi", "s_lo", "s_acc", "s_ev0", "s_ev1",
                 "s_gh", "s_gl", "s_out", "s_fin", "s_outdma",
                 "s_fence", "s_nln", "a_ln", "g_nln"] + [f"s_raw{i}" for i in range(RING)]
        names += [f"s_{n}" for n in ("sq", "sqadd", "nps", "rs", "nt", "nhh", "nhf", "nhl")]
        names += [f"a_{n}" for n in ("sq", "ms", "rs", "nrm", "rot", "rsin", "rcos", "rope", "khi", "klo", "one", "zone", "vps",
                                     "vtok", "qhi", "qlo", "M", "mx", "smax", "R", "row", "e", "S", "exp", "pv", "osb", "fln",
                                     "ri", "mul", "ohi", "olo")]
        names += [f"g_{n}" for n in ("z", "zc", "abs", "exp", "ln", "dec", "cm", "scan", "ref", "refe", "d", "dc", "e1",
                                     "e2", "qe", "ke", "vT", "vcpA", "vcpD", "kT", "kcpA", "kcpD", "A", "am", "am2", "at", "O",
                                     "ocp", "U", "ud", "uk", "st", "sr", "I", "oi", "sq", "ms", "rs", "on", "of", "hi",
                                     "lo")]
        for n_ in names:
            sem(n_)

        def ev(n):
            return sem(f"s_ev{n % 2}"), n // 2 + 1

        U = [attention_units(0), attention_units(1)]
        NORM = [dict(q=0, a=0, layer=0, sh=0, tok=T), dict(q=1, a=1, layer=0, sh=24, tok=T),
                dict(q=2, a=2, layer=1, sh=0, tok=T), dict(q=3, a=3, layer=1, sh=24, tok=NX),
                dict(q=4, a=None, layer=1, sh=None, tok=NX)]
        NORM_FOR = {("proj", 0): 0, ("w1", 0): 1, ("proj", 1): 2, ("w1", 1): 3}

        def nq(name, q, v):
            per = {"sq": KT, "sqadd": KT - 1, "nps": 1, "rs": 1, "nt": KT, "nhl": KT}
            if name in ("nhh", "nhf"):
                return sem("s_" + name), v + sum(KT * len(parts(NORM[p]["tok"])) for p in range(q))
            return sem("s_" + name), v + per[name] * q

        ONCE = {"smax": 0, "rot": 5, "rsin": 5, "rcos": 5, "rope": 5, "khi": 4, "klo": 2, "one": 2, "vps": 1, "vtok": 2,
                "qhi": 2 * 8, "qlo": 8, "M": U[0][-1]["m0"] + 2, "mx": U[0][-1]["m0"] + 2,
                "S": U[0][-1]["t0"] + 2, "exp": U[0][-1]["t0"] + 2, "pv": U[0][-1]["t0"] + 2}

        def na(name, L, v):
            return sem("a_" + name), v + L * ONCE.get(name, len(U[0]))

        def norm_tmp(q, i):
            return big[:, KT + i, :] if q == 0 else tmps[:, i, :]

        def parts(tok):
            return [(0, 0, NX)] + ([(1, NX, T)] if tok == T else [])

        def qsrc(L, u):
            return big[64 * u["g"]:64 * u["g"] + 64, (12 if L == 0 else 2) + u["j"], 0:QW[L]]

        def ksrc(L):
            return ex[:, 1, :] if L == 0 else big[:, 0, :]

        def vsrc(L):
            return ex[:, 2, :] if L == 0 else big[:, 1, :]

        def prep_tiles(L):
            return [(ksrc(0), PC_KN)] + [(big[:, 12 + t, :], PC_QN) for t in range(4)] if L == 0 else \
                [(ksrc(1), None)] + [(big[:, 2 + t, :], None) for t in range(8)]

        def mix_rows(L, u):
            k = (4 if L == 0 else 0) + u["j"]
            rows, toks = slice(64 * u["g"], 64 * u["g"] + 64), slice(u["q0"], u["q0"] + u["nq"])
            return hh(k)[rows, toks], hl(k)[rows, toks]

        def steps_of(L):
            return [(i, a) for i, u in enumerate(U[L]) for a in range(len(u["steps"]))]

        def heads_before(L, i):
            us = U[L]
            if 0 <= i < len(us) and (i == 0 or us[i]["head"] != us[i - 1]["head"]):
                return us[i]["head"]
            return None

        def last_step_of_head(L, head):
            u = [x for x in U[L] if x["head"] == head][-1]
            return u["t0"] + len(u["steps"])

        NSEQ = [[8, 9, 10, 11] + list(range(8)), [11, 10, 9, 8] + list(range(7, -1, -1))]

        def fence(eng, which, k):
            eng.drain().then_inc(sem("s_fence"), 1)
            eng.wait_ge(sem("s_fence"), 3 * k)

        block = ctx.enter_context(nc.Block())

        @block.sync
        def _(sp):
            def load_raw(n):
                if n >= RING:
                    sp.wait_ge(sem("s_lo"), n - RING + 1)
                sp.dma_start(raw[:, n % RING, :], weights[n, :, :]).then_inc(sem(f"s_raw{n % RING}"), 16)

            def load_ada(h):
                if h >= ADA_RING:
                    sp.wait_ge(sem("s_adamm"), h - ADA_RING + 1)
                sp.dma_start(ada_w[:, h % ADA_RING, :, :], ada[h, :, :].rearrange("p (k n) -> p k n", k=4)) \
                    .then_inc(sem(f"s_adaload{h % ADA_RING}"), 16)

            sp.dma_start(par[:, :], params).then_inc(sem("s_par"), 16)
            sp.dma_start(con[:, :], consts).then_inc(sem("s_con"), 16)
            for h in range(ADA_RING):
                load_ada(h)
            sp.dma_start(xT[:, :, :], x_in.rearrange("p (k t) -> p k t", k=KT)).then_inc(sem("s_x"), 16)
            sp.dma_start(gkw[0:32, :], gkw_in).then_inc(sem("s_con"), 16)
            for n in range(RING):
                load_raw(n)
            for h in range(ADA_RING, 2 * ADA_EARLY):
                load_ada(h)
            h = 2 * ADA_EARLY
            for n in range(RING, NB):
                load_raw(n)
                for _ in range(2):
                    if h < 4 * NADA:
                        load_ada(h)
                        h += 1
            for k in range(KT):
                sp.wait_ge(sem("s_fin"), k + 1)
                sp.dma_start(out[:, k * NX:(k + 1) * NX], big[:, k, 0:NX]).then_inc(sem("s_outdma"), 16)
            sp.wait_ge(sem("s_outdma"), 16 * KT)

        @block.gpsimd
        def _(pool):
            pool.dma_start(bandm[:, :], masks).then_inc(sem("s_idr"), 16)
            pool.dma_start(identr[:, :], consts[:, CC_ID:CC_ID + P]).then_inc(sem("s_idr"), 16)
            for n in range(NB):
                s = n % RING
                w = BLOCKS[n]["nk"] * P
                pool.wait_ge(sem("s_hi"), n + 1)
                if n >= RING:
                    pool.wait_ge(sem("s_acc"), n - RING + 1)
                nc.gpsimd.tensor_tensor(wlo[:, s, 0:w], raw[:, s, 0:w], whi[:, s, 0:w].bitcast(F32),
                                        ALU.subtract).then_inc(sem("s_lo"), 1)

        @block.scalar
        def _(act):
            A = nc.scalar.activation

            def high(n):
                if n >= NB:
                    return
                s = n % RING
                w = BLOCKS[n]["nk"] * P
                act.wait_ge(sem(f"s_raw{s}"), 16 * (n // RING + 1))
                if n >= RING:
                    act.wait_ge(sem("s_acc"), n - RING + 1)
                    act.wait_ge(sem("s_lo"), n - RING + 1)
                A(whi[:, s, 0:w], raw[:, s, 0:w], ACT.Copy).then_inc(sem("s_hi"), 1)

            def ada_copy(c):
                act.wait_ge(sem("s_adamm"), 2 * (c + 1))
                if c >= 2:
                    act.wait_ge(sem("s_adaT"), c - 1)
                A(adasb[:, c % 2, :], wk[0][:, 512 * (c % 2):512 * (c % 2) + 512], ACT.Copy) \
                    .then_inc(sem("s_adacp"), 1)

            def square(q, k, tok):
                if k >= 3:
                    act.wait_ge(*nq("sqadd", q, k - 2))
                A(norm_tmp(q, 0 if k == 0 else 1 + k % 2)[:, 0:tok], xT[:, k, 0:tok], ACT.Square) \
                    .then_inc(sem("s_sq"), 1)

            def root(q, tok):
                nc.scalar.preload_act_table_set(LN_EXP)
                act.wait_ge(*nq("nps", q, 1))
                y = norm_tmp(q, 3)[:, 0:tok]
                A(y, wk[0][:, 0:tok], ACT.Ln, bias=epsc[:, 0:1]).then_inc(sem("s_nln"), 1)
                act.wait_ge(sem("s_nln"), q + 1)
                A(y, y, ACT.Exp, scale=-0.5).then_inc(sem("s_rs"), 1)

            def norm_high(nd):
                q, tok = nd["q"], nd["tok"]
                root(q, tok)
                act.wait_ge(sem("s_modA"), 1 if q == 0 else 4)
                for k in range(KT):
                    act.wait_ge(*nq("nt", q, k + 1))
                    for c, a, b in parts(tok):
                        A(hh(k)[:, a:b], norm_tmp(q, 4 + k % 2)[:, a:b], ACT.Identity,
                          scale=modA[:, nd["a"], k, c:c + 1],
                          bias=mod[:, nd["layer"], nd["sh"] + k, c:c + 1]).then_inc(sem("s_nhh"), 1)

            act.wait_ge(sem("s_par"), 16)
            act.wait_ge(sem("s_cpad0"), 1)
            A(cpad[:, :, 0:2], par[:, PC_C:PC_C + 16].rearrange("p (k c) -> p k c", c=2), ACT.Silu) \
                .then_inc(sem("s_cpad"), 1)
            act.wait_ge(sem("s_x"), 16)
            for k in range(KT):
                square(0, k, T)
            high(0)
            high(1)
            for c in range(ADA_EARLY):
                ada_copy(c)
            norm_high(NORM[0])

            def mixer_projection(layer, n, b):
                m = b["m"]
                tok = b["tok"]
                act.wait_ge(sem("s_acc"), n + 1)
                s_, v_ = ev(n)
                ps = lin[n % 2][:, 0:tok]
                if layer == 1:
                    A(big[:, m, 0:tok], ps, ACT.Copy).then_inc(s_, 1)
                elif m < 2:
                    A(big[:, m, :], ps, ACT.Copy, scale=DK ** -0.5).then_inc(s_, 1)
                elif 8 <= m < 12:
                    A(big[:, m, :], ps, ACT.Silu).then_inc(s_, 1)
                elif m < 16:
                    A(big[:, m, :], ps, ACT.Copy).then_inc(s_, 1)
                else:
                    A(ex[:, m - 16, :], ps, ACT.Copy).then_inc(s_, 1)

            def attention(L):
                units = U[L]
                tiles = prep_tiles(L)
                def keys_high():
                    act.wait_ge(*na("rope", L, 1))
                    for g in range(2):
                        for k_ in (kst1, kst2):
                            A(k_[L][0:64, g, :], ksrc(L)[64 * g:64 * g + 64, :], ACT.Copy).then_inc(sem("a_khi"), 1)

                def head_square(j):
                    if j >= 2:
                        act.wait_ge(sem("a_ms"), j - 1)
                    A(hsq[:, j % 2, :], tiles[j][0], ACT.Square).then_inc(sem("a_sq"), 1)

                def head_root(j):
                    act.wait_ge(sem("a_ms"), j + 1)
                    if j >= 2:
                        act.wait_ge(sem("a_nrm"), j - 1)
                    y = hrs[:, j % 2, :]
                    A(y, wk[j % 2][:, 0:T], ACT.Ln, bias=epsc[:, 0:1]).then_inc(sem("a_ln"), 1)
                    act.wait_ge(sem("a_ln"), j + 1)
                    A(y, y, ACT.Exp, scale=-0.5).then_inc(sem("a_rs"), 1)

                nc.scalar.preload_act_table_set(LN_EXP)
                if L == 0:
                    head_square(0)
                    for j in range(len(tiles)):
                        if j + 1 < len(tiles):
                            head_square(j + 1)
                        head_root(j)
                        if j == 1:
                            keys_high()
                else:
                    keys_high()

                def q_high(head):
                    u = next(x for x in units if x["head"] == head)
                    act.wait_ge(*na("rope", L, 1 + u["j"] + 1))
                    if head >= NQ[L]:
                        act.wait_ge(*na("S", L, last_step_of_head(L, head - NQ[L])))
                    for half in range(2):
                        A(qst1[L][64 * half:64 * half + 64, head % NQ[L], :], qsrc(L, u), ACT.Copy) \
                            .then_inc(sem("a_qhi"), 1)

                def row(i):
                    u = units[i]
                    act.wait_ge(*na("R", L, i + 1))
                    if u["head"] >= NQ[L]:
                        act.wait_ge(*na("S", L, last_step_of_head(L, u["head"] - NQ[L])))
                    r_ = qst2[L][64:65, u["head"] % NQ[L], u["q0"]:u["q0"] + u["nq"]]
                    A(r_, wk[1][64:65, 512:512 + u["nq"]], ACT.Copy, scale=-1.0).then_inc(sem("a_row"), 1)
                    if L == 1:
                        act.wait_ge(*na("row", L, i + 1))
                        if i >= 2:
                            act.wait_ge(*na("pv", L, units[i - 2]["t0"] + 6))
                        s_ = PC_SINK + 8 * u["g"] + u["j"]
                        A(esink[64:65, i % 2, :], r_.bitcast(F32), ACT.Exp, scale=SCALE, bias=par[64:65, s_:s_ + 1]) \
                            .then_inc(sem("a_e"), 1)

                def exponential(i, a):
                    u = units[i]
                    t = u["t0"] + a
                    _, qa, qb, _ = u["steps"][a]
                    act.wait_ge(*na("S", L, t + 1))
                    if t >= NPT:
                        act.wait_ge(*na("pv", L, t - NPT + 1))
                    A(probT[:, t % NPT, qa:qb], wk[0][:, 512 * (t % 2) + qa:512 * (t % 2) + qb], ACT.Exp,
                      scale=SCALE).then_inc(sem("a_exp"), 1)

                def inverse(i):
                    u = units[i]
                    g = u["g"]
                    act.wait_ge(*na("osb", L, i + 1))
                    if i >= 2:
                        act.wait_ge(*na("mul", L, i - 1))
                    y = rsum[64 * g:64 * g + 64, i % 2, 0:u["nq"]]
                    A(y, osb[64 - 64 * g:128 - 64 * g, i % 2, 0:u["nq"]], ACT.Ln).then_inc(sem("a_fln"), 1)
                    act.wait_ge(*na("fln", L, i + 1))
                    A(y, y, ACT.Exp, scale=-1.0).then_inc(sem("a_ri"), 1)

                def out_high(i):
                    u = units[i]
                    act.wait_ge(*na("mul", L, i + 1))
                    A(mix_rows(L, u)[0], osb[64 * u["g"]:64 * u["g"] + 64, i % 2, 0:u["nq"]], ACT.Copy) \
                        .then_inc(sem("a_ohi"), 1)

                for i in range(2):
                    head = heads_before(L, i)
                    if head is not None:
                        q_high(head)
                row(0)
                for i, u in enumerate(units):
                    for a in range(len(u["steps"])):
                        exponential(i, a)
                        short = len(u["steps"]) < 4
                        if a == 0 and i + 1 < len(units):
                            row(i + 1)
                        head = heads_before(L, i + 2)
                        if a == 1 and head is not None:
                            q_high(head)
                        if a == (1 if short else 2) and i >= 1:
                            inverse(i - 1)
                        if a == (1 if short else 4) and i >= 1:
                            out_high(i - 1)
                inverse(len(units) - 1)
                out_high(len(units) - 1)

            def gla():
                for i in range(4):
                    act.wait_ge(sem("g_z"), i + 1)
                    z = (lin[i] if i < 2 else wk[i - 2])[:, 0:T]
                    A(gsc[:, i, :], z, ACT.Abs, bias=par[:, PC_GKB + i:PC_GKB + i + 1]).then_inc(sem("g_abs"), 1)
                    A(dec[:, i, :], z, ACT.Identity, bias=par[:, PC_GKB + i:PC_GKB + i + 1]) \
                        .then_inc(sem("g_zc"), 1)
                for i in range(4):
                    act.wait_ge(sem("g_abs"), i + 1)
                    A(gsc[:, i, :], gsc[:, i, :], ACT.Exp, scale=-1.0).then_inc(sem("g_exp"), 1)
                for tt in range(0, 6, 2):
                    act.wait_ge(sem("g_vT"), tt + 1)
                    A(vgt[:, tt, :], lin[0][:, 0:512], ACT.Copy).then_inc(sem("g_vcpA"), 1)
                for i in range(4):
                    act.wait_ge(sem("g_exp"), i + 1)
                    A(gsc[:, 4 + i, :], gsc[:, i, :], ACT.Ln, bias=epsc[:, 1:2]).then_inc(sem("g_ln"), 1)
                act.wait_ge(sem("g_ref"), 8)
                A(ge[:, 0, :, :], gd[:, :, :], ACT.Exp, scale=1.0 / TAU).then_inc(sem("g_refe"), 1)
                act.wait_ge(sem("g_ref"), 12)
                A(ge[:, 1, :, :], ge[:, 1, :, :], ACT.Exp, scale=1.0 / TAU).then_inc(sem("g_refe"), 1)
                A(ge[:, 2, :, :], ge[:, 2, :, :], ACT.Exp, scale=1.0 / TAU).then_inc(sem("g_refe"), 1)
                for i in range(4):
                    act.wait_ge(sem("g_dc"), i + 1)
                    A(gsc[:, i, :], dec[:, i, :], ACT.Exp, scale=1.0 / TAU).then_inc(sem("g_e1"), 1)
                    A(gsc[:, 4 + i, :], dec[:, i, :], ACT.Exp, scale=-1.0 / TAU).then_inc(sem("g_e2"), 1)
                for i in range(0, 4, 2):
                    act.wait_ge(sem("g_kT"), i + 1)
                    A(kgt[:, i, :, :], lin[0][:, 0:T].rearrange("p (t d) -> p t d", d=P), ACT.Copy) \
                        .then_inc(sem("g_kcpA"), 1)
                for pr in range(6):
                    act.wait_ge(sem("g_O"), pr + 1)
                    src = wk[pr % 2].rearrange("p (half x) -> p half x", half=2)
                    src = src[:, :, 0:256].rearrange("p half (h t) -> p h half t", h=4)
                    A(og[:, :, pr * P:pr * P + P].rearrange("p h (half t) -> p h half t", half=2), src, ACT.Copy) \
                        .then_inc(sem("g_ocp"), 1)
                nc.scalar.preload_act_table_set(LN_EXP)
                act.wait_ge(sem("g_oi"), 2 * (NCH - 1))
                for t in range(6):
                    if t < 4:
                        if t >= 2:
                            act.wait_ge(sem("g_ms"), t - 1)
                        A(big[:, 4 + t % 2, :], og[:, t, :], ACT.Square).then_inc(sem("g_sq"), 1)
                    if 1 <= t < 5:
                        act.wait_ge(sem("g_ms"), t)
                        if t >= 3:
                            act.wait_ge(sem("g_on"), t - 2)
                        y = big[:, 6 + (t - 1) % 2, :]
                        A(y, wk[(t - 1) % 2][:, 0:T], ACT.Ln, bias=epsc[:, 0:1]).then_inc(sem("g_nln"), 1)
                        act.wait_ge(sem("g_nln"), t)
                        A(y, y, ACT.Exp, scale=-0.5).then_inc(sem("g_rs"), 1)
                    if t >= 2:
                        act.wait_ge(sem("g_of"), t - 1)
                        A(hhA[:, t - 2, :], gt[:, t - 2, :], ACT.Copy).then_inc(sem("g_hi"), 1)

            for n, b in enumerate(BLOCKS):
                kind, L = b["kind"], b["layer"]
                if n == FIRST[("out", 0)]:
                    fence(act, "act", 1)
                    attention(0)
                    fence(act, "act", 2)
                    gla()
                    fence(act, "act", 3)
                if n == FIRST[("out", 1)]:
                    fence(act, "act", 4)
                    attention(1)
                    fence(act, "act", 5)
                if (kind, L) in NORM_FOR and n == FIRST[(kind, L)] and n > 0:
                    norm_high(NORM[NORM_FOR[(kind, L)]])
                high(n + 2)
                if kind == "proj":
                    mixer_projection(L, n, b)
                    if L == 0:
                        ada_copy(ADA_EARLY + n)
                        if n == 18:
                            ada_copy(2 * NADA - 1)
                elif kind == "w1":
                    i = (n - FIRST[("w1", L)])
                    act.wait_ge(sem("s_acc"), n + 1)
                    j = b["h"] + FT * L
                    if j >= 2:
                        act.wait_ge(sem("s_gl"), j - 1)
                    A(tmps[:, 4 + b["h"] % 2, 0:b["tok"]], lin[n % 2][:, 0:b["tok"]], ACT.Silu).then_inc(ev(n)[0], 1)
                elif kind == "w3":
                    act.wait_ge(*ev(n))
                    A(gh[:, b["i"], 0:b["tok"]], tmps[:, 6 + b["h"] % 2, 0:b["tok"]], ACT.Copy) \
                        .then_inc(sem("s_gh"), 1)
                elif kind == "out" or (kind == "w2" and b["g"] == len(GROUPS) - 1):
                    q = {("out", 0): 1, ("w2", 0): 2, ("out", 1): 3, ("w2", 1): 4}[(kind, L)]
                    act.wait_ge(*ev(n))
                    square(q, b["m"], NORM[q]["tok"])
            root(4, NX)

        @block.vector
        def _(dve):
            V = nc.vector
            TT, TS, STT = V.tensor_tensor, V.tensor_scalar, V.scalar_tensor_tensor

            V.memset(epsc[:, 0:1], EPS)
            V.memset(epsc[:, 1:2], 1.0)
            V.memset(cpad[:, :, :], 0.0).then_inc(sem("s_cpad0"), 1)

            def ada_reduce(c):
                layer, cc = divmod(c, NADA)
                dve.wait_ge(sem("s_adaT"), c + 1)
                dst = mod[:, layer, 4 * cc:4 * cc + 4, :]
                src = wk[1][:, 512 * (c % 2):512 * (c % 2) + 512].rearrange("p (q g r) -> p q r g", g=4, r=32)
                V.tensor_reduce(dst, src[:, :, 0:2, :], AX.X, ALU.add).then_inc(sem("s_adar"), 1)
                dve.wait_ge(sem("s_adar"), c + 1)
                bias = par[:, PC_ADAB + 48 * layer + 4 * cc:PC_ADAB + 48 * layer + 4 * cc + 4]
                TT(dst, dst, bias.unsqueeze(2).to_broadcast([P, 4, 2]), ALU.add).then_inc(sem("s_mod"), 1)

            def mod_scale(a):
                layer, second = divmod(a, 2)
                c0 = 32 if second else 8
                gain = par[:, PC_N + KT * a:PC_N + KT * a + KT].unsqueeze(2).to_broadcast([P, KT, 2])
                STT(out=modA[:, a, :, :], in0=mod[:, layer, c0:c0 + KT, :], scalar=1.0, in1=gain, op0=ALU.add,
                    op1=ALU.mult).then_inc(sem("s_modA"), 1)

            def add_square(q, k, tok):
                if k == 0:
                    return
                dve.wait_ge(*nq("sq", q, k + 1))
                if k > 1:
                    dve.wait_ge(*nq("sqadd", q, k - 1))
                acc = norm_tmp(q, 0)[:, 0:tok]
                TT(acc, acc, norm_tmp(q, 1 + k % 2)[:, 0:tok], ALU.add).then_inc(sem("s_sqadd"), 1)

            def rstd(q, tok):
                dve.wait_ge(*nq("rs", q, 1))

            def norm_apply(nd):
                q, tok = nd["q"], nd["tok"]
                rstd(q, tok)
                dve.wait_ge(sem("s_modA"), 1 if q == 0 else 4)

                def scaled(k):
                    if k >= 2:
                        dve.wait_ge(*nq("nhh", q, len(parts(tok)) * (k - 1)))
                    TT(norm_tmp(q, 4 + k % 2)[:, 0:tok], xT[:, k, 0:tok], norm_tmp(q, 3)[:, 0:tok], ALU.mult) \
                        .then_inc(sem("s_nt"), 1)

                scaled(0)
                for k in range(KT):
                    if k + 1 < KT:
                        scaled(k + 1)
                    dve.wait_ge(*nq("nt", q, k + 1))
                    if k >= 2:
                        dve.wait_ge(*nq("nhl", q, k - 1))
                    for c, a, b in parts(tok):
                        TS(norm_tmp(q, 6 + k % 2)[:, a:b], norm_tmp(q, 4 + k % 2)[:, a:b],
                           modA[:, nd["a"], k, c:c + 1], mod[:, nd["layer"], nd["sh"] + k, c:c + 1],
                           ALU.mult, ALU.add).then_inc(sem("s_nhf"), 1)
                    dve.wait_ge(*nq("nhf", q, len(parts(tok)) * (k + 1)))
                    dve.wait_ge(*nq("nhh", q, len(parts(tok)) * (k + 1)))
                    TT(hl(k)[:, 0:tok], norm_tmp(q, 6 + k % 2)[:, 0:tok], hh(k)[:, 0:tok].bitcast(F32),
                       ALU.subtract).then_inc(sem("s_nhl"), 1)

            dve.wait_ge(sem("s_par"), 16)
            for k in range(KT):
                if k == 1:
                    dve.wait_ge(*nq("sq", 0, 1))
                add_square(0, k, T)
            for c in range(ADA_EARLY):
                ada_reduce(c)
            dve.wait_ge(sem("s_mod"), ADA_EARLY)
            mod_scale(0)
            norm_apply(NORM[0])

            def attention(L):
                units = U[L]
                tiles = prep_tiles(L)

                def normed(j):
                    t, g = tiles[j]
                    dve.wait_ge(sem("a_rs"), j + 1)
                    STT(out=t, in0=t, scalar=par[:, g:g + 1], in1=hrs[:, j % 2, :], op0=ALU.mult,
                        op1=ALU.mult).then_inc(sem("a_nrm"), 1)

                def roped(j):
                    t = tiles[j][0][:, 0:NX]
                    dve.wait_ge(*na("rot", L, j + 1))
                    rs_ = ropet[L][:, j % 2, 0:NX]
                    TT(rs_, lin[j % 2][:, 0:NX], sin, ALU.mult).then_inc(sem("a_rsin"), 1)
                    TT(t, t, cos, ALU.mult).then_inc(sem("a_rcos"), 1)
                    dve.wait_ge(*na("rsin", L, j + 1))
                    dve.wait_ge(*na("rcos", L, j + 1))
                    TT(t, t, rs_, ALU.add).then_inc(sem("a_rope"), 1)

                def keys_low():
                    dve.wait_ge(*na("khi", L, 4))
                    k_ = ksrc(L)
                    for g in range(2):
                        TT(kst1[L][64:128, g, :], k_[64 * g:64 * g + 64, :], kst1[L][0:64, g, :].bitcast(F32),
                           ALU.subtract).then_inc(sem("a_klo"), 1)
                        V.tensor_copy(kst2[L][64:65, g, :], epsc[64:65, 1:2].to_broadcast([1, T])) \
                            .then_inc(sem("a_one"), 1)

                dve.wait_ge(sem("s_con"), 32)
                if L == 0:
                    normed(0)
                for j in range(len(tiles)):
                    if L == 0 and j + 1 < len(tiles):
                        normed(j + 1)
                    roped(j)
                    if j == 0:
                        keys_low()
                        dve.wait_ge(*na("vps", L, 1))
                        if L == 1:
                            V.memset(zones[:, 0, 0:64], 0.0)
                            V.memset(zones[:, 0, 64:128], 1.0)
                            V.memset(zones[:, 1, 0:64], 1.0)
                            V.memset(zones[:, 1, 64:128], 0.0).then_inc(sem("a_zone"), 1)
                            TS(sink8[:, :], par[:, PC_SINK:PC_SINK + 16], 1.0 / SCALE, None, ALU.mult) \
                                .then_inc(sem("a_zone"), 1)
                        vT = lin[1][:, 0:T].rearrange("p (t d) -> p t d", d=P)
                        V.memset(vaug[L][:, :, 0, 64:128], 1.0)
                        V.memset(vaug[L][:, :, 1, 0:64], 1.0)
                        for g in range(2):
                            V.tensor_copy(vaug[L][:, :, g, 64 * g:64 * g + 64], vT[:, :, 64 * g:64 * g + 64]) \
                                .then_inc(sem("a_vtok"), 1)

                def q_low(head):
                    u = next(x for x in units if x["head"] == head)
                    dve.wait_ge(*na("qhi", L, 2 * (head + 1)))
                    g = u["g"]
                    TT(qst2[L][0:64, head % NQ[L], :], qsrc(L, u),
                       qst1[L][64 * g:64 * g + 64, head % NQ[L], :].bitcast(F32), ALU.subtract) \
                        .then_inc(sem("a_qlo"), 1)

                def maxima(i, q):
                    u = units[i]
                    m = u["m0"] + q
                    n = u["n"] or sum(x[2] for x in u["maxima"][q])
                    dve.wait_ge(*na("M", L, m + 1))
                    if i >= 3:
                        dve.wait_ge(*na("R", L, i - 2))
                    V.reduce_max(st_mx[:, i % 3, q:q + 1], lin[m % 2][:, u["c0"]:u["c0"] + n], AX.X) \
                        .then_inc(sem("a_mx"), 1)

                def sink_maxima(i):
                    u = units[i]
                    s_ = 8 * u["g"] + u["j"]
                    dve.wait_ge(*na("mx", L, u["m0"] + 4))
                    TS(st_mx[:, i % 3, :], st_mx[:, i % 3, :], sink8[:, s_:s_ + 1], None, ALU.max) \
                        .then_inc(sem("a_smax"), 1)

                def evacuate(i):
                    u = units[i]
                    dve.wait_ge(*na("pv", L, u["t0"] + len(u["steps"])))
                    if i >= 2:
                        dve.wait_ge(*na("ohi", L, i - 1))
                        dve.wait_ge(*na("olo", L, i - 1))
                        dve.wait_ge(*na("fln", L, i - 1))
                    V.tensor_copy(osb[:, i % 2, 0:u["nq"]], wk[1][:, 0:u["nq"]]).then_inc(sem("a_osb"), 1)

                def outputs(i):
                    u = units[i]
                    rows = slice(64 * u["g"], 64 * u["g"] + 64)
                    dve.wait_ge(*na("osb", L, i + 1))
                    dve.wait_ge(*na("ri", L, i + 1))
                    TT(osb[rows, i % 2, 0:u["nq"]], osb[rows, i % 2, 0:u["nq"]], rsum[rows, i % 2, 0:u["nq"]],
                       ALU.mult).then_inc(sem("a_mul"), 1)

                def out_low(i):
                    u = units[i]
                    h_, l_ = mix_rows(L, u)
                    dve.wait_ge(*na("ohi", L, i + 1))
                    TT(l_, osb[64 * u["g"]:64 * u["g"] + 64, i % 2, 0:u["nq"]], h_.bitcast(F32), ALU.subtract) \
                        .then_inc(sem("a_olo"), 1)

                def unit_maxima(i):
                    if i < len(units):
                        for q in range(len(units[i]["maxima"])):
                            maxima(i, q)
                        if L == 1:
                            sink_maxima(i)

                if L == 1:
                    dve.wait_ge(sem("a_zone"), 2)
                for i in range(2):
                    head = heads_before(L, i)
                    if head is not None:
                        q_low(head)
                for i in range(2):
                    unit_maxima(i)
                for i, u in enumerate(units):
                    if i >= 1:
                        evacuate(i - 1)
                    head = heads_before(L, i + 2)
                    if head is not None:
                        q_low(head)
                    later = units[i + 2]["maxima"] if i + 2 < len(units) else []
                    for q in range(len(later)):
                        if q == 2 and i >= 1:
                            outputs(i - 1)
                        maxima(i + 2, q)
                    if later and L == 1:
                        sink_maxima(i + 2)
                    if i >= 1:
                        if len(later) <= 2:
                            outputs(i - 1)
                        out_low(i - 1)
                evacuate(len(units) - 1)
                outputs(len(units) - 1)
                out_low(len(units) - 1)

            def gla():
                for d in range(2):
                    V.memset(cmask[:, d, :], 1.0).then_inc(sem("g_cm"), 1)
                dve.wait_ge(sem("g_cm"), 2)
                for d in range(2):
                    V.memset(cmask[:, d, :].rearrange("p (c t) -> p c t", t=CH)[:, :, (CH - 1) * d], 0.0) \
                        .then_inc(sem("g_cm"), 1)
                for tt in range(1, 6, 2):
                    dve.wait_ge(sem("g_vT"), tt + 1)
                    V.tensor_copy(vgt[:, tt, :], lin[1][:, 0:512]).then_inc(sem("g_vcpD"), 1)
                for i in range(4):
                    dve.wait_ge(sem("g_ln"), i + 1)
                    STT(out=dec[:, i, :], in0=dec[:, i, :], scalar=0.0, in1=gsc[:, 4 + i, :], op0=ALU.min,
                        op1=ALU.subtract).then_inc(sem("g_dec"), 1)
                dve.wait_ge(sem("g_cm"), 4)
                for i in range(4):
                    dve.wait_ge(sem("g_dec"), i + 1)
                    if i < 2:
                        V.tensor_tensor_scan(gsc[:, i, :], cmask[:, 0, :], dec[:, i, :], 0.0, ALU.mult, ALU.add) \
                            .then_inc(sem("g_scan"), 1)
                    else:
                        V.tensor_tensor_scan(gsc[:, i, T - 1::-1], cmask[:, 1, T - 1::-1], dec[:, i, T - 1::-1], 0.0,
                                             ALU.mult, ALU.add).then_inc(sem("g_scan"), 1)

                def chunks(i):
                    return gsc[:, i, :].rearrange("p (c t) -> p c t", t=CH)

                dve.wait_ge(sem("g_scan"), 4)
                for i in range(4):
                    V.tensor_copy(gd[:, i, :], chunks(i)[:, :, CH // 2 - 1]).then_inc(sem("g_ref"), 1)
                for i in range(4):
                    last = (CH - 1) if i < 2 else 0
                    V.tensor_copy(ge[:, 1, i, :], chunks(i)[:, :, last]).then_inc(sem("g_ref"), 1)
                for i in range(4):
                    last = (CH - 1) if i < 2 else 0
                    TT(ge[:, 2, i, :], chunks(i)[:, :, last], chunks(i)[:, :, CH // 2 - 1], ALU.subtract) \
                        .then_inc(sem("g_ref"), 1)
                dve.wait_ge(sem("g_ref"), 4)
                for i in range(4):
                    TT(dec[:, i, :].rearrange("p (c t) -> p c t", t=CH), chunks(i),
                       gd[:, i, :].unsqueeze(2).to_broadcast([P, NCH, CH]), ALU.subtract).then_inc(sem("g_d"), 1)
                for i in range(4):
                    dve.wait_ge(sem("g_d"), i + 1)
                    TS(dec[:, i, :], dec[:, i, :], -CLAMP, CLAMP, ALU.max, ALU.min).then_inc(sem("g_dc"), 1)
                for i in range(4):
                    g2 = i % 2
                    dve.wait_ge(sem("g_e1"), i + 1)
                    TT(gsc[:, i, :], gsc[:, i, :], big[:, g2, :], ALU.mult).then_inc(sem("g_qe"), 1)
                    dve.wait_ge(sem("g_e2"), i + 1)
                    TT(gsc[:, 4 + i, :], gsc[:, 4 + i, :], big[:, 2 + g2, :], ALU.mult).then_inc(sem("g_ke"), 1)
                for i in range(1, 4, 2):
                    dve.wait_ge(sem("g_kT"), i + 1)
                    V.tensor_copy(kgt[:, i, :, :], lin[1][:, 0:T].rearrange("p (t d) -> p t d", d=P)) \
                        .then_inc(sem("g_kcpD"), 1)
                for pr in range(6):
                    dve.wait_ge(sem("g_A"), pr + 1)
                    if pr >= 2:
                        dve.wait_ge(sem("g_O"), pr - 1)
                    ps = psum[:, 0:2048].rearrange("p (r x) -> p r x", r=4)
                    ps = [ps[:, :, P * d:P * d + P].rearrange("p r (g t) -> p r g t", g=2) for d in range(2)]
                    bc = [m_.unsqueeze(1).unsqueeze(1).to_broadcast([P, 4, 2, CH]) for m_ in mgla]
                    o_ = attnT[:, pr % 2, :].rearrange("p (r g t) -> p r g t", r=4, g=2)
                    TT(o_, ps[0], bc[0], ALU.mult).then_inc(sem("g_am"), 1)
                    if pr >= 1:
                        dve.wait_ge(sem("g_at"), pr)
                    TT(attnM[:, :].rearrange("p (r g t) -> p r g t", r=4, g=2), ps[1], bc[1], ALU.mult) \
                        .then_inc(sem("g_am2"), 1)
                    dve.wait_ge(sem("g_am"), pr + 1)
                    dve.wait_ge(sem("g_am2"), pr + 1)
                    TT(attnT[:, pr % 2, :], attnT[:, pr % 2, :], attnM[:, :], ALU.add).then_inc(sem("g_at"), 1)
                dve.wait_ge(sem("g_refe"), 3)
                dve.wait_ge(sem("g_ocp"), 6)
                nst = 0
                for s in range(NCH):
                    for d in range(2):
                        c = NSEQ[d][s]
                        j = 2 * s + d
                        if s >= 1:
                            dve.wait_ge(sem("g_I"), 2 * (s - 1) + d + 1)
                            o_ = og[:, :, c * CH:c * CH + CH].rearrange("p (g b) t -> p b g t", b=2)
                            if d == 1 or s >= 2:
                                dve.wait_ge(sem("g_oi"), 2 * (s - 1) + d)
                            give = (lin[1] if d == 0 else wk[1]).rearrange("p (b x) -> p b x", b=2)
                            give = give[:, :, 0:2 * CH].rearrange("p b (g t) -> p b g t", g=2)
                            TT(o_, o_, give, ALU.add) \
                                .then_inc(sem("g_oi"), 1)
                        if s == NCH - 1:
                            continue
                        dve.wait_ge(sem("g_U"), j + 1)
                        gi = slice(2 * d, 2 * d + 2)
                        new = state[:, d, (s + 1) % 2, :, :]
                        old = state[:, d, s % 2, :, :]
                        kept, upd = supd[:, d, 0, :, :], supd[:, d, 1, :, :]
                        el = ge[:, 1, gi, c:c + 1].to_broadcast([P, 2, CH])
                        U_ = (wk[0] if d == 0 else lin[0])[:, 0:512]
                        if s >= 2:
                            dve.wait_ge(sem("g_st"), 2 * (s - 2) + d + 1)
                        for r in range(4):
                            rows = slice(32 * r, 32 * r + 32)
                            tgt = upd if s >= 1 else new
                            TT(tgt[rows], U_[rows, :].rearrange("p (g v) -> p g v", g=2)[:, :, 64 * r:64 * r + 64],
                               ge[rows, 2, gi, c:c + 1].to_broadcast([32, 2, CH]), ALU.mult) \
                                .then_inc(sem("g_ud"), 1)
                        if s >= 1:
                            TT(kept, old, el, ALU.mult).then_inc(sem("g_uk"), 1)
                            dve.wait_ge(sem("g_ud"), 4 * (j + 1))
                            dve.wait_ge(sem("g_uk"), 2 * (s - 1) + d + 1)
                            TT(new, kept, upd, ALU.add).then_inc(sem("g_st"), 1)
                            dve.wait_ge(sem("g_st"), 2 * (s - 1) + d + 1)
                        else:
                            dve.wait_ge(sem("g_ud"), 4 * (j + 1))
                        cn = NSEQ[d][s + 1]
                        if s >= 1:
                            dve.wait_ge(sem("g_I"), 2 * (s - 1) + d + 1)
                        TT(statr[:, d, :, :], new, ge[:, 0, gi, cn:cn + 1].to_broadcast([P, 2, CH]), ALU.mult) \
                            .then_inc(sem("g_sr"), 1)
                for t in range(4):
                    dve.wait_ge(sem("g_rs"), t + 1)
                    TT(og[:, t, :], og[:, t, :], big[:, 6 + t % 2, :], ALU.mult).then_inc(sem("g_on"), 1)
                    dve.wait_ge(sem("g_on"), t + 1)
                    STT(out=gt[:, t, :], in0=og[:, t, :], scalar=par[:, PC_GLAG:PC_GLAG + 1], in1=big[:, 8 + t, :],
                        op0=ALU.mult, op1=ALU.mult).then_inc(sem("g_of"), 1)
                    dve.wait_ge(sem("g_hi"), t + 1)
                    TT(hlA[:, t, :], gt[:, t, :], hhA[:, t, :].bitcast(F32), ALU.subtract).then_inc(sem("g_lo"), 1)

            def residual(n, b, gate):
                L, m = b["layer"], b["m"]
                dve.wait_ge(sem("s_acc"), n + 1)
                if n >= 1 and BLOCKS[n - 1]["kind"] == "x":
                    pass
                for c, a, e in parts(b["tok"]):
                    ins = STT(out=xT[:, m, a:e], in0=lin[n % 2][:, a:e], scalar=mod[:, L, gate + m, c:c + 1],
                              in1=xT[:, m, a:e], op0=ALU.mult, op1=ALU.add)
                ins.then_inc(ev(n)[0], 1)

            for n, b in enumerate(BLOCKS):
                kind, L = b["kind"], b["layer"]
                if n == FIRST[("out", 0)]:
                    ada_reduce(2 * NADA - 1)
                    dve.wait_ge(sem("s_mod"), 2 * NADA)
                    for a in range(1, 4):
                        mod_scale(a)
                    fence(dve, "dve", 1)
                    attention(0)
                    fence(dve, "dve", 2)
                    gla()
                    fence(dve, "dve", 3)
                if n == FIRST[("out", 1)]:
                    fence(dve, "dve", 4)
                    attention(1)
                    fence(dve, "dve", 5)
                if (kind, L) in NORM_FOR and n == FIRST[(kind, L)] and n > 0:
                    add_square(NORM_FOR[(kind, L)], KT - 1, NORM[NORM_FOR[(kind, L)]]["tok"])
                    norm_apply(NORM[NORM_FOR[(kind, L)]])
                if kind == "proj" and L == 0:
                    ada_reduce(ADA_EARLY + n)
                elif kind == "w3":
                    j = b["h"] + FT * L
                    dve.wait_ge(sem("s_acc"), n + 1)
                    dve.wait_ge(*ev(n - 1))
                    TT(tmps[:, 6 + b["h"] % 2, 0:b["tok"]], tmps[:, 4 + b["h"] % 2, 0:b["tok"]],
                       lin[n % 2][:, 0:b["tok"]], ALU.mult).then_inc(ev(n)[0], 1)
                    dve.wait_ge(*ev(n))
                    dve.wait_ge(sem("s_gh"), j + 1)
                    TT(gl[:, b["i"], 0:b["tok"]], tmps[:, 6 + b["h"] % 2, 0:b["tok"]],
                       gh[:, b["i"], 0:b["tok"]].bitcast(F32), ALU.subtract).then_inc(sem("s_gl"), 1)
                elif kind in ("out", "w2"):
                    if kind == "w2" or n == FIRST[(kind, L)]:
                        pass
                    if kind == "w2" and b["g"] > 0:
                        dve.wait_ge(*ev(n - (BLOCKS[n]["nk"] * 2 + KT)))
                    residual(n, b, 16 if kind == "out" else 40)
                    if (kind == "out" or b["g"] == len(GROUPS) - 1) and b["m"] >= 1:
                        q = {("out", 0): 1, ("w2", 0): 2, ("out", 1): 3, ("w2", 1): 4}[(kind, L)]
                        add_square(q, b["m"] - 1, NORM[q]["tok"])
            add_square(4, KT - 1, NX)
            dve.wait_ge(*nq("nhl", 3, KT))
            rstd(4, NX)
            for k in range(KT):
                STT(out=big[:, k, 0:NX], in0=xT[:, k, 0:NX], scalar=par[:, PC_FIN + k:PC_FIN + k + 1],
                    in1=norm_tmp(4, 3)[:, 0:NX], op0=ALU.mult, op1=ALU.mult).then_inc(sem("s_fin"), 1)

        @block.tensor
        def _(pe):
            MM, TR = nc.tensor.matmul, nc.tensor.transpose

            def ada_mm(c):
                if c >= 2:
                    pe.wait_ge(sem("s_adacp"), c - 1)
                for half in range(2):
                    h = 2 * c + half
                    pe.wait_ge(sem(f"s_adaload{h % ADA_RING}"), 16 * (h // ADA_RING + 1))
                    for g in range(4):
                        last = MM(wk[0][32 * g:32 * g + 32, 512 * (c % 2):512 * (c % 2) + 512],
                                  cpad[:, 4 * half + g, :], ada_w[:, h % ADA_RING, g, :], start=half == 0,
                                  stop=half == 1, skip_group_check=True)
                    last.then_inc(sem("s_adamm"), 1)

            def ada_T(c):
                pe.wait_ge(sem("s_adacp"), c + 1)
                if c >= 2:
                    pe.wait_ge(sem("s_mod"), c - 1)
                for q in range(4):
                    last = TR(wk[1][:, 512 * (c % 2) + P * q:512 * (c % 2) + P * q + P],
                              adasb[:, c % 2, q * P:q * P + P], ident)
                last.then_inc(sem("s_adaT"), 1)

            def block_product(n):
                b = BLOCKS[n]
                kind, L, tok = b["kind"], b["layer"], b["tok"]
                s = n % RING
                pe.wait_ge(sem("s_hi"), n + 1)
                pe.wait_ge(sem("s_lo"), n + 1)
                if n >= 2:
                    pe.wait_ge(*ev(n - 2))
                q = NORM_FOR.get((kind, L)) if n == FIRST[(kind, L)] else None
                out_ = lin[n % 2]
                for k in range(b["nk"]):
                    if q is not None:
                        np_ = len(parts(NORM[q]["tok"]))
                        pe.wait_ge(*nq("nhh", q, np_ * (k + 1)))
                        pe.wait_ge(*nq("nhl", q, k + 1))
                    if kind == "w2" and b["m"] == 0:
                        j = GROUPS[b["g"]][0] + FT * L + k + 1
                        pe.wait_ge(sem("s_gh"), j)
                        pe.wait_ge(sem("s_gl"), j)
                    hi_, lo_ = (gh[:, k, :], gl[:, k, :]) if kind == "w2" else (hh(k), hl(k))
                    wh_, wl_ = whi[:, s, k * P:k * P + P], wlo[:, s, k * P:k * P + P]
                    first, end = k == 0, k == b["nk"] - 1
                    for j, (w_, a_) in enumerate(((wh_, hi_), (wh_, lo_), (wl_, hi_))):
                        for _, t0, t1 in parts(tok):
                            last = MM(out_[:, t0:t1], w_, a_[:, t0:t1], start=first and j == 0, stop=end and j == 2)
                last.then_inc(sem("s_acc"), 1)

            def mean_square(q, tok):
                pe.wait_ge(*nq("sqadd", q, KT - 1))
                for _, a, b in parts(tok):
                    last = MM(wk[0][:, a:b], ones, norm_tmp(q, 0)[:, a:b], start=True, stop=True)
                last.then_inc(sem("s_nps"), 1)

            pe.wait_ge(sem("s_cpad"), 1)
            pe.wait_ge(sem("s_con"), 32)
            for c in range(ADA_EARLY):
                ada_mm(c)
                if c >= 1:
                    ada_T(c - 1)
            ada_T(ADA_EARLY - 1)
            pe.wait_ge(sem("s_adacp"), ADA_EARLY)
            mean_square(0, T)

            def attention(L):
                units = U[L]
                tiles = prep_tiles(L)

                def means(j):
                    pe.wait_ge(sem("a_sq"), j + 1)
                    if j >= 2:
                        pe.wait_ge(sem("a_rs"), j - 1)
                    for a, b in ((0, NX), (NX, T)):
                        last = MM(wk[j % 2][:, a:b], blk, hsq[:, j % 2, a:b], start=True, stop=True)
                    last.then_inc(sem("a_ms"), 1)

                def rotated(j):
                    if L == 0:
                        pe.wait_ge(sem("a_nrm"), j + 1)
                    if j >= 2:
                        pe.wait_ge(*na("rsin", L, j - 1))
                    if j == 1:
                        pe.wait_ge(*na("vtok", L, 2))
                    MM(lin[j % 2][:, 0:NX], rot, tiles[j][0][:, 0:NX], start=True, stop=True) \
                        .then_inc(sem("a_rot"), 1)

                if L == 0:
                    means(0)
                    means(1)
                for tt in range(6):
                    last = TR(lin[1][:, tt * P:tt * P + P], vsrc(L)[:, tt * P:tt * P + P], ident)
                last.then_inc(sem("a_vps"), 1)
                for j in range(len(tiles)):
                    rotated(j)
                    if L == 0 and j + 2 < len(tiles):
                        means(j + 2)

                def maxima(i, q):
                    u = units[i]
                    m = u["m0"] + q
                    if q == 0:
                        pe.wait_ge(*na("qhi", L, 2 * (u["head"] + 1)))
                    if m >= 2:
                        pe.wait_ge(*na("mx", L, m - 1))
                    a = u["q0"] + q * P
                    for col, key, w, mask in u["maxima"][q]:
                        last = MM(lin[m % 2][:, col:col + w], qst1[L][:, u["head"] % NQ[L], a:a + P],
                                  kst1[L][:, u["g"], key:key + w], start=True, stop=mask is None)
                        if mask is not None:
                            last = MM(lin[m % 2][:, col:col + w], identr[:, :], bandm[:, mask:mask + w],
                                      start=False, stop=True)
                    last.then_inc(sem("a_M"), 1)

                def rows(i):
                    u = units[i]
                    nt = len(u["maxima"])
                    pe.wait_ge(*(na("smax", L, i + 1) if L == 1 else na("mx", L, u["m0"] + nt)))
                    if i >= 1:
                        pe.wait_ge(*na("row", L, i))
                    for q in range(nt):
                        last = MM(wk[1][64:65, 512 + P * q:512 + P * q + P], st_mx[:, i % 3, q:q + 1], ident,
                                  start=True, stop=True, tile_position=(0, 64), skip_group_check=True)
                    last.then_inc(sem("a_R"), 1)

                def scores(i, a):
                    u = units[i]
                    t = u["t0"] + a
                    kt, qa, qb, mask = u["steps"][a]
                    hd, g, q0 = u["head"] % NQ[L], u["g"], u["q0"]
                    if a == 0:
                        pe.wait_ge(*na("qlo", L, u["head"] + 1))
                        pe.wait_ge(*na("row", L, i + 1))
                    if t >= 2:
                        pe.wait_ge(*na("exp", L, t - 1))
                    o_ = wk[0][:, 512 * (t % 2) + qa:512 * (t % 2) + qb]
                    MM(o_, kst1[L][:, g, kt * P:kt * P + P], qst1[L][:, hd, q0 + qa:q0 + qb], start=True, stop=False)
                    last = MM(o_, kst2[L][0:65, g, kt * P:kt * P + P], qst2[L][0:65, hd, q0 + qa:q0 + qb],
                              start=False, stop=mask is None)
                    if mask is not None:
                        last = MM(o_, identr[:, :], bandm[:, mask:mask + qb - qa], start=False, stop=True)
                    last.then_inc(sem("a_S"), 1)

                def values(i, a):
                    u = units[i]
                    t = u["t0"] + a
                    kt, qa, qb, _ = u["steps"][a]
                    if a == 0 and i >= 1:
                        pe.wait_ge(*na("osb", L, i))
                    end = a == len(u["steps"]) - 1
                    if L == 1 and end:
                        pe.wait_ge(sem("a_e"), i + 1)
                        MM(wk[1][:, 0:NX], zones[64:65, u["g"], :], esink[64:65, i % 2, :], start=False, stop=False,
                           skip_group_check=True)
                    pe.wait_ge(*na("exp", L, t + 1))
                    MM(wk[1][:, qa:qb], vaug[L][:, kt, u["g"], :], probT[:, t % NPT, qa:qb], start=a == 0, stop=end,
                       skip_group_check=True).then_inc(sem("a_pv"), 1)

                pe.wait_ge(sem("s_idr"), 32)
                pe.wait_ge(*na("klo", L, 2))
                pe.wait_ge(*na("one", L, 2))
                pe.wait_ge(*na("rope", L, len(tiles)))
                for i in range(2):
                    for q in range(len(units[i]["maxima"])):
                        maxima(i, q)
                rows(0)
                order = steps_of(L)
                scores(0, 0)
                for t, (i, a) in enumerate(order):
                    if a == 0 and i + 1 < len(units):
                        rows(i + 1)
                    if t + 1 < len(order):
                        scores(*order[t + 1])
                    if i + 2 < len(units):
                        short = len(units[i]["steps"]) < 4
                        for q in ((a,) if short else ((), (), (0,), (1, 2), (3,), ())[a]):
                            maxima(i + 2, q)
                    values(i, a)

            def gla():
                for d in range(2):
                    for g2 in range(2):
                        i = 2 * d + g2
                        for a, b in ((0, NX), (NX, T)):
                            last = MM((lin[i] if i < 2 else wk[i - 2])[:, a:b],
                                      gkw[0:32, 256 * d + P * g2:256 * d + P * g2 + P], ex[0:32, 0, a:b],
                                      start=True, stop=True)
                        last.then_inc(sem("g_z"), 1)
                for tt in range(6):
                    if tt < 2:
                        pe.wait_ge(sem("g_zc"), tt + 1)
                    else:
                        pe.wait_ge(sem("g_vcpA" if tt % 2 == 0 else "g_vcpD"), tt // 2)
                    for t in range(4):
                        last = TR(lin[tt % 2][:, P * t:P * t + P], big[:, 4 + t, tt * P:tt * P + P], ident)
                    last.then_inc(sem("g_vT"), 1)
                pe.wait_ge(sem("g_vcpA"), 3)
                pe.wait_ge(sem("g_vcpD"), 3)
                for i in range(4):
                    pe.wait_ge(sem("g_ke"), i + 1)
                    if i >= 2:
                        pe.wait_ge(sem("g_kcpA" if i % 2 == 0 else "g_kcpD"), i // 2)
                    for tt in range(6):
                        last = TR(lin[i % 2][:, P * tt:P * tt + P], gsc[:, 4 + i, tt * P:tt * P + P], ident)
                    last.then_inc(sem("g_kT"), 1)

                def scores(pr):
                    if pr == 0:
                        pe.wait_ge(sem("g_kcpA"), 2)
                        pe.wait_ge(sem("g_kcpD"), 2)
                        pe.wait_ge(sem("g_qe"), 4)
                    if pr >= 1:
                        pe.wait_ge(sem("g_at"), pr)
                    for d in range(2):
                        for h in range(8):
                            i, r = 2 * d + h // 4, h % 4
                            rows = slice(32 * r, 32 * r + 32)
                            for half in range(2):
                                c = pr * P + half * CH
                                col = 512 * r + P * d + CH * (h // 4)
                                last = MM(psum[64 * half:64 * half + 64, col:col + CH],
                                          gsc[rows, 4 + i, c:c + CH], gsc[rows, i, c:c + CH], start=True, stop=True,
                                          tile_position=(32 * r, 64 * half), skip_group_check=True)
                    last.then_inc(sem("g_A"), 1)

                def within(pr):
                    pe.wait_ge(sem("g_at"), pr + 1)
                    if pr >= 2:
                        pe.wait_ge(sem("g_ocp"), pr - 1)
                    for h in range(8):
                        for half in range(2):
                            rows = slice(64 * half, 64 * half + 64)
                            c = 512 * half + CH * (h // 2)
                            a = CH * (2 * (h % 4) + h // 4)
                            last = MM(wk[pr % 2][64 * (h % 2):64 * (h % 2) + 64, c:c + CH],
                                      vgt[rows, pr, 64 * h:64 * h + 64], attnT[rows, pr % 2, a:a + CH],
                                      start=True, stop=True, skip_group_check=True)
                    last.then_inc(sem("g_O"), 1)

                scores(0)
                for pr in range(6):
                    if pr + 1 < 6:
                        scores(pr + 1)
                    within(pr)
                pe.wait_ge(sem("g_ocp"), 6)
                for s in range(NCH):
                    for d in range(2):
                        j = 2 * s + d
                        if s >= 1:
                            c = NSEQ[d][s]
                            pe.wait_ge(sem("g_sr"), 2 * (s - 1) + d + 1)
                            if s >= 2:
                                pe.wait_ge(sem("g_oi"), 2 * (s - 2) + d + 1)
                            for h in range(8):
                                g2, r = h // 4, h % 4
                                rows = slice(32 * r, 32 * r + 32)
                                col = 512 * (r // 2) + CH * g2
                                last = MM((lin[1] if d == 0 else wk[1])[64 * (h % 2):64 * (h % 2) + 64, col:col + CH],
                                          statr[rows, d, g2, :], gsc[rows, 2 * d + g2, c * CH:c * CH + CH],
                                          start=True, stop=True, tile_position=(32 * r, 64 * (h % 2)),
                                          skip_group_check=True)
                            last.then_inc(sem("g_I"), 1)
                        if s == NCH - 1:
                            continue
                        c = NSEQ[d][s]
                        if s >= 1:
                            pe.wait_ge(sem("g_ud"), 4 * (2 * (s - 1) + d + 1))
                        rows = slice(64 * (c % 2), 64 * (c % 2) + 64)
                        for g2 in range(2):
                            last = MM((wk[0] if d == 0 else lin[0])[:, 256 * g2:256 * g2 + 256],
                                      kgt[rows, 2 * d + g2, c // 2, :], vgt[rows, c // 2, 256 * g2:256 * g2 + 256],
                                      start=True, stop=True, skip_group_check=True)
                        last.then_inc(sem("g_U"), 1)
                for t in range(4):
                    pe.wait_ge(sem("g_sq"), t + 1)
                    if t >= 2:
                        pe.wait_ge(sem("g_rs"), t - 1)
                    for a, b in ((0, NX), (NX, T)):
                        last = MM(wk[t % 2][:, a:b], blk, big[:, 4 + t % 2, a:b], start=True, stop=True)
                    last.then_inc(sem("g_ms"), 1)

            for n, b in enumerate(BLOCKS):
                kind, L = b["kind"], b["layer"]
                if n == FIRST[("out", 0)]:
                    ada_mm(2 * NADA - 1)
                    ada_T(2 * NADA - 2)
                    ada_T(2 * NADA - 1)
                    fence(pe, "pe", 1)
                    attention(0)
                    fence(pe, "pe", 2)
                    gla()
                    fence(pe, "pe", 3)
                if n == FIRST[("out", 1)]:
                    fence(pe, "pe", 4)
                    attention(1)
                    fence(pe, "pe", 5)
                if (kind, L) in NORM_FOR and n == FIRST[(kind, L)] and n > 0:
                    mean_square(NORM_FOR[(kind, L)], NORM[NORM_FOR[(kind, L)]]["tok"])
                block_product(n)
                if kind == "proj" and L == 0:
                    ada_mm(ADA_EARLY + n)
                    if n >= 1:
                        ada_T(ADA_EARLY + n - 1)
            mean_square(4, NX)


def _shape_constants():
    import numpy as np
    half, quarter, width = HD // 2, HD // 4, 64
    tok = np.arange(NX)
    inv = (10000.0 ** (-np.arange(0, half, 2, dtype=np.float32) / half)).astype(np.float32)
    ang_r = (tok // width).astype(np.float32)[:, None] * inv[None]
    ang_c = (tok % width).astype(np.float32)[:, None] * inv[None]
    ang = np.concatenate([ang_r, ang_r, ang_c, ang_c], axis=-1).T
    con = np.zeros((P, NCONST), np.float32)
    con[:, CC_COS:CC_COS + NX] = np.tile(np.cos(ang), (2, 1))
    con[:, CC_SIN:CC_SIN + NX] = np.tile(np.sin(ang), (2, 1))
    con[:, CC_ID:CC_ID + P] = np.eye(P)
    con[:, CC_ONES:CC_ONES + P] = 1.0 / D
    con[:, CC_BLK:CC_BLK + P] = np.kron(np.eye(2), np.ones((64, 64))) / 64.0
    r = np.zeros((64, 64), np.float32)
    for j in range(quarter):
        r[quarter + j, j] = -1.0
        r[j, quarter + j] = 1.0
        r[3 * quarter + j, 2 * quarter + j] = -1.0
        r[2 * quarter + j, 3 * quarter + j] = 1.0
    con[:, CC_ROT:CC_ROT + P] = np.kron(np.eye(2), r)
    j, i = np.arange(CH)[:, None], np.arange(CH)[None, :]
    con[:, CC_MF:CC_MF + CH] = np.tile(j <= i, (2, 1))
    con[:, CC_MB:CC_MB + CH] = np.tile(j >= i, (2, 1))
    q, k = np.arange(P)[:, None], np.arange(P)[None, :]
    band = np.zeros((P, 3 * P), np.float32)
    band[:, 0:P] = np.where(k >= q, 0.0, NEG)
    band[:, 2 * P:] = np.where(k <= q, 0.0, NEG)
    return con, band


def kernel(**inputs):
    import numpy as np
    import concourse.bacc as bacc
    from concourse.bass_utils import run_bass_kernel_spmd

    a = {k: np.asarray(v) for k, v in inputs.items()}
    f = np.float32

    x = np.concatenate([a["x"][0], a["ctx"][0]], axis=0)
    x_in = x.T.reshape(KT, P, T).transpose(1, 0, 2).reshape(P, KT * T)

    def cols(v):
        return v.reshape(-1, P).T

    params = np.zeros((P, NPAR), f)
    params[:, PC_C:PC_C + 2 * KT] = np.stack([cols(a["c"][0]), cols(a["c_ctx"])], axis=2).reshape(P, 2 * KT)
    for layer in range(2):
        params[:, PC_ADAB + 48 * layer:PC_ADAB + 48 * layer + 48] = cols(a["ada_b"][layer])
        params[:, PC_N + 2 * KT * layer:PC_N + 2 * KT * layer + KT] = cols(a["norm1_g"][layer])
        params[:, PC_N + 2 * KT * layer + KT:PC_N + 2 * KT * layer + 2 * KT] = cols(a["norm2_g"][layer])
    params[:, PC_FIN:PC_FIN + KT] = cols(a["final_g"])
    params[:, PC_GKB:PC_GKB + 4] = cols(a["gla_gk_b"][0].reshape(-1))
    for col, name in ((PC_GLAG, "gla_norm_g"), (PC_QN, "attn_qnorm_g"), (PC_KN, "attn_knorm_g")):
        params[:, col] = np.tile(a[name][0], 2)
    params[:, PC_SINK:PC_SINK + 16] = a["win_sink"][0][None, :]
    gkw = np.zeros((32, 512), f)
    gkw[0:16, 0:256] = a["gla_gk_w"][0, 0]
    gkw[16:32, 256:512] = a["gla_gk_w"][0, 1]

    ada = a["ada_w"].reshape(2, 2, 4, P, NADA, 512).transpose(0, 4, 1, 3, 2, 5).reshape(4 * NADA, P, 4 * 512)

    def heads_paired(w, n_heads):
        order = np.arange(n_heads).reshape(2, n_heads // 2).T.reshape(-1)
        return w.reshape(w.shape[0], n_heads, HD)[:, order].reshape(w.shape[0], n_heads * HD)

    win = a["mixab_w_in"][0]
    lr = np.zeros((D, P), f)
    lr[:, 0:32] = win[:, 1536:1568]
    proj0 = np.concatenate([win[:, 0:1536], heads_paired(win[:, 1568:2080], 8), lr, win[:, 2080:2336]], axis=1)
    wout0 = a["mixab_w_out"][0]
    out0 = np.concatenate([wout0[0:512], heads_paired(wout0[512:].T, 8).T], axis=0)
    win1 = a["win_w_in"][0]
    proj1 = np.concatenate([win1[:, 1024:1280], heads_paired(win1[:, 0:1024], 16)], axis=1)
    out1 = heads_paired(a["win_w_out"][0].T, 16).T

    weights = np.zeros((NB, P, KT * P), f)
    for n, b in enumerate(BLOCKS):
        kind, layer = b["kind"], b["layer"]
        if kind in ("proj", "out"):
            w = {("proj", 0): proj0, ("out", 0): out0, ("proj", 1): proj1, ("out", 1): out1}[(kind, layer)]
            sub = w[:, b["m"] * P:b["m"] * P + P]
        elif kind in ("w1", "w3"):
            sub = a["ffn_w1" if kind == "w1" else "ffn_w3"][layer][:, b["h"] * P:b["h"] * P + P]
        else:
            h0, nh = GROUPS[b["g"]]
            sub = a["ffn_w2"][layer][h0 * P:(h0 + nh) * P, b["m"] * P:b["m"] * P + P]
        nk = b["nk"]
        weights[n, :, 0:nk * P] = sub.reshape(nk, P, P).transpose(1, 0, 2).reshape(P, nk * P)

    con, band = _shape_constants()
    arrays = {"x_in": x_in, "params": params, "consts": con, "masks": band, "gkw": gkw, "ada": ada,
              "weights": weights}
    nc = bacc.Bacc("TRN2", target_bir_lowering=False, num_devices=1)
    args, feed = [], {}
    for name, arr in arrays.items():
        arr = np.ascontiguousarray(arr, dtype=f)
        feed[name + "_dram"] = arr
        args.append(nc.dram_tensor(name + "_dram", arr.shape, F32, kind="ExternalInput").ap())
    out = nc.dram_tensor("out_dram", (P, KT * NX), F32, kind="ExternalOutput").ap()
    build(nc, *args, out)
    r = run_bass_kernel_spmd(nc, [feed], core_ids=[0])
    got = r.results[0]["out_dram"]
    return got.reshape(P, KT, NX).transpose(2, 1, 0).reshape(1, NX, D)
```

```python
import math
from contextlib import ExitStack

import concourse.bass as bass
from concourse import mybir

F32 = mybir.dt.float32
F32R = mybir.dt.float32r
ALU = mybir.AluOpType
ACT = mybir.ActivationFunctionType
AX = mybir.AxisListType

P = 128
D = 1024
KT = D // P
NX = 512
NC_ = 256
T = NX + NC_
EPS = 1e-6
HD = 64
FFN = 2816
FT = FFN // P
GROUPS = [(0, 8), (8, 7), (15, 7)]
CH = 64
NCH = T // CH
DK = 32
TAU = 16.0
CLAMP = 80.0 * TAU
RING = 3
ADA_RING = 3
NADA = 12
ADA_EARLY = 4

PC_C = 0
PC_ADAB = PC_C + 2 * KT
PC_N = PC_ADAB + 2 * 48
PC_FIN = PC_N + 4 * KT
PC_GKB = PC_FIN + KT
PC_GLAG = PC_GKB + 4
PC_QN = PC_GLAG + 1
PC_KN = PC_QN + 1
PC_SINK = PC_KN + 1
NPAR = PC_SINK + 16

CC_COS = 0
CC_SIN = CC_COS + NX
CC_ID = CC_SIN + NX
CC_ONES = CC_ID + P
CC_BLK = CC_ONES + P
CC_ROT = CC_BLK + P
CC_MF = CC_ROT + P
CC_MB = CC_MF + CH
NCONST = CC_MB + CH

NEG = -1.0e30
LN_EXP = "natural_log_exp_and_others"
NPT = 4
SCALE = HD ** -0.5


def blocks_of_the_stream():
    out = [dict(kind="proj", layer=0, m=m, nk=KT, tok=T) for m in range(19)]
    out += [dict(kind="out", layer=0, m=m, nk=KT, tok=T) for m in range(KT)]

    def ffn(layer, tok):
        for g, (h0, nh) in enumerate(GROUPS):
            for i in range(nh):
                out.append(dict(kind="w1", layer=layer, g=g, i=i, h=h0 + i, nk=KT, tok=tok))
                out.append(dict(kind="w3", layer=layer, g=g, i=i, h=h0 + i, nk=KT, tok=tok))
            for m in range(KT):
                out.append(dict(kind="w2", layer=layer, g=g, m=m, nk=nh, tok=tok))

    ffn(0, T)
    out += [dict(kind="proj", layer=1, m=m, nk=KT, tok=T if m < 2 else NX) for m in range(10)]
    out += [dict(kind="out", layer=1, m=m, nk=KT, tok=NX) for m in range(KT)]
    ffn(1, NX)
    return out


BLOCKS = blocks_of_the_stream()
NB = len(BLOCKS)
FIRST = {}
for _n, _b in enumerate(BLOCKS):
    FIRST.setdefault((_b["kind"], _b["layer"]), _n)


def attention_units(layer):
    units = []
    for head in range(8 if layer == 0 else 16):
        j, g = divmod(head, 2)
        base = dict(head=head, j=j, g=g)
        if layer == 0:
            units.append(dict(base, q0=0, nq=NX, c0=0, n=T, maxima=[[(0, 0, NX, None), (NX, NX, NC_, None)]] * 4,
                              steps=[(kt, 0, NX, None) for kt in range(6)]))
            units.append(dict(base, q0=NX, nq=NC_, c0=0, n=NC_, maxima=[[(0, NX, NC_, None)]] * 2,
                              steps=[(4, 0, NC_, None), (5, 0, NC_, None)]))
        else:
            near = [(max(t - 1, 0), min(t + 1, 3)) for t in range(4)]
            units.append(dict(base, q0=0, nq=NX, c0=256, n=None,
                              maxima=[[(256, NX, NC_, None), (512, lo * P, (hi - lo + 1) * P, (lo - t + 1) * P)]
                                      for t, (lo, hi) in enumerate(near)],
                              steps=[(4, 0, NX, None), (5, 0, NX, None)] +
                                    [(t, lo * P, (hi + 1) * P, (lo - t + 1) * P) for t, (lo, hi) in enumerate(near)]))
    m = t = 0
    for u in units:
        u["m0"], u["t0"] = m, t
        m += len(u["maxima"])
        t += len(u["steps"])
    return units


def build(nc, x_in, params, consts, masks, gkw_in, ada, weights, out):
    ctx = ExitStack()
    with ctx:
        def sb(name, shape, dt=F32):
            return ctx.enter_context(nc.sbuf_tensor(name, shape, dt))

        base = nc.sbuf_base
        top = [0]

        arena = sb("arena", [P, (nc.sbuf_bytes_remaining - 128) // 4])
        origin = (base + 31) // 32 * 32

        def at(name, shape, offset, dt=F32):
            return nc.alloc_sbuf_tensor_at(name, shape, dt, offset=origin + offset)

        def take(nbytes):
            o = top[0]
            top[0] += (nbytes + 31) // 32 * 32
            return o

        TILE = T * 4
        xT = at("xT", [P, KT, T], take(KT * TILE))
        raw = at("raw", [P, RING, KT * P], take(RING * KT * P * 4))
        whi = at("whi", [P, RING, KT * P], take(RING * KT * P * 4), F32R)
        wlo = at("wlo", [P, RING, KT * P], take(RING * KT * P * 4), F32R)
        con = at("con", [P, NCONST], take(NCONST * 4))
        identr = at("identr", [P, P], take(P * 4), F32R)
        bandm = at("bandm", [P, 3 * P], take(3 * P * 4), F32R)
        par = at("par", [P, NPAR], take(NPAR * 4))
        epsc = at("epsc", [P, 8], take(32))
        gkw = at("gkw", [P, 512], take(512 * 4))
        cpad = at("cpad", [P, KT, 32], take(KT * 32 * 4))
        mod = at("mod", [P, 2, 48, 2], take(2 * 96 * 4))
        modA = at("modA", [P, 4, KT, 2], take(4 * 16 * 4))
        O_ADASB = take(2 * 2048)
        adasb = at("adasb", [P, 2, 512], O_ADASB)
        st_mx = at("st_mx", [P, 3, 4], take(48))
        ge = at("ge", [P, 3, 4, NCH], take(3 * 4 * NCH * 4))
        gd = at("gd", [P, 4, NCH], take(4 * NCH * 4))
        gpos = at("gpos", [P, 2, 4, NCH], take(2 * 4 * NCH * 4))
        H = take(2 * KT * TILE)
        G = take(2 * KT * TILE)
        E = take(11 * TILE)
        assert top[0] + 32 <= arena.shape[1] * 4, (top[0], arena.shape)

        hhA = at("hhA", [P, 4, T], H, F32R)
        hlA = at("hlA", [P, 4, T], H + 4 * TILE, F32R)
        hhB = at("hhB", [P, 4, T], H + 8 * TILE, F32R)
        hlB = at("hlB", [P, 4, T], H + 12 * TILE, F32R)

        def hh(k):
            return (hhA if k < 4 else hhB)[:, k % 4, :]

        def hl(k):
            return (hlA if k < 4 else hlB)[:, k % 4, :]

        gh = at("gh", [P, KT, T], G, F32R)
        gl = at("gl", [P, KT, T], G + KT * TILE, F32R)
        big = at("big", [P, 2 * KT, T], G)
        ex = at("ex", [P, 3, T], E)
        ada_w = at("ada_w", [P, ADA_RING, 4, 512], E + 3 * TILE)
        tmps = at("tmps", [P, 8, T], E + 3 * TILE)

        S = [H, G + 10 * TILE]
        NQ = [2, 3]
        QW = [T, NX]
        kst1 = [at(f"kst1_{L}", [P, 2, T], S[L], F32R) for L in range(2)]
        kst2 = [at(f"kst2_{L}", [P, 2, T], S[L] + 2 * TILE, F32R) for L in range(2)]
        vaug = [at(f"vaug{L}", [P, 6, 2, P], S[L] + 4 * TILE) for L in range(2)]
        qst1 = [at(f"qst1_{L}", [P, NQ[L], QW[L]], E + 3 * TILE, F32R) for L in range(2)]
        qst2 = [at(f"qst2_{L}", [P, NQ[L], QW[L]], E + 5 * TILE, F32R) for L in range(2)]
        probT = at("probT", [P, NPT, NX], E + 7 * TILE)
        osb = at("osb", [P, 2, NX], E + 7 * TILE + NPT * NX * 4)
        rsum = at("rsum", [P, 2, NX], O_ADASB)
        esink = at("esink", [P, 2, NX], E)
        zones = at("zones", [P, 2, P], E + 2 * NX * 4)
        sink8 = at("sink8", [P, 16], E + 2 * NX * 4 + 2 * P * 4)
        ropet = [at("ropet0", [P, 2, T], S[0] + 6 * TILE), at("ropet1", [P, 2, T], E + 9 * TILE)]
        hsq = at("hsq", [P, 2, T], E + 7 * TILE)
        hrs = at("hrs", [P, 2, T], E + 9 * TILE)
        assert top[0] + 32 <= arena.shape[1] * 4, (top[0], arena.shape)

        gsc = at("gsc", [P, 8, T], H)
        dec = at("dec", [P, 4, T], G + 12 * TILE)
        vgt = at("vgt", [P, 6, 512], E + 3 * TILE)
        kgt = at("kgt", [P, 4, 6, P], G + 4 * TILE)
        cmask = at("cmask", [P, 2, T], E + 7 * TILE)
        states = at("states", [P, 2, 2, CH, NCH], G + 12 * TILE)
        statr = at("statr", [P, 2, NCH, 2, CH], E + 7 * TILE)
        keep = at("keep", [P, 2, CH, NCH], E + 9 * TILE)
        lrs = at("lrs", [P, T], S[0] + 6 * TILE, F32R)
        gks = at("gks", [P, 512], S[0] + 7 * TILE, F32R)
        attnT = at("attnT", [P, 2, 512], E)
        attnM = at("attnM", [P, 512], E + TILE + 1024)
        og = at("og", [P, 4, T], G)
        gt = at("gt", [P, 4, T], G + 12 * TILE)

        psum = ctx.enter_context(nc.psum_tensor("psum", [P, 4096], F32))
        lin = [psum[:, 1024 * i:1024 * i + 1024] for i in range(2)]
        wk = [psum[:, 1024 * i:1024 * i + 1024] for i in range(2, 4)]

        ident = con[:, CC_ID:CC_ID + P]
        ones = con[:, CC_ONES:CC_ONES + P]
        blk = con[:, CC_BLK:CC_BLK + P]
        rot = con[:, CC_ROT:CC_ROT + P]
        cos = con[:, CC_COS:CC_COS + NX]
        sin = con[:, CC_SIN:CC_SIN + NX]
        mgla = [con[:, CC_MF:CC_MF + CH], con[:, CC_MB:CC_MB + CH]]

        sems = {}

        def sem(name):
            if name not in sems:
                sems[name] = ctx.enter_context(nc.semaphore(name))
            return sems[name]

        names = ["s_par", "s_rope", "s_con", "s_x", "s_adaload0", "s_adaload1", "s_adaload2", "s_adamm", "s_adacp", "s_adaT",
                 "s_adar", "s_mod", "s_modA", "s_cpad0", "s_cpad", "s_idr", "s_hi", "s_lo", "s_acc", "s_ev0", "s_ev1",
                 "s_gh", "s_gl", "s_fin", "s_outdma",
                 "s_fence", "s_nln", "a_ln", "g_nln"] + [f"s_raw{i}" for i in range(RING)]
        names += [f"s_{n}" for n in ("sq", "sqadd", "nps", "rs", "nt", "nhh", "nhf", "nhl", "nhp")]
        names += [f"a_{n}" for n in ("sq", "ms", "rs", "nrm", "rot", "rsin", "rcos", "rope", "khi", "klo", "one", "zone", "vps",
                                     "vtok", "qhi", "qlo", "M", "mx", "smax", "R", "row", "e", "S", "exp", "pv", "osb", "fln",
                                     "ri", "mul", "ohi", "olo")]
        names += [f"g_{n}" for n in ("lh", "ll", "z", "zc", "abs", "exp", "ln", "dec", "cm", "scan", "ref", "refe", "d", "dc", "e1",
                                     "e2", "qe", "ke", "vT", "vcpA", "vcpD", "kT", "kcpA", "kcpD", "A", "am", "am2", "at", "O",
                                     "ocp", "U", "ud", "sr", "I", "oi", "pos", "carry", "keep", "sq", "ms", "rs", "on", "of", "hi",
                                     "lo")]
        for n_ in names:
            sem(n_)

        def ev(n):
            return sem(f"s_ev{n % 2}"), n // 2 + 1

        U = [attention_units(0), attention_units(1)]
        NORM = [dict(q=0, a=0, layer=0, sh=0, tok=T), dict(q=1, a=1, layer=0, sh=24, tok=T),
                dict(q=2, a=2, layer=1, sh=0, tok=T), dict(q=3, a=3, layer=1, sh=24, tok=NX),
                dict(q=4, a=None, layer=1, sh=None, tok=NX)]
        NORM_FOR = {("proj", 0): 0, ("w1", 0): 1, ("proj", 1): 2, ("w1", 1): 3}

        def nq(name, q, v):
            per = {"sq": KT, "sqadd": KT - 1, "nps": 1, "rs": 1, "nt": KT, "nhl": KT // 2, "nhp": KT // 2}
            if name in ("nhh", "nhf"):
                tiles_ = KT if name == "nhh" else KT // 2
                return sem("s_" + name), v + sum(tiles_ * len(parts(NORM[p]["tok"])) for p in range(q))
            return sem("s_" + name), v + per[name] * q

        ONCE = {"smax": 0, "rot": 5, "rsin": 5, "rcos": 5, "rope": 5, "khi": 4, "klo": 2, "one": 2, "vps": 1, "vtok": 2,
                "qhi": 2 * 8, "qlo": 8, "M": U[0][-1]["m0"] + 2, "mx": U[0][-1]["m0"] + 2,
                "S": U[0][-1]["t0"] + 2, "exp": U[0][-1]["t0"] + 2, "pv": U[0][-1]["t0"] + 2}

        def na(name, L, v):
            return sem("a_" + name), v + L * ONCE.get(name, len(U[0]))

        def norm_tmp(q, i):
            return big[:, KT + i, :] if q == 0 else tmps[:, i, :]

        def scaled_tmp(q, k):
            return norm_tmp(q, (4, 5, 1, 2)[k % 4])

        def odd_tmp(q, k):
            return norm_tmp(q, (7, 0)[k // 2 % 2])

        def parts(tok):
            return [(0, 0, NX)] + ([(1, NX, T)] if tok == T else [])

        def qsrc(L, u):
            return big[64 * u["g"]:64 * u["g"] + 64, (12 if L == 0 else 2) + u["j"], 0:QW[L]]

        def ksrc(L):
            return ex[:, 1, :] if L == 0 else big[:, 0, :]

        def vsrc(L):
            return ex[:, 2, :] if L == 0 else big[:, 1, :]

        def prep_tiles(L):
            return [(ksrc(0), PC_KN)] + [(big[:, 12 + t, :], PC_QN) for t in range(4)] if L == 0 else \
                [(ksrc(1), None)] + [(big[:, 2 + t, :], None) for t in range(8)]

        def rot_out(L, j):
            return (lin if L == 0 else wk)[0][:, 512 * (j % 2):512 * (j % 2) + NX]

        def vT_out(L):
            return (lin[1] if L == 0 else wk[1])[:, 0:T]

        def ready_tiles(m):
            return [t for t in (m - 1, m) if t >= 0 and (t == m - 1 or m == 9)]

        def mix_rows(L, u):
            k = (4 if L == 0 else 0) + u["j"]
            rows, toks = slice(64 * u["g"], 64 * u["g"] + 64), slice(u["q0"], u["q0"] + u["nq"])
            return hh(k)[rows, toks], hl(k)[rows, toks]

        def steps_of(L):
            return [(i, a) for i, u in enumerate(U[L]) for a in range(len(u["steps"]))]

        def heads_before(L, i):
            us = U[L]
            if 0 <= i < len(us) and (i == 0 or us[i]["head"] != us[i - 1]["head"]):
                return us[i]["head"]
            return None

        def last_step_of_head(L, head):
            u = [x for x in U[L] if x["head"] == head][-1]
            return u["t0"] + len(u["steps"])


        def fence(eng, k):
            eng.drain().then_inc(sem("s_fence"), 1)
            eng.wait_ge(sem("s_fence"), 3 * k)

        block = ctx.enter_context(nc.Block())

        @block.sync
        def _(sp):
            def load_raw(n):
                if n >= RING:
                    sp.wait_ge(sem("s_lo"), n - RING + 1)
                sp.dma_start(raw[:, n % RING, :], weights[n, :, :]).then_inc(sem(f"s_raw{n % RING}"), 16)

            def load_ada(h):
                if h >= ADA_RING:
                    sp.wait_ge(sem("s_adamm"), h - ADA_RING + 1)
                sp.dma_start(ada_w[:, h % ADA_RING, :, :], ada[h, :, :].rearrange("p (k n) -> p k n", k=4)) \
                    .then_inc(sem(f"s_adaload{h % ADA_RING}"), 16)

            sp.dma_start(par[:, :], params).then_inc(sem("s_par"), 16)
            sp.dma_start(con[:, CC_ID:], consts[:, CC_ID:]).then_inc(sem("s_con"), 16)
            for h in range(ADA_RING):
                load_ada(h)
            sp.dma_start(xT[:, :, :], x_in.rearrange("p (k t) -> p k t", k=KT)).then_inc(sem("s_x"), 16)
            for h in range(ADA_RING, 2 * ADA_EARLY):
                load_ada(h)
            for n in range(RING):
                load_raw(n)
            sp.dma_start(con[:, 0:CC_ID], consts[:, 0:CC_ID]).then_inc(sem("s_rope"), 16)
            sp.dma_start(gkw[0:32, :], gkw_in).then_inc(sem("s_rope"), 16)
            h = 2 * ADA_EARLY
            for n in range(RING, NB):
                load_raw(n)
                for _ in range(2):
                    if h < 4 * NADA:
                        load_ada(h)
                        h += 1
            for k in range(KT):
                sp.wait_ge(sem("s_fin"), k + 1)
                sp.dma_start(out[:, k * NX:(k + 1) * NX], big[:, k, 0:NX]).then_inc(sem("s_outdma"), 16)
            sp.wait_ge(sem("s_outdma"), 16 * KT)

        @block.gpsimd
        def _(pool):
            pool.dma_start(bandm[:, :], masks).then_inc(sem("s_idr"), 16)
            pool.dma_start(identr[:, :], consts[:, CC_ID:CC_ID + P]).then_inc(sem("s_idr"), 16)
            def norm_low(nd):
                q, tok = nd["q"], nd["tok"]
                for k in range(1, KT, 2):
                    pool.wait_ge(*nq("nhh", q, len(parts(tok)) * (k + 1)))
                    nc.gpsimd.tensor_tensor(hl(k)[:, 0:tok], odd_tmp(q, k)[:, 0:tok],
                                            hh(k)[:, 0:tok].bitcast(F32), ALU.subtract).then_inc(sem("s_nhp"), 1)

            def queries_scaled():
                for i in range(4):
                    pool.wait_ge(sem("g_e1"), i + 1)
                    nc.gpsimd.tensor_tensor(gsc[:, i, :], gsc[:, i, :], big[:, i % 2, :], ALU.mult) \
                        .then_inc(sem("g_qe"), 1)

            for n in range(NB):
                if n == FIRST[("out", 0)] + 2:
                    queries_scaled()
                b = BLOCKS[max(n - 2, 0)]
                key = (b["kind"], b["layer"])
                if n >= 2 and key in NORM_FOR and FIRST[key] == n - 2:
                    norm_low(NORM[NORM_FOR[key]])
                s = n % RING
                w = BLOCKS[n]["nk"] * P
                pool.wait_ge(sem("s_hi"), n + 1)
                if n >= RING:
                    pool.wait_ge(sem("s_acc"), n - RING + 1)
                nc.gpsimd.tensor_tensor(wlo[:, s, 0:w], raw[:, s, 0:w], whi[:, s, 0:w].bitcast(F32),
                                        ALU.subtract).then_inc(sem("s_lo"), 1)

        @block.scalar
        def _(act):
            A = nc.scalar.activation

            def high(n):
                if n >= NB:
                    return
                s = n % RING
                w = BLOCKS[n]["nk"] * P
                act.wait_ge(sem(f"s_raw{s}"), 16 * (n // RING + 1))
                if n >= RING:
                    act.wait_ge(sem("s_acc"), n - RING + 1)
                    act.wait_ge(sem("s_lo"), n - RING + 1)
                A(whi[:, s, 0:w], raw[:, s, 0:w], ACT.Copy).then_inc(sem("s_hi"), 1)

            def ada_copy(c):
                act.wait_ge(sem("s_adamm"), 2 * (c + 1))
                if c >= 2:
                    act.wait_ge(sem("s_adaT"), c - 1)
                A(adasb[:, c % 2, :], wk[0][:, 512 * (c % 2):512 * (c % 2) + 512], ACT.Copy) \
                    .then_inc(sem("s_adacp"), 1)

            def square(q, k, tok):
                if k >= 3:
                    act.wait_ge(*nq("sqadd", q, k - 2))
                A(norm_tmp(q, 0 if k == 0 else 1 + k % 2)[:, 0:tok], xT[:, k, 0:tok], ACT.Square) \
                    .then_inc(sem("s_sq"), 1)

            def root(q, tok):
                nc.scalar.preload_act_table_set(LN_EXP)
                act.wait_ge(*nq("nps", q, 1))
                y = norm_tmp(q, 3)[:, 0:tok]
                ps = (lin if q == 0 else wk)[0]
                A(y, ps[:, 0:tok], ACT.Ln, bias=epsc[:, 0:1]).then_inc(sem("s_nln"), 1)
                act.wait_ge(sem("s_nln"), q + 1)
                A(y, y, ACT.Exp, scale=-0.5).then_inc(sem("s_rs"), 1)

            def norm_high(nd):
                q, tok = nd["q"], nd["tok"]
                if q > 0:
                    root(q, tok)
                act.wait_ge(sem("s_modA"), 1 if q == 0 else 4)
                for k in range(KT):
                    act.wait_ge(*nq("nt", q, k + 1))
                    if k % 2 == 1:
                        if k >= 5:
                            act.wait_ge(*nq("nhp", q, k // 2 - 1))
                        for c, a, b in parts(tok):
                            A(odd_tmp(q, k)[:, a:b], scaled_tmp(q, k)[:, a:b], ACT.Identity,
                              scale=modA[:, nd["a"], k, c:c + 1],
                              bias=mod[:, nd["layer"], nd["sh"] + k, c:c + 1])
                    for c, a, b in parts(tok):
                        A(hh(k)[:, a:b], scaled_tmp(q, k)[:, a:b], ACT.Identity,
                          scale=modA[:, nd["a"], k, c:c + 1],
                          bias=mod[:, nd["layer"], nd["sh"] + k, c:c + 1]).then_inc(sem("s_nhh"), 1)

            act.wait_ge(sem("s_par"), 16)
            act.wait_ge(sem("s_cpad0"), 1)
            A(cpad[:, :, 0:2], par[:, PC_C:PC_C + 16].rearrange("p (k c) -> p k c", c=2), ACT.Silu) \
                .then_inc(sem("s_cpad"), 1)
            for k in range(KT):
                if k == 0:
                    ada_copy(0)
                    act.wait_ge(sem("s_x"), 16)
                if k == 5:
                    ada_copy(1)
                square(0, k, T)
            root(0, T)
            for c in range(2, ADA_EARLY):
                ada_copy(c)
            high(0)
            high(1)
            norm_high(NORM[0])

            def mixer_projection(layer, n, b):
                m = b["m"]
                tok = b["tok"]
                act.wait_ge(sem("s_acc"), n + 1)
                s_, v_ = ev(n)
                ps = lin[n % 2][:, 0:tok]
                if layer == 1:
                    A(big[:, m, 0:tok], ps, ACT.Copy).then_inc(s_, 1)
                elif m < 2:
                    A(big[:, m, :], ps, ACT.Copy, scale=DK ** -0.5).then_inc(s_, 1)
                elif 8 <= m < 12:
                    A(big[:, m, :], ps, ACT.Silu).then_inc(s_, 1)
                elif m < 16:
                    A(big[:, m, :], ps, ACT.Copy).then_inc(s_, 1)
                else:
                    A(ex[:, m - 16, :], ps, ACT.Copy).then_inc(s_, 1)

            def keys_high(L):
                act.wait_ge(*na("rope", L, 1))
                for g in range(2):
                    for k_ in (kst1, kst2):
                        A(k_[L][0:64, g, :], ksrc(L)[64 * g:64 * g + 64, :], ACT.Copy).then_inc(sem("a_khi"), 1)

            def low_rank_high():
                act.wait_ge(*na("rope", 0, 5))
                act.wait_ge(sem("s_rope"), 32)
                A(lrs[0:32, :], ex[0:32, 0, :], ACT.Copy).then_inc(sem("g_lh"), 1)
                A(gks[0:32, :], gkw[0:32, :], ACT.Copy).then_inc(sem("g_lh"), 1)
                A(lrs[64:96, :], ex[0:32, 0, :], ACT.Copy).then_inc(sem("g_lh"), 1)
                A(gks[32:64, :], gkw[0:32, :], ACT.Copy).then_inc(sem("g_lh"), 1)

            def attention(L):
                units = U[L]
                tiles = prep_tiles(L)

                def head_square(j):
                    if j >= 2:
                        act.wait_ge(sem("a_ms"), j - 1)
                    A(hsq[:, j % 2, :], tiles[j][0], ACT.Square).then_inc(sem("a_sq"), 1)

                def head_root(j):
                    act.wait_ge(sem("a_ms"), j + 1)
                    if j >= 2:
                        act.wait_ge(sem("a_nrm"), j - 1)
                    y = hrs[:, j % 2, :]
                    A(y, wk[j % 2][:, 0:T], ACT.Ln, bias=epsc[:, 0:1]).then_inc(sem("a_ln"), 1)
                    act.wait_ge(sem("a_ln"), j + 1)
                    A(y, y, ACT.Exp, scale=-0.5).then_inc(sem("a_rs"), 1)

                nc.scalar.preload_act_table_set(LN_EXP)
                if L == 0:
                    head_square(0)
                    for j in range(len(tiles)):
                        if j + 1 < len(tiles):
                            head_square(j + 1)
                        head_root(j)
                        if j == 2:
                            keys_high(0)

                def q_high(head):
                    u = next(x for x in units if x["head"] == head)
                    act.wait_ge(*na("rope", L, 1 + u["j"] + 1))
                    if head >= NQ[L]:
                        act.wait_ge(*na("S", L, last_step_of_head(L, head - NQ[L])))
                    for half in range(2):
                        A(qst1[L][64 * half:64 * half + 64, head % NQ[L], :], qsrc(L, u), ACT.Copy) \
                            .then_inc(sem("a_qhi"), 1)

                def row(i):
                    u = units[i]
                    act.wait_ge(*na("R", L, i + 1))
                    if u["head"] >= NQ[L]:
                        act.wait_ge(*na("S", L, last_step_of_head(L, u["head"] - NQ[L])))
                    r_ = qst2[L][64:65, u["head"] % NQ[L], u["q0"]:u["q0"] + u["nq"]]
                    A(r_, wk[1][64:65, 512:512 + u["nq"]], ACT.Copy, scale=-1.0).then_inc(sem("a_row"), 1)
                    if L == 1:
                        act.wait_ge(*na("row", L, i + 1))
                        if i >= 2:
                            act.wait_ge(*na("pv", L, units[i - 2]["t0"] + 6))
                        s_ = PC_SINK + 8 * u["g"] + u["j"]
                        A(esink[64:65, i % 2, :], r_.bitcast(F32), ACT.Exp, scale=SCALE, bias=par[64:65, s_:s_ + 1]) \
                            .then_inc(sem("a_e"), 1)

                def exponential(i, a):
                    u = units[i]
                    t = u["t0"] + a
                    _, qa, qb, _ = u["steps"][a]
                    act.wait_ge(*na("S", L, t + 1))
                    if t >= NPT:
                        act.wait_ge(*na("pv", L, t - NPT + 1))
                    A(probT[:, t % NPT, qa:qb], wk[0][:, 512 * (t % 2) + qa:512 * (t % 2) + qb], ACT.Exp,
                      scale=SCALE).then_inc(sem("a_exp"), 1)

                def inverse(i):
                    u = units[i]
                    g = u["g"]
                    act.wait_ge(*na("osb", L, i + 1))
                    if i >= 2:
                        act.wait_ge(*na("mul", L, i - 1))
                    y = rsum[64 * g:64 * g + 64, i % 2, 0:u["nq"]]
                    A(y, osb[64 - 64 * g:128 - 64 * g, i % 2, 0:u["nq"]], ACT.Ln).then_inc(sem("a_fln"), 1)
                    act.wait_ge(*na("fln", L, i + 1))
                    A(y, y, ACT.Exp, scale=-1.0).then_inc(sem("a_ri"), 1)

                def out_high(i):
                    u = units[i]
                    act.wait_ge(*na("mul", L, i + 1))
                    A(mix_rows(L, u)[0], osb[64 * u["g"]:64 * u["g"] + 64, i % 2, 0:u["nq"]], ACT.Copy) \
                        .then_inc(sem("a_ohi"), 1)

                for i in range(2):
                    head = heads_before(L, i)
                    if head is not None:
                        q_high(head)
                row(0)
                for i, u in enumerate(units):
                    for a in range(len(u["steps"])):
                        exponential(i, a)
                        short = len(u["steps"]) < 4
                        if a == 0 and i + 1 < len(units):
                            row(i + 1)
                        if L == 0 and i == 0 and a == 5:
                            low_rank_high()
                        head = heads_before(L, i + 2)
                        if a == 1 and head is not None:
                            q_high(head)
                        if a == (1 if short else 2) and i >= 1:
                            inverse(i - 1)
                        if a == (1 if short else 4) and i >= 1:
                            out_high(i - 1)
                inverse(len(units) - 1)
                out_high(len(units) - 1)

            def gla():
                for i in range(4):
                    act.wait_ge(sem("g_z"), i + 1)
                    z = (lin[i] if i < 2 else wk[i - 2])[:, 0:T]
                    A(gsc[:, i, :], z, ACT.Abs, bias=par[:, PC_GKB + i:PC_GKB + i + 1]).then_inc(sem("g_abs"), 1)
                    A(dec[:, i, :], z, ACT.Identity, bias=par[:, PC_GKB + i:PC_GKB + i + 1]) \
                        .then_inc(sem("g_zc"), 1)
                for i in range(4):
                    act.wait_ge(sem("g_abs"), i + 1)
                    A(gsc[:, i, :], gsc[:, i, :], ACT.Exp, scale=-1.0).then_inc(sem("g_exp"), 1)

                def values_out(tt):
                    act.wait_ge(sem("g_vT"), tt + 1)
                    A(vgt[:, tt, :], lin[0][:, 0:512], ACT.Copy).then_inc(sem("g_vcpA"), 1)

                values_out(0)
                for i in range(4):
                    act.wait_ge(sem("g_exp"), i + 1)
                    A(gsc[:, 4 + i, :], gsc[:, i, :], ACT.Ln, bias=epsc[:, 1:2]).then_inc(sem("g_ln"), 1)
                def exponentials(i):
                    act.wait_ge(sem("g_dc"), i + 1)
                    A(gsc[:, i, :], dec[:, i, :], ACT.Exp, scale=1.0 / TAU).then_inc(sem("g_e1"), 1)
                    A(gsc[:, 4 + i, :], dec[:, i, :], ACT.Exp, scale=-1.0 / TAU).then_inc(sem("g_e2"), 1)

                def keys_out(i, bank):
                    act.wait_ge(sem("g_kT"), i + 1)
                    A(kgt[:, i, :, :], bank[:, 0:T].rearrange("p (t d) -> p t d", d=P), ACT.Copy) \
                        .then_inc(sem("g_kcpA"), 1)

                values_out(2)
                exponentials(0)
                exponentials(1)
                values_out(4)
                keys_out(0, lin[0])
                exponentials(2)
                exponentials(3)
                act.wait_ge(sem("g_ref"), 12)
                A(ge[:, 0, :, :], gd[:, :, :], ACT.Exp, scale=1.0 / TAU).then_inc(sem("g_refe"), 1)
                A(ge[:, 1, :, :], ge[:, 1, :, :], ACT.Exp, scale=1.0 / TAU).then_inc(sem("g_refe"), 1)
                A(ge[:, 2, :, :], ge[:, 2, :, :], ACT.Exp, scale=1.0 / TAU).then_inc(sem("g_refe"), 1)
                keys_out(2, wk[1])
                for pr in range(6):
                    act.wait_ge(sem("g_O"), pr + 1)
                    src = wk[0].rearrange("p (half x) -> p half x", half=2)
                    src = src[:, :, 0:256].rearrange("p half (h t) -> p h half t", h=4)
                    A(og[:, :, pr * P:pr * P + P].rearrange("p h (half t) -> p h half t", half=2), src, ACT.Copy) \
                        .then_inc(sem("g_ocp"), 1)
                nc.scalar.preload_act_table_set(LN_EXP)
                act.wait_ge(sem("g_oi"), 6)
                for t in range(6):
                    if t < 4:
                        if t >= 2:
                            act.wait_ge(sem("g_ms"), t - 1)
                        A(big[:, 4 + t % 2, :], og[:, t, :], ACT.Square).then_inc(sem("g_sq"), 1)
                    if 1 <= t < 5:
                        act.wait_ge(sem("g_ms"), t)
                        if t >= 3:
                            act.wait_ge(sem("g_on"), t - 2)
                        y = big[:, 6 + (t - 1) % 2, :]
                        A(y, wk[(t - 1) % 2][:, 0:T], ACT.Ln, bias=epsc[:, 0:1]).then_inc(sem("g_nln"), 1)
                        act.wait_ge(sem("g_nln"), t)
                        A(y, y, ACT.Exp, scale=-0.5).then_inc(sem("g_rs"), 1)
                    if t >= 2:
                        act.wait_ge(sem("g_of"), t - 1)
                        A(hhA[:, t - 2, :], gt[:, t - 2, :], ACT.Copy).then_inc(sem("g_hi"), 1)

            for n, b in enumerate(BLOCKS):
                kind, L = b["kind"], b["layer"]
                if n == FIRST[("out", 0)]:
                    fence(act, 1)
                    attention(0)
                    gla()
                if n == FIRST[("out", 1)]:
                    attention(1)
                if (kind, L) in NORM_FOR and n == FIRST[(kind, L)] and n > 0:
                    norm_high(NORM[NORM_FOR[(kind, L)]])
                high(n + 2)
                if kind == "proj":
                    mixer_projection(L, n, b)
                    if L == 1 and b["m"] == 3:
                        keys_high(1)
                    if L == 0:
                        ada_copy(ADA_EARLY + n)
                        if n == 18:
                            ada_copy(2 * NADA - 1)
                elif kind == "w1":
                    i = (n - FIRST[("w1", L)])
                    act.wait_ge(sem("s_acc"), n + 1)
                    j = b["h"] + FT * L
                    if j >= 2:
                        act.wait_ge(sem("s_gl"), j - 1)
                    A(tmps[:, 4 + b["h"] % 2, 0:b["tok"]], lin[n % 2][:, 0:b["tok"]], ACT.Silu).then_inc(ev(n)[0], 1)
                elif kind == "w3":
                    act.wait_ge(*ev(n))
                    A(gh[:, b["i"], 0:b["tok"]], tmps[:, 6 + b["h"] % 2, 0:b["tok"]], ACT.Copy) \
                        .then_inc(sem("s_gh"), 1)
                elif kind == "out" or (kind == "w2" and b["g"] == len(GROUPS) - 1):
                    q = {("out", 0): 1, ("w2", 0): 2, ("out", 1): 3, ("w2", 1): 4}[(kind, L)]
                    act.wait_ge(*ev(n))
                    square(q, b["m"], NORM[q]["tok"])
            root(4, NX)

        @block.vector
        def _(dve):
            V = nc.vector
            TT, TS, STT = V.tensor_tensor, V.tensor_scalar, V.scalar_tensor_tensor

            V.memset(epsc[:, 0:1], EPS)
            V.memset(epsc[:, 1:2], 1.0)
            V.memset(cpad[:, :, :], 0.0).then_inc(sem("s_cpad0"), 1)

            def ada_reduce(c):
                layer, cc = divmod(c, NADA)
                dve.wait_ge(sem("s_adaT"), c + 1)
                dst = mod[:, layer, 4 * cc:4 * cc + 4, :]
                src = wk[1][:, 512 * (c % 2):512 * (c % 2) + 512].rearrange("p (q g r) -> p q r g", g=4, r=32)
                V.tensor_reduce(dst, src[:, :, 0:2, :], AX.X, ALU.add).then_inc(sem("s_adar"), 1)
                dve.wait_ge(sem("s_adar"), c + 1)
                bias = par[:, PC_ADAB + 48 * layer + 4 * cc:PC_ADAB + 48 * layer + 4 * cc + 4]
                TT(dst, dst, bias.unsqueeze(2).to_broadcast([P, 4, 2]), ALU.add).then_inc(sem("s_mod"), 1)

            def mod_scale(a):
                layer, second = divmod(a, 2)
                c0 = 32 if second else 8
                gain = par[:, PC_N + KT * a:PC_N + KT * a + KT].unsqueeze(2).to_broadcast([P, KT, 2])
                STT(out=modA[:, a, :, :], in0=mod[:, layer, c0:c0 + KT, :], scalar=1.0, in1=gain, op0=ALU.add,
                    op1=ALU.mult).then_inc(sem("s_modA"), 1)

            def add_square(q, k, tok):
                if k == 0:
                    return
                dve.wait_ge(*nq("sq", q, k + 1))
                if k > 1:
                    dve.wait_ge(*nq("sqadd", q, k - 1))
                acc = norm_tmp(q, 0)[:, 0:tok]
                TT(acc, acc, norm_tmp(q, 1 + k % 2)[:, 0:tok], ALU.add).then_inc(sem("s_sqadd"), 1)

            def rstd(q, tok):
                dve.wait_ge(*nq("rs", q, 1))

            def norm_apply(nd):
                q, tok = nd["q"], nd["tok"]
                rstd(q, tok)

                def scaled(k):
                    if k >= 4:
                        dve.wait_ge(*nq("nhh", q, len(parts(tok)) * (k - 3)))
                    TT(scaled_tmp(q, k)[:, 0:tok], xT[:, k, 0:tok], norm_tmp(q, 3)[:, 0:tok], ALU.mult) \
                        .then_inc(sem("s_nt"), 1)

                dve.wait_ge(*nq("sqadd", q, KT - 1))
                scaled(0)
                scaled(1)
                if q == 0:
                    for c in range(ADA_EARLY):
                        ada_reduce(c)
                    dve.wait_ge(sem("s_mod"), ADA_EARLY)
                    mod_scale(0)
                dve.wait_ge(sem("s_modA"), 1 if q == 0 else 4)
                for k in range(KT):
                    if k + 2 < KT:
                        scaled(k + 2)
                    if k % 2 == 1:
                        continue
                    dve.wait_ge(*nq("nt", q, k + 1))
                    if k >= 2:
                        dve.wait_ge(*nq("nhl", q, k // 2))
                    for c, a, b in parts(tok):
                        TS(norm_tmp(q, 6)[:, a:b], scaled_tmp(q, k)[:, a:b],
                           modA[:, nd["a"], k, c:c + 1], mod[:, nd["layer"], nd["sh"] + k, c:c + 1],
                           ALU.mult, ALU.add).then_inc(sem("s_nhf"), 1)
                    dve.wait_ge(*nq("nhf", q, len(parts(tok)) * (k // 2 + 1)))
                    dve.wait_ge(*nq("nhh", q, len(parts(tok)) * (k + 1)))
                    TT(hl(k)[:, 0:tok], norm_tmp(q, 6)[:, 0:tok], hh(k)[:, 0:tok].bitcast(F32),
                       ALU.subtract).then_inc(sem("s_nhl"), 1)

            dve.wait_ge(sem("s_par"), 16)
            for k in range(KT):
                if k == 1:
                    dve.wait_ge(*nq("sq", 0, 1))
                add_square(0, k, T)
            norm_apply(NORM[0])

            def normed(j):
                t, g = prep_tiles(0)[j]
                dve.wait_ge(sem("a_rs"), j + 1)
                STT(out=t, in0=t, scalar=par[:, g:g + 1], in1=hrs[:, j % 2, :], op0=ALU.mult,
                    op1=ALU.mult).then_inc(sem("a_nrm"), 1)

            def roped(L, j):
                t = prep_tiles(L)[j][0][:, 0:NX]
                dve.wait_ge(*na("rot", L, j + 1))
                rs_ = ropet[L][:, j % 2, 0:NX]
                TT(rs_, rot_out(L, j), sin, ALU.mult).then_inc(sem("a_rsin"), 1)
                TT(t, t, cos, ALU.mult).then_inc(sem("a_rcos"), 1)
                dve.wait_ge(*na("rsin", L, j + 1))
                dve.wait_ge(*na("rcos", L, j + 1))
                TT(t, t, rs_, ALU.add).then_inc(sem("a_rope"), 1)

            def keys_low(L):
                dve.wait_ge(*na("khi", L, 4))
                k_ = ksrc(L)
                for g in range(2):
                    TT(kst1[L][64:128, g, :], k_[64 * g:64 * g + 64, :], kst1[L][0:64, g, :].bitcast(F32),
                       ALU.subtract).then_inc(sem("a_klo"), 1)
                    V.tensor_copy(kst2[L][64:65, g, :], epsc[64:65, 1:2].to_broadcast([1, T])) \
                        .then_inc(sem("a_one"), 1)

            def values_in(L):
                if L == 1:
                    V.memset(zones[:, 0, 0:64], 0.0)
                    V.memset(zones[:, 0, 64:128], 1.0)
                    V.memset(zones[:, 1, 0:64], 1.0)
                    V.memset(zones[:, 1, 64:128], 0.0).then_inc(sem("a_zone"), 1)
                    TS(sink8[:, :], par[:, PC_SINK:PC_SINK + 16], 1.0 / SCALE, None, ALU.mult) \
                        .then_inc(sem("a_zone"), 1)
                dve.wait_ge(*na("vps", L, 1))
                vT = vT_out(L).rearrange("p (t d) -> p t d", d=P)
                V.memset(vaug[L][:, :, 0, 64:128], 1.0)
                V.memset(vaug[L][:, :, 1, 0:64], 1.0)
                for g in range(2):
                    V.tensor_copy(vaug[L][:, :, g, 64 * g:64 * g + 64], vT[:, :, 64 * g:64 * g + 64]) \
                        .then_inc(sem("a_vtok"), 1)

            def attention(L):
                units = U[L]
                if L == 0:
                    dve.wait_ge(sem("s_con"), 16)
                    dve.wait_ge(sem("s_rope"), 32)
                    normed(0)
                    for j in range(len(prep_tiles(0))):
                        if j + 1 < len(prep_tiles(0)):
                            normed(j + 1)
                        roped(0, j)
                        if j == 1:
                            values_in(0)
                        if j == 3:
                            keys_low(0)

                def q_low(head):
                    u = next(x for x in units if x["head"] == head)
                    dve.wait_ge(*na("qhi", L, 2 * (head + 1)))
                    g = u["g"]
                    TT(qst2[L][0:64, head % NQ[L], :], qsrc(L, u),
                       qst1[L][64 * g:64 * g + 64, head % NQ[L], :].bitcast(F32), ALU.subtract) \
                        .then_inc(sem("a_qlo"), 1)

                def maxima(i, q):
                    u = units[i]
                    m = u["m0"] + q
                    n = u["n"] or sum(x[2] for x in u["maxima"][q])
                    dve.wait_ge(*na("M", L, m + 1))
                    if i >= 3:
                        dve.wait_ge(*na("R", L, i - 2))
                    V.reduce_max(st_mx[:, i % 3, q:q + 1], lin[m % 2][:, u["c0"]:u["c0"] + n], AX.X) \
                        .then_inc(sem("a_mx"), 1)

                def sink_maxima(i):
                    u = units[i]
                    s_ = 8 * u["g"] + u["j"]
                    dve.wait_ge(*na("mx", L, u["m0"] + 4))
                    TS(st_mx[:, i % 3, :], st_mx[:, i % 3, :], sink8[:, s_:s_ + 1], None, ALU.max) \
                        .then_inc(sem("a_smax"), 1)

                def evacuate(i):
                    u = units[i]
                    dve.wait_ge(*na("pv", L, u["t0"] + len(u["steps"])))
                    if i >= 2:
                        dve.wait_ge(*na("ohi", L, i - 1))
                        dve.wait_ge(*na("olo", L, i - 1))
                        dve.wait_ge(*na("fln", L, i - 1))
                    V.tensor_copy(osb[:, i % 2, 0:u["nq"]], wk[1][:, 0:u["nq"]]).then_inc(sem("a_osb"), 1)

                def outputs(i):
                    u = units[i]
                    rows = slice(64 * u["g"], 64 * u["g"] + 64)
                    dve.wait_ge(*na("osb", L, i + 1))
                    dve.wait_ge(*na("ri", L, i + 1))
                    TT(osb[rows, i % 2, 0:u["nq"]], osb[rows, i % 2, 0:u["nq"]], rsum[rows, i % 2, 0:u["nq"]],
                       ALU.mult).then_inc(sem("a_mul"), 1)

                def out_low(i):
                    u = units[i]
                    h_, l_ = mix_rows(L, u)
                    dve.wait_ge(*na("ohi", L, i + 1))
                    TT(l_, osb[64 * u["g"]:64 * u["g"] + 64, i % 2, 0:u["nq"]], h_.bitcast(F32), ALU.subtract) \
                        .then_inc(sem("a_olo"), 1)

                def unit_maxima(i):
                    if i < len(units):
                        for q in range(len(units[i]["maxima"])):
                            maxima(i, q)
                        if L == 1:
                            sink_maxima(i)

                if L == 1:
                    dve.wait_ge(sem("a_zone"), 2)
                for i in range(2):
                    head = heads_before(L, i)
                    if head is not None:
                        q_low(head)
                for i in range(2):
                    unit_maxima(i)
                for i, u in enumerate(units):
                    if i >= 1:
                        evacuate(i - 1)
                    if L == 0 and i == 2:
                        dve.wait_ge(sem("g_lh"), 2)
                        TT(lrs[32:64, :], ex[0:32, 0, :], lrs[0:32, :].bitcast(F32), ALU.subtract) \
                            .then_inc(sem("g_ll"), 1)
                        TT(gks[64:96, :], gkw[0:32, :], gks[0:32, :].bitcast(F32), ALU.subtract) \
                            .then_inc(sem("g_ll"), 1)
                    head = heads_before(L, i + 2)
                    if head is not None:
                        q_low(head)
                    later = units[i + 2]["maxima"] if i + 2 < len(units) else []
                    for q in range(len(later)):
                        if q == 2 and i >= 1:
                            outputs(i - 1)
                        maxima(i + 2, q)
                    if later and L == 1:
                        sink_maxima(i + 2)
                    if i >= 1:
                        if len(later) <= 2:
                            outputs(i - 1)
                        out_low(i - 1)
                evacuate(len(units) - 1)
                outputs(len(units) - 1)
                out_low(len(units) - 1)

            def gla():
                for d in range(2):
                    V.memset(cmask[:, d, :], 1.0).then_inc(sem("g_cm"), 1)
                dve.wait_ge(sem("g_cm"), 2)
                for d in range(2):
                    V.memset(cmask[:, d, :].rearrange("p (c t) -> p c t", t=CH)[:, :, (CH - 1) * d], 0.0) \
                        .then_inc(sem("g_cm"), 1)

                def values_out(tt):
                    dve.wait_ge(sem("g_vT"), tt + 1)
                    V.tensor_copy(vgt[:, tt, :], lin[1][:, 0:512]).then_inc(sem("g_vcpD"), 1)

                values_out(1)
                def chunks(i):
                    return gsc[:, i, :].rearrange("p (c t) -> p c t", t=CH)

                def decays(i):
                    dve.wait_ge(sem("g_ln"), i + 1)
                    STT(out=dec[:, i, :], in0=dec[:, i, :], scalar=0.0, in1=gsc[:, 4 + i, :], op0=ALU.min,
                        op1=ALU.subtract).then_inc(sem("g_dec"), 1)
                    dve.wait_ge(sem("g_cm"), 4)
                    dve.wait_ge(sem("g_dec"), i + 1)
                    if i < 2:
                        V.tensor_tensor_scan(gsc[:, i, :], cmask[:, 0, :], dec[:, i, :], 0.0, ALU.mult, ALU.add) \
                            .then_inc(sem("g_scan"), 1)
                    else:
                        V.tensor_tensor_scan(gsc[:, i, T - 1::-1], cmask[:, 1, T - 1::-1], dec[:, i, T - 1::-1], 0.0,
                                             ALU.mult, ALU.add).then_inc(sem("g_scan"), 1)

                def relative(i):
                    last = (CH - 1) if i < 2 else 0
                    dve.wait_ge(sem("g_scan"), i + 1)
                    V.tensor_copy(gd[:, i, :], chunks(i)[:, :, CH // 2 - 1]).then_inc(sem("g_ref"), 1)
                    V.tensor_copy(ge[:, 1, i, :], chunks(i)[:, :, last]).then_inc(sem("g_ref"), 1)
                    TT(ge[:, 2, i, :], chunks(i)[:, :, last], chunks(i)[:, :, CH // 2 - 1], ALU.subtract) \
                        .then_inc(sem("g_ref"), 1)
                    dve.wait_ge(sem("g_ref"), 3 * i + 1)
                    TT(dec[:, i, :].rearrange("p (c t) -> p c t", t=CH), chunks(i),
                       gd[:, i, :].unsqueeze(2).to_broadcast([P, NCH, CH]), ALU.subtract).then_inc(sem("g_d"), 1)
                    dve.wait_ge(sem("g_d"), i + 1)
                    TS(dec[:, i, :], dec[:, i, :], -CLAMP, CLAMP, ALU.max, ALU.min).then_inc(sem("g_dc"), 1)

                def keys_scaled(i):
                    dve.wait_ge(sem("g_e2"), i + 1)
                    TT(gsc[:, 4 + i, :], gsc[:, 4 + i, :], big[:, 2 + i % 2, :], ALU.mult).then_inc(sem("g_ke"), 1)

                def keys_out(i, bank):
                    dve.wait_ge(sem("g_kT"), i + 1)
                    V.tensor_copy(kgt[:, i, :, :], bank[:, 0:T].rearrange("p (t d) -> p t d", d=P)) \
                        .then_inc(sem("g_kcpD"), 1)

                for i in range(2):
                    decays(i)
                for i in range(2):
                    relative(i)
                values_out(3)
                decays(2)
                keys_scaled(0)
                values_out(5)
                decays(3)
                keys_scaled(1)
                relative(2)
                keys_out(1, lin[1])
                relative(3)
                keys_scaled(2)
                keys_scaled(3)
                keys_out(3, wk[0])
                dve.wait_ge(sem("g_refe"), 3)
                for k in range(2):
                    V.tensor_copy(gpos[:, k, 0:2, 4:12], ge[:, k, 0:2, 0:8])
                    V.tensor_copy(gpos[:, k, 0:2, 0:4], ge[:, k, 0:2, 8:12])
                    V.tensor_copy(gpos[:, k, 2:4, :], ge[:, k, 2:4, NCH - 1::-1]).then_inc(sem("g_pos"), 1)
                dve.wait_ge(sem("g_pos"), 2)
                V.memset(gpos[:, 1, :, 0:1], 0.0).then_inc(sem("g_pos"), 1)

                def updates(k3):
                    dve.wait_ge(sem("g_U"), k3 + 1)
                    for par_ in range(2):
                        bank = psum[:, 512 * (2 * k3 + par_):512 * (2 * k3 + par_) + 512]
                        for d in range(2):
                            slots = [k for k in range(4 * k3, 4 * k3 + 4) if k // 6 == d]
                            if not slots:
                                continue
                            n_, k0 = len(slots), slots[0]
                            c = 2 * (k0 % 6) + par_
                            src = bank[:, P * (k0 - 4 * k3):P * (k0 - 4 * k3 + n_)] \
                                .rearrange("p (c g v) -> p c g v", g=2, v=CH)
                            dec_ = ge[:, 2, 2 * d:2 * d + 2, c:c + 2 * n_ - 1:2].rearrange("p g c -> p c g") \
                                .unsqueeze(3).to_broadcast([P, n_, 2, CH])
                            if d == 0:
                                p0 = (c + 4) % NCH
                                dst = states[:, d, :, :, p0:p0 + 2 * n_ - 1:2]
                            else:
                                p0 = NCH - 1 - c
                                stop = p0 - 2 * n_ + 1
                                dst = states[:, d, :, :, p0:(stop if stop >= 0 else None):-2]
                            TT(dst.rearrange("p g v c -> p c g v"), src, dec_, ALU.mult).then_inc(sem("g_ud"), 1)

                def masked(pr):
                    dve.wait_ge(sem("g_A"), pr + 1)
                    if pr >= 2:
                        dve.wait_ge(sem("g_O"), pr - 1)
                    ps = psum[:, 0:2048].rearrange("p (r x) -> p r x", r=4)
                    ps = [ps[:, :, P * d:P * d + P].rearrange("p r (g t) -> p r g t", g=2) for d in range(2)]
                    bc = [m_.unsqueeze(1).unsqueeze(1).to_broadcast([P, 4, 2, CH]) for m_ in mgla]
                    o_ = attnT[:, pr % 2, :].rearrange("p (r g t) -> p r g t", r=4, g=2)
                    TT(o_, ps[0], bc[0], ALU.mult).then_inc(sem("g_am"), 1)
                    if pr >= 1:
                        dve.wait_ge(sem("g_at"), pr)
                    TT(attnM[:, :].rearrange("p (r g t) -> p r g t", r=4, g=2), ps[1], bc[1], ALU.mult) \
                        .then_inc(sem("g_am2"), 1)
                    dve.wait_ge(sem("g_am"), pr + 1)
                    dve.wait_ge(sem("g_am2"), pr + 1)
                    TT(attnT[:, pr % 2, :], attnT[:, pr % 2, :], attnM[:, :], ALU.add).then_inc(sem("g_at"), 1)

                def carry(d):
                    dve.wait_ge(sem("g_pos"), 3)
                    dve.wait_ge(sem("g_ud"), 8)
                    if d == 1:
                        dve.wait_ge(sem("g_carry"), 1)
                    for g in range(2):
                        V.tensor_copy(keep[:, g, :, :], gpos[:, 1, 2 * d + g, :].unsqueeze(1)
                                      .to_broadcast([P, CH, NCH])).then_inc(sem("g_keep"), 1)
                    dve.wait_ge(sem("g_keep"), 2 * d + 2)
                    run = states[:, d, :, :, :].rearrange("p g v c -> p (g v c)")
                    V.tensor_tensor_scan(run, keep[:, :, :, :].rearrange("p g v c -> p (g v c)"), run, 0.0,
                                         ALU.mult, ALU.add).then_inc(sem("g_carry"), 1)

                def given(d):
                    dve.wait_ge(sem("g_carry"), 2 if d == 1 else 1)
                    ref_ = gpos[:, 0, 2 * d:2 * d + 2, 1:NCH].unsqueeze(3).to_broadcast([P, 2, NCH - 1, CH])
                    TT(statr[:, d, 1:NCH, :, :].rearrange("p c g v -> p g c v"),
                       states[:, d, :, :, 0:NCH - 1].rearrange("p g v c -> p g c v"), ref_, ALU.mult) \
                        .then_inc(sem("g_sr"), 1)

                for k3 in range(3):
                    updates(k3)
                masked(0)
                carry(0)
                carry(1)
                masked(1)
                given(0)
                given(1)
                for pr in range(6):
                    if pr + 2 < 6:
                        masked(pr + 2)
                    dve.wait_ge(sem("g_I"), pr + 1)
                    dve.wait_ge(sem("g_ocp"), pr + 1)
                    o_ = og[:, :, pr * P:pr * P + P].rearrange("p (g b) t -> p b g t", b=2)
                    give = wk[1].rearrange("p (b x) -> p b x", b=2)[:, :, 0:2 * P] \
                        .rearrange("p b (g t) -> p b g t", g=2)
                    TT(o_, o_, give, ALU.add).then_inc(sem("g_oi"), 1)
                for t in range(4):
                    dve.wait_ge(sem("g_rs"), t + 1)
                    TT(og[:, t, :], og[:, t, :], big[:, 6 + t % 2, :], ALU.mult).then_inc(sem("g_on"), 1)
                    dve.wait_ge(sem("g_on"), t + 1)
                    STT(out=gt[:, t, :], in0=og[:, t, :], scalar=par[:, PC_GLAG:PC_GLAG + 1], in1=big[:, 8 + t, :],
                        op0=ALU.mult, op1=ALU.mult).then_inc(sem("g_of"), 1)
                    dve.wait_ge(sem("g_hi"), t + 1)
                    TT(hlA[:, t, :], gt[:, t, :], hhA[:, t, :].bitcast(F32), ALU.subtract).then_inc(sem("g_lo"), 1)

            def residual(n, b, gate):
                L, m = b["layer"], b["m"]
                dve.wait_ge(sem("s_acc"), n + 1)
                for c, a, e in parts(b["tok"]):
                    ins = STT(out=xT[:, m, a:e], in0=lin[n % 2][:, a:e], scalar=mod[:, L, gate + m, c:c + 1],
                              in1=xT[:, m, a:e], op0=ALU.mult, op1=ALU.add)
                ins.then_inc(ev(n)[0], 1)

            for n, b in enumerate(BLOCKS):
                kind, L = b["kind"], b["layer"]
                if n == FIRST[("out", 0)]:
                    ada_reduce(2 * NADA - 1)
                    dve.wait_ge(sem("s_mod"), 2 * NADA)
                    for a in range(1, 4):
                        mod_scale(a)
                    fence(dve, 1)
                    attention(0)
                    gla()
                if n == FIRST[("out", 1)]:
                    attention(1)
                if (kind, L) in NORM_FOR and n == FIRST[(kind, L)] and n > 0:
                    add_square(NORM_FOR[(kind, L)], KT - 1, NORM[NORM_FOR[(kind, L)]]["tok"])
                    norm_apply(NORM[NORM_FOR[(kind, L)]])
                if kind == "proj" and L == 0:
                    ada_reduce(ADA_EARLY + n)
                elif kind == "proj":
                    for m in ready_tiles(b["m"]):
                        if m == 1:
                            values_in(1)
                        else:
                            roped(1, max(m - 1, 0))
                    if b["m"] == 5:
                        keys_low(1)
                elif kind == "w3":
                    j = b["h"] + FT * L
                    dve.wait_ge(sem("s_acc"), n + 1)
                    dve.wait_ge(*ev(n - 1))
                    TT(tmps[:, 6 + b["h"] % 2, 0:b["tok"]], tmps[:, 4 + b["h"] % 2, 0:b["tok"]],
                       lin[n % 2][:, 0:b["tok"]], ALU.mult).then_inc(ev(n)[0], 1)
                    dve.wait_ge(*ev(n))
                    dve.wait_ge(sem("s_gh"), j + 1)
                    TT(gl[:, b["i"], 0:b["tok"]], tmps[:, 6 + b["h"] % 2, 0:b["tok"]],
                       gh[:, b["i"], 0:b["tok"]].bitcast(F32), ALU.subtract).then_inc(sem("s_gl"), 1)
                elif kind in ("out", "w2"):
                    if kind == "w2" and b["g"] > 0:
                        dve.wait_ge(*ev(n - (BLOCKS[n]["nk"] * 2 + KT)))
                    residual(n, b, 16 if kind == "out" else 40)
                    if (kind == "out" or b["g"] == len(GROUPS) - 1) and b["m"] >= 1:
                        q = {("out", 0): 1, ("w2", 0): 2, ("out", 1): 3, ("w2", 1): 4}[(kind, L)]
                        add_square(q, b["m"] - 1, NORM[q]["tok"])
            add_square(4, KT - 1, NX)
            dve.wait_ge(*nq("nhl", 3, KT // 2))
            rstd(4, NX)
            for k in range(KT):
                STT(out=big[:, k, 0:NX], in0=xT[:, k, 0:NX], scalar=par[:, PC_FIN + k:PC_FIN + k + 1],
                    in1=norm_tmp(4, 3)[:, 0:NX], op0=ALU.mult, op1=ALU.mult).then_inc(sem("s_fin"), 1)

        @block.tensor
        def _(pe):
            MM, TR = nc.tensor.matmul, nc.tensor.transpose

            def ada_mm(c):
                if c >= 2:
                    pe.wait_ge(sem("s_adacp"), c - 1)
                for half in range(2):
                    h = 2 * c + half
                    pe.wait_ge(sem(f"s_adaload{h % ADA_RING}"), 16 * (h // ADA_RING + 1))
                    for g in range(4):
                        last = MM(wk[0][32 * g:32 * g + 32, 512 * (c % 2):512 * (c % 2) + 512],
                                  cpad[:, 4 * half + g, :], ada_w[:, h % ADA_RING, g, :], start=half == 0,
                                  stop=half == 1, skip_group_check=True)
                    last.then_inc(sem("s_adamm"), 1)

            def ada_T(c):
                pe.wait_ge(sem("s_adacp"), c + 1)
                if c >= 2:
                    pe.wait_ge(sem("s_mod"), c - 1)
                for q in range(4):
                    last = TR(wk[1][:, 512 * (c % 2) + P * q:512 * (c % 2) + P * q + P],
                              adasb[:, c % 2, q * P:q * P + P], ident)
                last.then_inc(sem("s_adaT"), 1)

            def block_products(ns):
                b = BLOCKS[ns[0]]
                kind, L, tok = b["kind"], b["layer"], b["tok"]
                for n in ns:
                    pe.wait_ge(sem("s_hi"), n + 1)
                    pe.wait_ge(sem("s_lo"), n + 1)
                    if n >= 2:
                        pe.wait_ge(*ev(n - 2))
                q = NORM_FOR.get((kind, L)) if ns[0] == FIRST[(kind, L)] else None
                order = [4, 5, 6, 7, 0, 1, 2, 3] if kind == "out" and L == 0 else list(range(b["nk"]))
                for k in order:
                    if kind == "out" and b["m"] == 0:
                        if L == 0 and k < 4:
                            pe.wait_ge(sem("g_lo"), k + 1)
                        elif L == 0:
                            pe.wait_ge(*na("olo", 0, 4 * (k - 3)))
                        else:
                            pe.wait_ge(*na("olo", 1, 2 * (k + 1)))
                    if q is not None:
                        pe.wait_ge(*nq("nhh", q, len(parts(NORM[q]["tok"])) * (k + 1)))
                        pe.wait_ge(*nq("nhp" if k % 2 else "nhl", q, k // 2 + 1))
                    if kind == "w2" and b["m"] == 0:
                        j = GROUPS[b["g"]][0] + FT * L + k + 1
                        pe.wait_ge(sem("s_gh"), j)
                        pe.wait_ge(sem("s_gl"), j)
                    hi_, lo_ = (gh[:, k, :], gl[:, k, :]) if kind == "w2" else (hh(k), hl(k))
                    first, end = k == order[0], k == order[-1]
                    for n in ns:
                        s, out_ = n % RING, lin[n % 2]
                        wh_, wl_ = whi[:, s, k * P:k * P + P], wlo[:, s, k * P:k * P + P]
                        for j, (w_, a_) in enumerate(((wh_, hi_), (wh_, lo_), (wl_, hi_))):
                            for _, t0, t1 in parts(tok):
                                last = MM(out_[:, t0:t1], w_, a_[:, t0:t1], start=first and j == 0,
                                          stop=end and j == 2)
                        if end:
                            last.then_inc(sem("s_acc"), 1)

            def mean_square(q, tok):
                pe.wait_ge(*nq("sqadd", q, KT - 1))
                for _, a, b in parts(tok):
                    last = MM((lin if q == 0 else wk)[0][:, a:b], ones, norm_tmp(q, 0)[:, a:b], start=True, stop=True)
                last.then_inc(sem("s_nps"), 1)

            pe.wait_ge(sem("s_cpad"), 1)
            pe.wait_ge(sem("s_con"), 16)
            for c in range(ADA_EARLY):
                ada_mm(c)
                if c == 2:
                    mean_square(0, T)
                if c >= 1:
                    ada_T(c - 1)
            ada_T(ADA_EARLY - 1)

            def rotated(L, j):
                if L == 0:
                    pe.wait_ge(sem("a_nrm"), j + 1)
                if j >= 2:
                    pe.wait_ge(*na("rsin", L, j - 1))
                MM(rot_out(L, j), rot, prep_tiles(L)[j][0][:, 0:NX], start=True, stop=True) \
                    .then_inc(sem("a_rot"), 1)

            def values_turned(L):
                for tt in range(6):
                    last = TR(vT_out(L)[:, tt * P:tt * P + P], vsrc(L)[:, tt * P:tt * P + P], ident)
                last.then_inc(sem("a_vps"), 1)

            def attention(L):
                units = U[L]
                tiles = prep_tiles(L)

                def means(j):
                    pe.wait_ge(sem("a_sq"), j + 1)
                    if j >= 2:
                        pe.wait_ge(sem("a_rs"), j - 1)
                    for a, b in ((0, NX), (NX, T)):
                        last = MM(wk[j % 2][:, a:b], blk, hsq[:, j % 2, a:b], start=True, stop=True)
                    last.then_inc(sem("a_ms"), 1)

                if L == 0:
                    means(0)
                    means(1)
                    values_turned(0)
                    for j in range(len(tiles)):
                        rotated(0, j)
                        if j + 2 < len(tiles):
                            means(j + 2)

                def maxima(i, q):
                    u = units[i]
                    m = u["m0"] + q
                    if q == 0:
                        pe.wait_ge(*na("qhi", L, 2 * (u["head"] + 1)))
                    if m >= 2:
                        pe.wait_ge(*na("mx", L, m - 1))
                    a = u["q0"] + q * P
                    for col, key, w, mask in u["maxima"][q]:
                        last = MM(lin[m % 2][:, col:col + w], qst1[L][:, u["head"] % NQ[L], a:a + P],
                                  kst1[L][:, u["g"], key:key + w], start=True, stop=mask is None)
                        if mask is not None:
                            last = MM(lin[m % 2][:, col:col + w], identr[:, :], bandm[:, mask:mask + w],
                                      start=False, stop=True)
                    last.then_inc(sem("a_M"), 1)

                def rows(i):
                    u = units[i]
                    nt = len(u["maxima"])
                    pe.wait_ge(*(na("smax", L, i + 1) if L == 1 else na("mx", L, u["m0"] + nt)))
                    if i >= 1:
                        pe.wait_ge(*na("row", L, i))
                    for q in range(nt):
                        last = MM(wk[1][64:65, 512 + P * q:512 + P * q + P], st_mx[:, i % 3, q:q + 1], ident,
                                  start=True, stop=True, tile_position=(0, 64), skip_group_check=True)
                    last.then_inc(sem("a_R"), 1)

                def scores(i, a):
                    u = units[i]
                    t = u["t0"] + a
                    kt, qa, qb, mask = u["steps"][a]
                    hd, g, q0 = u["head"] % NQ[L], u["g"], u["q0"]
                    if a == 0:
                        pe.wait_ge(*na("qlo", L, u["head"] + 1))
                        pe.wait_ge(*na("row", L, i + 1))
                    if t >= 2:
                        pe.wait_ge(*na("exp", L, t - 1))
                    o_ = wk[0][:, 512 * (t % 2) + qa:512 * (t % 2) + qb]
                    MM(o_, kst1[L][:, g, kt * P:kt * P + P], qst1[L][:, hd, q0 + qa:q0 + qb], start=True, stop=False)
                    last = MM(o_, kst2[L][0:65, g, kt * P:kt * P + P], qst2[L][0:65, hd, q0 + qa:q0 + qb],
                              start=False, stop=mask is None)
                    if mask is not None:
                        last = MM(o_, identr[:, :], bandm[:, mask:mask + qb - qa], start=False, stop=True)
                    last.then_inc(sem("a_S"), 1)

                def values(i, a):
                    u = units[i]
                    t = u["t0"] + a
                    kt, qa, qb, _ = u["steps"][a]
                    if a == 0 and i >= 1:
                        pe.wait_ge(*na("osb", L, i))
                    end = a == len(u["steps"]) - 1
                    if L == 1 and end:
                        pe.wait_ge(sem("a_e"), i + 1)
                        MM(wk[1][:, 0:NX], zones[64:65, u["g"], :], esink[64:65, i % 2, :], start=False, stop=False,
                           skip_group_check=True)
                    pe.wait_ge(*na("exp", L, t + 1))
                    MM(wk[1][:, qa:qb], vaug[L][:, kt, u["g"], :], probT[:, t % NPT, qa:qb], start=a == 0, stop=end,
                       skip_group_check=True).then_inc(sem("a_pv"), 1)

                pe.wait_ge(sem("s_idr"), 32)
                pe.wait_ge(*na("klo", L, 2))
                pe.wait_ge(*na("one", L, 2))
                pe.wait_ge(*na("vtok", L, 2))
                pe.wait_ge(*na("rope", L, len(tiles)))
                if L == 1:
                    for n in range(2):
                        pe.wait_ge(*ev(FIRST[("out", 1)] - 2 + n))
                for i in range(2):
                    for q in range(len(units[i]["maxima"])):
                        maxima(i, q)
                rows(0)
                order = steps_of(L)
                scores(0, 0)
                for t, (i, a) in enumerate(order):
                    if a == 0 and i + 1 < len(units):
                        rows(i + 1)
                    if t + 1 < len(order):
                        scores(*order[t + 1])
                    if i + 2 < len(units):
                        short = len(units[i]["steps"]) < 4
                        for q in ((a,) if short else ((), (), (0,), (1, 2), (3,), ())[a]):
                            maxima(i + 2, q)
                    values(i, a)

            def gla():
                pe.wait_ge(sem("g_lh"), 4)
                pe.wait_ge(sem("g_ll"), 2)
                for d in range(2):
                    for g2 in range(2):
                        i = 2 * d + g2
                        if i == 2:
                            pe.wait_ge(*na("exp", 0, U[0][-1]["t0"] + 2))
                        if i == 3:
                            pe.wait_ge(*na("osb", 0, len(U[0])))
                        for a, b in ((0, NX), (NX, T)):
                            last = MM((lin[i] if i < 2 else wk[i - 2])[:, a:b],
                                      gks[0:96, 256 * d + P * g2:256 * d + P * g2 + P], lrs[0:96, a:b],
                                      start=True, stop=True)
                        last.then_inc(sem("g_z"), 1)
                for tt in range(6):
                    if tt < 2:
                        pe.wait_ge(sem("g_zc"), tt + 1)
                    else:
                        pe.wait_ge(sem("g_vcpA" if tt % 2 == 0 else "g_vcpD"), tt // 2)
                    for t in range(4):
                        last = TR(lin[tt % 2][:, P * t:P * t + P], big[:, 4 + t, tt * P:tt * P + P], ident)
                    last.then_inc(sem("g_vT"), 1)
                pe.wait_ge(sem("g_vcpA"), 3)
                pe.wait_ge(sem("g_vcpD"), 3)

                def keys_turned(i):
                    pe.wait_ge(sem("g_ke"), i + 1)
                    bank = (lin[0], lin[1], wk[1], wk[0])[i]
                    for tt in range(6):
                        last = TR(bank[:, P * tt:P * tt + P], gsc[:, 4 + i, tt * P:tt * P + P], ident)
                    last.then_inc(sem("g_kT"), 1)

                def updates(k3):
                    for k in range(4 * k3, 4 * k3 + 4):
                        d, cc = divmod(k, 6)
                        for g2 in range(2):
                            for r in range(4):
                                for par_ in range(2):
                                    rows = slice(64 * par_, 64 * par_ + 64)
                                    h = 4 * g2 + r
                                    col = 512 * (2 * k3 + par_) + P * (k % 4) + CH * g2
                                    last = MM(psum[32 * r:32 * r + 32, col:col + CH],
                                              kgt[rows, 2 * d + g2, cc, 32 * r:32 * r + 32],
                                              vgt[rows, cc, 64 * h:64 * h + 64], start=True, stop=True,
                                              tile_position=(64 * par_, 32 * r), skip_group_check=True)
                    last.then_inc(sem("g_U"), 1)

                def scores(pr):
                    if pr == 0:
                        pe.wait_ge(sem("g_ud"), 6)
                        pe.wait_ge(sem("g_qe"), 4)
                    if pr >= 1:
                        pe.wait_ge(sem("g_at"), pr)
                    for d in range(2):
                        for h in range(8):
                            i, r = 2 * d + h // 4, h % 4
                            rows = slice(32 * r, 32 * r + 32)
                            for half in range(2):
                                c = pr * P + half * CH
                                col = 512 * r + P * d + CH * (h // 4)
                                last = MM(psum[64 * half:64 * half + 64, col:col + CH],
                                          gsc[rows, 4 + i, c:c + CH], gsc[rows, i, c:c + CH], start=True, stop=True,
                                          tile_position=(32 * r, 64 * half), skip_group_check=True)
                    last.then_inc(sem("g_A"), 1)

                def within(pr):
                    pe.wait_ge(sem("g_at"), pr + 1)
                    if pr == 0:
                        pe.wait_ge(sem("g_ud"), 8)
                    if pr >= 1:
                        pe.wait_ge(sem("g_ocp"), pr)
                    for h in range(8):
                        for half in range(2):
                            rows = slice(64 * half, 64 * half + 64)
                            c = 512 * half + CH * (h // 2)
                            a = CH * (2 * (h % 4) + h // 4)
                            last = MM(wk[0][64 * (h % 2):64 * (h % 2) + 64, c:c + CH],
                                      vgt[rows, pr, 64 * h:64 * h + 64], attnT[rows, pr % 2, a:a + CH],
                                      start=True, stop=True, skip_group_check=True)
                    last.then_inc(sem("g_O"), 1)

                def between(pr):
                    if pr == 0:
                        pe.wait_ge(sem("g_sr"), 2)
                    if pr >= 1:
                        pe.wait_ge(sem("g_oi"), pr)
                    for half in range(2):
                        c = 2 * pr + half
                        pos = [(c + 4) % NCH, NCH - 1 - c]
                        dirs = [d for d in range(2) if pos[d] > 0]
                        for d in dirs:
                            for h in range(8):
                                g2, r = h // 4, h % 4
                                rows = slice(32 * r, 32 * r + 32)
                                col = 512 * (r // 2) + P * g2 + CH * half
                                last = MM(wk[1][64 * (h % 2):64 * (h % 2) + 64, col:col + CH],
                                          statr[rows, d, pos[d], g2, :], gsc[rows, 2 * d + g2, c * CH:c * CH + CH],
                                          start=half == 0 and d == dirs[0] and g2 == 0, stop=half == 1 and d == dirs[-1],
                                          tile_position=(32 * r, 64 * (h % 2)), skip_group_check=True)
                    last.then_inc(sem("g_I"), 1)

                keys_turned(0)
                keys_turned(1)
                pe.wait_ge(sem("g_kcpA"), 1)
                pe.wait_ge(sem("g_kcpD"), 1)
                updates(0)
                keys_turned(2)
                keys_turned(3)
                pe.wait_ge(sem("g_kcpA"), 2)
                pe.wait_ge(sem("g_kcpD"), 2)
                updates(1)
                updates(2)
                scores(0)
                for pr in range(6):
                    if pr + 1 < 6:
                        scores(pr + 1)
                    within(pr)
                    between(pr)
                for t in range(4):
                    pe.wait_ge(sem("g_sq"), t + 1)
                    if t >= 2:
                        pe.wait_ge(sem("g_rs"), t - 1)
                    for a, b in ((0, NX), (NX, T)):
                        last = MM(wk[t % 2][:, a:b], blk, big[:, 4 + t % 2, a:b], start=True, stop=True)
                    last.then_inc(sem("g_ms"), 1)

            for n, b in enumerate(BLOCKS):
                kind, L = b["kind"], b["layer"]
                if n == FIRST[("out", 0)]:
                    ada_mm(2 * NADA - 1)
                    ada_T(2 * NADA - 2)
                    ada_T(2 * NADA - 1)
                    fence(pe, 1)
                    attention(0)
                    gla()
                if n == FIRST[("out", 1)]:
                    attention(1)
                key = (kind, L) if kind != "w3" else ("w1", L)
                if key in NORM_FOR and n == FIRST[key] and n > 0:
                    mean_square(NORM_FOR[(kind, L)], NORM[NORM_FOR[(kind, L)]]["tok"])
                if n == FIRST[key] and kind != "w2":
                    block_products([n, n + 1])
                elif kind == "w2" or n != FIRST[key] + 1:
                    block_products([n])
                if kind == "proj" and L == 1:
                    for m in ready_tiles(b["m"]):
                        pe.wait_ge(*ev(FIRST[("proj", 1)] + m))
                        if m == 1:
                            values_turned(1)
                        else:
                            rotated(1, max(m - 1, 0))
                if kind == "proj" and L == 0:
                    ada_mm(ADA_EARLY + n)
                    if n >= 1:
                        ada_T(ADA_EARLY + n - 1)
            mean_square(4, NX)


def _shape_constants():
    import numpy as np
    half, quarter, width = HD // 2, HD // 4, 64
    tok = np.arange(NX)
    inv = (10000.0 ** (-np.arange(0, half, 2, dtype=np.float32) / half)).astype(np.float32)
    ang_r = (tok // width).astype(np.float32)[:, None] * inv[None]
    ang_c = (tok % width).astype(np.float32)[:, None] * inv[None]
    ang = np.concatenate([ang_r, ang_r, ang_c, ang_c], axis=-1).T
    con = np.zeros((P, NCONST), np.float32)
    con[:, CC_COS:CC_COS + NX] = np.tile(np.cos(ang), (2, 1))
    con[:, CC_SIN:CC_SIN + NX] = np.tile(np.sin(ang), (2, 1))
    con[:, CC_ID:CC_ID + P] = np.eye(P)
    con[:, CC_ONES:CC_ONES + P] = 1.0 / D
    con[:, CC_BLK:CC_BLK + P] = np.kron(np.eye(2), np.ones((64, 64))) / 64.0
    r = np.zeros((64, 64), np.float32)
    for j in range(quarter):
        r[quarter + j, j] = -1.0
        r[j, quarter + j] = 1.0
        r[3 * quarter + j, 2 * quarter + j] = -1.0
        r[2 * quarter + j, 3 * quarter + j] = 1.0
    con[:, CC_ROT:CC_ROT + P] = np.kron(np.eye(2), r)
    j, i = np.arange(CH)[:, None], np.arange(CH)[None, :]
    con[:, CC_MF:CC_MF + CH] = np.tile(j <= i, (2, 1))
    con[:, CC_MB:CC_MB + CH] = np.tile(j >= i, (2, 1))
    q, k = np.arange(P)[:, None], np.arange(P)[None, :]
    band = np.zeros((P, 3 * P), np.float32)
    band[:, 0:P] = np.where(k >= q, 0.0, NEG)
    band[:, 2 * P:] = np.where(k <= q, 0.0, NEG)
    return con, band


def kernel(**inputs):
    import numpy as np
    import concourse.bacc as bacc
    from concourse.bass_utils import run_bass_kernel_spmd

    a = {k: np.asarray(v) for k, v in inputs.items()}
    f = np.float32

    x = np.concatenate([a["x"][0], a["ctx"][0]], axis=0)
    x_in = x.T.reshape(KT, P, T).transpose(1, 0, 2).reshape(P, KT * T)

    def cols(v):
        return v.reshape(-1, P).T

    params = np.zeros((P, NPAR), f)
    params[:, PC_C:PC_C + 2 * KT] = np.stack([cols(a["c"][0]), cols(a["c_ctx"])], axis=2).reshape(P, 2 * KT)
    for layer in range(2):
        params[:, PC_ADAB + 48 * layer:PC_ADAB + 48 * layer + 48] = cols(a["ada_b"][layer])
        params[:, PC_N + 2 * KT * layer:PC_N + 2 * KT * layer + KT] = cols(a["norm1_g"][layer])
        params[:, PC_N + 2 * KT * layer + KT:PC_N + 2 * KT * layer + 2 * KT] = cols(a["norm2_g"][layer])
    params[:, PC_FIN:PC_FIN + KT] = cols(a["final_g"])
    params[:, PC_GKB:PC_GKB + 4] = cols(a["gla_gk_b"][0].reshape(-1))
    for col, name in ((PC_GLAG, "gla_norm_g"), (PC_QN, "attn_qnorm_g"), (PC_KN, "attn_knorm_g")):
        params[:, col] = np.tile(a[name][0], 2)
    params[:, PC_SINK:PC_SINK + 16] = a["win_sink"][0][None, :]
    gkw = np.zeros((32, 512), f)
    gkw[0:16, 0:256] = a["gla_gk_w"][0, 0]
    gkw[16:32, 256:512] = a["gla_gk_w"][0, 1]

    ada = a["ada_w"].reshape(2, 2, 4, P, NADA, 512).transpose(0, 4, 1, 3, 2, 5).reshape(4 * NADA, P, 4 * 512)

    def heads_paired(w, n_heads):
        order = np.arange(n_heads).reshape(2, n_heads // 2).T.reshape(-1)
        return w.reshape(w.shape[0], n_heads, HD)[:, order].reshape(w.shape[0], n_heads * HD)

    win = a["mixab_w_in"][0]
    lr = np.zeros((D, P), f)
    lr[:, 0:32] = win[:, 1536:1568]
    proj0 = np.concatenate([win[:, 0:1536], heads_paired(win[:, 1568:2080], 8), lr, win[:, 2080:2336]], axis=1)
    wout0 = a["mixab_w_out"][0]
    out0 = np.concatenate([wout0[0:512], heads_paired(wout0[512:].T, 8).T], axis=0)
    win1 = a["win_w_in"][0]
    proj1 = np.concatenate([win1[:, 1024:1280], heads_paired(win1[:, 0:1024], 16)], axis=1)
    out1 = heads_paired(a["win_w_out"][0].T, 16).T

    weights = np.zeros((NB, P, KT * P), f)
    for n, b in enumerate(BLOCKS):
        kind, layer = b["kind"], b["layer"]
        if kind in ("proj", "out"):
            w = {("proj", 0): proj0, ("out", 0): out0, ("proj", 1): proj1, ("out", 1): out1}[(kind, layer)]
            sub = w[:, b["m"] * P:b["m"] * P + P]
        elif kind in ("w1", "w3"):
            sub = a["ffn_w1" if kind == "w1" else "ffn_w3"][layer][:, b["h"] * P:b["h"] * P + P]
        else:
            h0, nh = GROUPS[b["g"]]
            sub = a["ffn_w2"][layer][h0 * P:(h0 + nh) * P, b["m"] * P:b["m"] * P + P]
        nk = b["nk"]
        weights[n, :, 0:nk * P] = sub.reshape(nk, P, P).transpose(1, 0, 2).reshape(P, nk * P)

    con, band = _shape_constants()
    arrays = {"x_in": x_in, "params": params, "consts": con, "masks": band, "gkw": gkw, "ada": ada,
              "weights": weights}
    nc = bacc.Bacc("TRN2", target_bir_lowering=False, num_devices=1)
    args, feed = [], {}
    for name, arr in arrays.items():
        arr = np.ascontiguousarray(arr, dtype=f)
        feed[name + "_dram"] = arr
        args.append(nc.dram_tensor(name + "_dram", arr.shape, F32, kind="ExternalInput").ap())
    out = nc.dram_tensor("out_dram", (P, KT * NX), F32, kind="ExternalOutput").ap()
    build(nc, *args, out)
    r = run_bass_kernel_spmd(nc, [feed], core_ids=[0])
    got = r.results[0]["out_dram"]
    return got.reshape(P, KT, NX).transpose(2, 1, 0).reshape(1, NX, D)
```
